# Optimizing a Trainium2 kernel written in Bass

```python
import jax
import jax.numpy as jnp
from jax import lax
import numpy as np
import math
import jax, jax.numpy as jnp

D_MODEL = 2048
BATCH = 1
SEQ = 256
DEPTH = 1

HEAD_DIM = 128
ATTN_WIDTH = 3 * D_MODEL // 4
N_ATTN_HEADS = ATTN_WIDTH // HEAD_DIM
ATTN_GROUPS = ((128, 1), (512, 4), (2048, 16))
N_GROUPS = len(ATTN_GROUPS)
HEADS_PER_GROUP = N_ATTN_HEADS // N_GROUPS
ATTN_OUT_WIDTH = HEADS_PER_GROUP * HEAD_DIM
BAND = 128
ROPE_THETA = 10000.0
POOL_WIDTH = D_MODEL // 4
POOL_WINDOWS = (2, 4, 8, 16)
POOL_GROUP = POOL_WIDTH // len(POOL_WINDOWS)
IN_WIDTH = 3 * ATTN_WIDTH + POOL_WIDTH + 2 * D_MODEL
PEER_HEADS = 8
PEER_QUERY_DIM = 256
PEER_HALF = PEER_QUERY_DIM // 2
PEER_N_KEYS = 128
PEER_N_EXPERTS = PEER_N_KEYS * PEER_N_KEYS
PEER_TOPK = 16
PEER_CHUNK = 128
EPS = 1e-6


def rms_norm(x, g):
    x32 = x.astype(jnp.float32)
    y = x32 * lax.rsqrt(jnp.mean(x32 * x32, axis=-1, keepdims=True) + EPS)
    return y.astype(x.dtype) * g

def apply_rope(t, pos):
    half = t.shape[-1] // 2
    inv = jnp.power(jnp.float32(ROPE_THETA), -jnp.arange(half, dtype=jnp.float32) / half)
    ang = pos[:, None] * inv[None, :]
    cos = jnp.cos(ang)[None, :, None, :]
    sin = jnp.sin(ang)[None, :, None, :]
    t32 = t.astype(jnp.float32)
    t1, t2 = t32[..., :half], t32[..., half:]
    return jnp.concatenate([t1 * cos - t2 * sin, t2 * cos + t1 * sin], axis=-1).astype(t.dtype)

def dilated_window_attention(q, k, v, dil, steps):
    B, S, H, Dh = q.shape
    L = S // dil
    nb = -(-L // BAND)
    Lp = nb * BAND

    def to_sub(t):
        t = t.reshape(B, L, dil, H, Dh).transpose(0, 2, 1, 3, 4)
        return jnp.pad(t, ((0, 0), (0, 0), (0, Lp - L), (0, 0), (0, 0)))

    def band(t):
        t = jnp.pad(t, ((0, 0), (0, 0), (BAND, 0), (0, 0), (0, 0))).reshape(B, dil, nb + 1, BAND, H, Dh)
        return jnp.concatenate([t[:, :, :-1], t[:, :, 1:]], axis=3)

    qb = to_sub(q).reshape(B, dil, nb, BAND, H, Dh)
    kb = band(to_sub(k))
    vb = band(to_sub(v))
    s = jnp.einsum('brnqhd,brnkhd->brnhqk', qb, kb).astype(jnp.float32) * (Dh ** -0.5)
    qi = jnp.arange(BAND)[:, None]
    kj = jnp.arange(2 * BAND)[None, :]
    dist = qi + BAND - kj
    key_idx = jnp.arange(nb)[:, None, None] * BAND + kj[None] - BAND
    valid = (dist[None] >= 0) & (dist[None] <= steps) & (key_idx >= 0)
    s = jnp.where(valid[None, None, :, None], s, -jnp.inf)
    m = jnp.max(s, axis=-1, keepdims=True)
    p = jnp.exp(s - m)
    denom = jnp.sum(p, axis=-1, keepdims=True)
    o = jnp.einsum('brnhqk,brnkhd->brnqhd', (p / denom).astype(v.dtype), vb)
    lse = (m + jnp.log(denom))[..., 0]
    o = o.reshape(B, dil, Lp, H, Dh)[:, :, :L].transpose(0, 2, 1, 3, 4).reshape(B, S, H, Dh)
    lse = lse.transpose(0, 1, 2, 4, 3).reshape(B, dil, Lp, H)[:, :, :L]
    lse = lse.transpose(0, 2, 1, 3).reshape(B, S, H)
    return o, lse

def dilated_mixture_attention(q, k, v):
    B, S, _, Dh = q.shape
    outs, lses = [], []
    for gi, (window, dil) in enumerate(ATTN_GROUPS):
        hs = slice(gi * HEADS_PER_GROUP, (gi + 1) * HEADS_PER_GROUP)
        o, l = dilated_window_attention(q[:, :, hs], k[:, :, hs], v[:, :, hs], dil, window // dil)
        outs.append(o)
        lses.append(l)
    o = jnp.stack(outs, axis=0).astype(jnp.float32)
    w = jax.nn.softmax(jnp.stack(lses, axis=0), axis=0)[..., None]
    y = jnp.sum(w * o, axis=0).astype(q.dtype)
    return y.reshape(B, S, ATTN_OUT_WIDTH)

def multiscale_pool(p, mix, scale):
    B, S, C = p.shape
    p32 = p.astype(jnp.float32)
    cs = jnp.concatenate([jnp.zeros((B, 1, C), jnp.float32), lax.cumsum(p32, axis=1)], axis=1)
    t = jnp.arange(S)
    outs = []
    for g, w in enumerate(POOL_WINDOWS):
        sl = slice(g * POOL_GROUP, (g + 1) * POOL_GROUP)
        c_g = cs[..., sl]
        lo = jnp.concatenate([jnp.zeros((B, w - 1, POOL_GROUP), jnp.float32), c_g[:, :S - w + 1]], axis=1)
        mean = (c_g[:, 1:] - lo) / jnp.minimum(t + 1, w).astype(jnp.float32)[None, :, None]
        outs.append(mean - p32[..., sl])
    d = jnp.stack(outs, axis=2).astype(p.dtype)
    y = jnp.einsum('bsgc,gcd->bsgd', d, mix).reshape(B, S, C)
    return y * scale

def peer_ffn(xn, w_query, sub_keys, w_down, w_up):
    B, S, D = xn.shape
    q = jnp.einsum('bsd,de->bse', xn, w_query).reshape(B, S, PEER_HEADS, 2, PEER_HALF)
    s = jnp.einsum('bshpd,hpnd->bshpn', q, sub_keys).astype(jnp.float32)
    top_s, top_i = lax.top_k(s, PEER_TOPK)
    cand = top_s[..., 0, :, None] + top_s[..., 1, None, :]
    cand_s, cand_i = lax.top_k(cand.reshape(B, S, PEER_HEADS, PEER_TOPK * PEER_TOPK), PEER_TOPK)
    i1 = jnp.take_along_axis(top_i[..., 0, :], cand_i // PEER_TOPK, axis=-1)
    i2 = jnp.take_along_axis(top_i[..., 1, :], cand_i % PEER_TOPK, axis=-1)
    expert = i1 * PEER_N_KEYS + i2
    gates = jax.nn.softmax(cand_s, axis=-1).astype(xn.dtype)
    n_chunk = (B * S) // PEER_CHUNK
    xs = xn.reshape(n_chunk, PEER_CHUNK, D)
    ids = expert.reshape(n_chunk, PEER_CHUNK, PEER_HEADS * PEER_TOPK)
    gs = gates.reshape(n_chunk, PEER_CHUNK, PEER_HEADS * PEER_TOPK)

    def one_block(args):
        xc, ic, gc = args
        u = jnp.take(w_down, ic, axis=0)
        a = jax.nn.gelu(jnp.einsum('cd,ced->ce', xc, u), approximate=False) * gc
        vv = jnp.take(w_up, ic, axis=0)
        return jnp.einsum('ce,ced->cd', a, vv)

    out = lax.map(one_block, (xs, ids, gs))
    return out.reshape(B, S, D)

def first_inputs(seed: int = 0) -> dict:
    key = jax.random.key(seed)
    ks = jax.random.split(key, 17)
    f32 = jnp.float32

    def nrm(k, shape, scale):
        return jax.random.normal(k, shape, f32) * scale

    n_pool = len(POOL_WINDOWS)
    return {
        'x': nrm(ks[0], (BATCH, SEQ, D_MODEL), 1.0),
        'c': nrm(ks[1], (BATCH, D_MODEL), 1.0),
        'ada_w': nrm(ks[2], (DEPTH, D_MODEL, 6 * D_MODEL), 0.5 * D_MODEL ** -0.5),
        'ada_b': nrm(ks[3], (DEPTH, 6 * D_MODEL), 0.02),
        'norm1_g': 1.0 + nrm(ks[4], (DEPTH, D_MODEL), 0.02),
        'w_in': nrm(ks[5], (DEPTH, D_MODEL, IN_WIDTH), D_MODEL ** -0.5),
        'pool_mix': nrm(ks[6], (DEPTH, n_pool, POOL_GROUP, POOL_GROUP), POOL_GROUP ** -0.5),
        'pool_scale': 1.0 + nrm(ks[7], (DEPTH, POOL_WIDTH), 0.1),
        'w_attn_branch': nrm(ks[8], (DEPTH, ATTN_OUT_WIDTH, D_MODEL), ATTN_OUT_WIDTH ** -0.5),
        'w_pool_branch': nrm(ks[9], (DEPTH, POOL_WIDTH, D_MODEL), POOL_WIDTH ** -0.5),
        'w_out': nrm(ks[10], (DEPTH, D_MODEL, D_MODEL), D_MODEL ** -0.5),
        'norm2_g': 1.0 + nrm(ks[11], (DEPTH, D_MODEL), 0.02),
        'peer_wq': nrm(ks[12], (DEPTH, D_MODEL, PEER_HEADS * PEER_QUERY_DIM), D_MODEL ** -0.5),
        'peer_keys': nrm(ks[13], (DEPTH, PEER_HEADS, 2, PEER_N_KEYS, PEER_HALF), PEER_HALF ** -0.5),
        'peer_down': nrm(ks[14], (DEPTH, PEER_N_EXPERTS, D_MODEL), D_MODEL ** -0.5),
        'peer_up': nrm(ks[15], (DEPTH, PEER_N_EXPERTS, D_MODEL), PEER_HEADS ** -0.5),
        'final_g': 1.0 + nrm(ks[16], (D_MODEL,), 0.02),
    }

def first_block(x, c, ada_w, ada_b, norm1_g, w_in, pool_mix, pool_scale, w_attn_branch, w_pool_branch, w_out, norm2_g, peer_wq, peer_keys, peer_down, peer_up, final_g):
    B, S, D = x.shape
    pos = jnp.arange(S, dtype=jnp.float32)
    h = x
    for layer in range(DEPTH):
        mod = jax.nn.silu(c) @ ada_w[layer] + ada_b[layer]
        shift1, scale1, gate1, shift2, scale2, gate2 = jnp.split(mod[:, None, :], 6, axis=-1)

        xn = rms_norm(h, norm1_g[layer]) * (1.0 + scale1) + shift1
        proj = xn @ w_in[layer]
        q = proj[..., :ATTN_WIDTH].reshape(B, S, N_ATTN_HEADS, HEAD_DIM)
        k = proj[..., ATTN_WIDTH:2 * ATTN_WIDTH].reshape(B, S, N_ATTN_HEADS, HEAD_DIM)
        v = proj[..., 2 * ATTN_WIDTH:3 * ATTN_WIDTH].reshape(B, S, N_ATTN_HEADS, HEAD_DIM)
        off = 3 * ATTN_WIDTH
        p_in = proj[..., off:off + POOL_WIDTH]
        gate_a = jax.nn.sigmoid(proj[..., off + POOL_WIDTH:off + POOL_WIDTH + D])
        gate_b = jax.nn.sigmoid(proj[..., off + POOL_WIDTH + D:])
        q = apply_rope(q, pos)
        k = apply_rope(k, pos)
        attn = dilated_mixture_attention(q, k, v)
        pool = multiscale_pool(p_in, pool_mix[layer], pool_scale[layer])
        merged = gate_a * (attn @ w_attn_branch[layer]) + gate_b * (pool @ w_pool_branch[layer])
        h = h + gate1 * (merged @ w_out[layer])

        xn2 = rms_norm(h, norm2_g[layer]) * (1.0 + scale2) + shift2
        h = h + gate2 * peer_ffn(xn2, peer_wq[layer], peer_keys[layer], peer_down[layer], peer_up[layer])
    return rms_norm(h, final_g)


CTX_LEN = 256
GRID_W = 64

DA_HEADS = 8
DA_HALF = HEAD_DIM // 2
MLA_HEADS = 8
MLA_NOPE = 128
MLA_ROPE = 64
MLA_V = 128
Q_RANK = 384
KV_RANK = 256
ROPE_DIM = 64
ROPE_BASE = 10000.0
D_FF = 5632
CONV_W = 3
N_MOD = 6
Q_BLOCK = 128

DA_WIDTH = DA_HEADS * HEAD_DIM
MLA_WIDTH = MLA_HEADS * MLA_V
MIX_WIDTH = DA_WIDTH + MLA_WIDTH
MLA_QK = MLA_NOPE + MLA_ROPE
IN_WIDTH_2 = 3 * DA_WIDTH + Q_RANK + KV_RANK + MLA_ROPE
DA_SCALE = 1.0 / math.sqrt(DA_HALF)
MLA_SCALE = 1.0 / math.sqrt(MLA_QK)


def _rmsnorm(x, w):
    xf = x.astype(jnp.float32)
    y = xf * lax.rsqrt(jnp.mean(xf * xf, axis=-1, keepdims=True) + EPS)
    return y.astype(x.dtype) * w

def _modulate(h, shift, scale):
    return h * (1.0 + scale) + shift

def _axial_rope_tables(n_tokens):
    rows = n_tokens // GRID_W
    row = jnp.broadcast_to(jnp.arange(rows)[:, None], (rows, GRID_W)).reshape(-1).astype(jnp.float32)
    col = jnp.broadcast_to(jnp.arange(GRID_W)[None, :], (rows, GRID_W)).reshape(-1).astype(jnp.float32)
    nf = ROPE_DIM // 4
    inv = ROPE_BASE ** (-jnp.arange(nf, dtype=jnp.float32) / nf)
    ang_r = row[:, None] * inv
    ang_c = col[:, None] * inv
    return (jnp.cos(ang_r), jnp.sin(ang_r), jnp.cos(ang_c), jnp.sin(ang_c))

def _rot(x, cos, sin):
    cos = cos.astype(x.dtype)
    sin = sin.astype(x.dtype)
    x1, x2 = jnp.split(x, 2, axis=-1)
    return jnp.concatenate([x1 * cos - x2 * sin, x2 * cos + x1 * sin], axis=-1)

def _axial_rope(x, tabs):
    cos_r, sin_r, cos_c, sin_c = tabs
    xr, xc = jnp.split(x, 2, axis=-1)
    return jnp.concatenate([_rot(xr, cos_r, sin_r), _rot(xc, cos_c, sin_c)], axis=-1)

def _mixer_inputs(h, tabs, w_in, q_norm_w, kv_norm_w, w_uq, w_ukv):
    B, T, _ = h.shape
    p = h @ w_in
    o1, o2, o3 = DA_WIDTH, 2 * DA_WIDTH, 3 * DA_WIDTH
    o4 = o3 + Q_RANK
    o5 = o4 + KV_RANK

    def heads(a, n):
        return a.reshape(B, T, n, -1).transpose(0, 2, 1, 3)

    q_da = heads(p[..., :o1], DA_HEADS)
    k_da = heads(p[..., o1:o2], DA_HEADS)
    v_da = heads(p[..., o2:o3], DA_HEADS)
    c_q = _rmsnorm(p[..., o3:o4], q_norm_w)
    c_kv = _rmsnorm(p[..., o4:o5], kv_norm_w)
    k_rope = p[..., o5:][:, None]
    q_mla = heads(c_q @ w_uq, MLA_HEADS)
    kv = heads(c_kv @ w_ukv, MLA_HEADS)
    q_nope, q_rope = q_mla[..., :MLA_NOPE], q_mla[..., MLA_NOPE:]
    k_nope, v_mla = kv[..., :MLA_NOPE], kv[..., MLA_NOPE:]
    if tabs is not None:
        q_da = jnp.concatenate([_axial_rope(q_da[..., :DA_HALF], tabs), _axial_rope(q_da[..., DA_HALF:], tabs)], -1)
        k_da = jnp.concatenate([_axial_rope(k_da[..., :DA_HALF], tabs), _axial_rope(k_da[..., DA_HALF:], tabs)], -1)
        q_rope = _axial_rope(q_rope, tabs)
        k_rope = _axial_rope(k_rope, tabs)
    q_mla = jnp.concatenate([q_nope, q_rope], axis=-1)
    k_mla = jnp.concatenate([k_nope, jnp.broadcast_to(k_rope, (B, MLA_HEADS, T, MLA_ROPE))], axis=-1)
    return q_da, k_da, v_da, q_mla, k_mla, v_mla

def _diff_attend(q, k, v, lam):
    q1, q2 = jnp.split(q, 2, axis=-1)
    k1, k2 = jnp.split(k, 2, axis=-1)
    s1 = jnp.einsum('bhqd,bhkd->bhqk', q1, k1).astype(jnp.float32) * DA_SCALE
    s2 = jnp.einsum('bhqd,bhkd->bhqk', q2, k2).astype(jnp.float32) * DA_SCALE
    w = jax.nn.softmax(s1, axis=-1) - lam * jax.nn.softmax(s2, axis=-1)
    return jnp.einsum('bhqk,bhkd->bhqd', w.astype(v.dtype), v)

def _softmax_attend(q, k, v, scale):
    s = jnp.einsum('bhqd,bhkd->bhqk', q, k).astype(jnp.float32) * scale
    p = jax.nn.softmax(s, axis=-1)
    return jnp.einsum('bhqk,bhkd->bhqd', p.astype(v.dtype), v)

def _sweep(block_fn, q):
    B, H, S, d = q.shape
    nb = S // Q_BLOCK
    qb = q.reshape(B, H, nb, Q_BLOCK, d).transpose(2, 0, 1, 3, 4)
    out = lax.map(block_fn, qb)
    return out.transpose(1, 2, 0, 3, 4).reshape(B, H, S, out.shape[-1])

def _merge_heads(o_da, o_mla, subln_w, lambda_init):
    o_da = _rmsnorm(o_da, subln_w) * (1.0 - lambda_init)
    B, _, T, _ = o_da.shape
    o_da = o_da.transpose(0, 2, 1, 3).reshape(B, T, DA_WIDTH)
    o_mla = o_mla.transpose(0, 2, 1, 3).reshape(B, T, MLA_WIDTH)
    return jnp.concatenate([o_da, o_mla], axis=-1)

def _conv_ffn(h, w_up, conv_w, conv_b, w_down):
    g, u = jnp.split(h @ w_up, 2, axis=-1)
    T = g.shape[1]
    pad = CONV_W // 2
    gp = jnp.pad(g, ((0, 0), (pad, pad), (0, 0)))
    g = sum(gp[:, j:j + T] * conv_w[j] for j in range(CONV_W)) + conv_b
    return (jax.nn.silu(g) * u) @ w_down

def second_inputs(seed: int = 0) -> dict:
    key = jax.random.key(seed)
    ks = jax.random.split(key, 24)
    f32 = jnp.float32

    def nrm(k, shape, fan_in, gain=1.0):
        return (gain * fan_in ** -0.5) * jax.random.normal(k, shape, f32)

    def gain(k, shape):
        return 1.0 + 0.05 * jax.random.normal(k, shape, f32)

    L = DEPTH
    return {
        "x": jax.random.normal(ks[0], (BATCH, SEQ, D_MODEL), f32),
        "c": jax.random.normal(ks[1], (BATCH, D_MODEL), f32),
        "ctx": jax.random.normal(ks[2], (BATCH, CTX_LEN, D_MODEL), f32),
        "c_ctx": jax.random.normal(ks[3], (D_MODEL,), f32),
        "w_ada": nrm(ks[4], (L, D_MODEL, N_MOD * D_MODEL), D_MODEL, 0.5),
        "b_ada": 0.02 * jax.random.normal(ks[5], (L, N_MOD * D_MODEL), f32),
        "norm1_w": gain(ks[6], (L, D_MODEL)),
        "w_in": nrm(ks[7], (L, D_MODEL, IN_WIDTH_2), D_MODEL),
        "q_norm_w": gain(ks[8], (L, Q_RANK)),
        "kv_norm_w": gain(ks[9], (L, KV_RANK)),
        "w_uq": nrm(ks[10], (L, Q_RANK, MLA_HEADS * MLA_QK), Q_RANK),
        "w_ukv": nrm(ks[11], (L, KV_RANK, MLA_HEADS * (MLA_NOPE + MLA_V)), KV_RANK),
        "lambda_q1": 0.1 * jax.random.normal(ks[12], (L, DA_HALF), f32),
        "lambda_k1": 0.1 * jax.random.normal(ks[13], (L, DA_HALF), f32),
        "lambda_q2": 0.1 * jax.random.normal(ks[14], (L, DA_HALF), f32),
        "lambda_k2": 0.1 * jax.random.normal(ks[15], (L, DA_HALF), f32),
        "subln_w": gain(ks[16], (L, HEAD_DIM)),
        "w_o": nrm(ks[17], (L, MIX_WIDTH, D_MODEL), MIX_WIDTH),
        "norm2_w": gain(ks[18], (L, D_MODEL)),
        "w_up": nrm(ks[19], (L, D_MODEL, 2 * D_FF), D_MODEL),
        "conv_w": nrm(ks[20], (L, CONV_W, D_FF), CONV_W),
        "conv_b": 0.02 * jax.random.normal(ks[21], (L, D_FF), f32),
        "w_down": nrm(ks[22], (L, D_FF, D_MODEL), D_FF),
        "final_w": gain(ks[23], (D_MODEL,)),
    }

def second_block(x, c, ctx, c_ctx, w_ada, b_ada, norm1_w, w_in, q_norm_w, kv_norm_w, w_uq, w_ukv,
              lambda_q1, lambda_k1, lambda_q2, lambda_k2, subln_w, w_o, norm2_w, w_up,
              conv_w, conv_b, w_down, final_w):
    B, S, D = x.shape
    tabs = _axial_rope_tables(S)
    xc = jnp.broadcast_to(ctx, ctx.shape)
    sc_ = jax.nn.silu(c)
    scc = jax.nn.silu(c_ctx)
    for l in range(DEPTH):
        mod_x = (sc_ @ w_ada[l] + b_ada[l])[:, None, :]
        mod_c = (scc @ w_ada[l] + b_ada[l])[None, None, :]
        sh1, s1, g1, sh2, s2, g2 = jnp.split(mod_x, N_MOD, axis=-1)
        sh1c, s1c, g1c, sh2c, s2c, g2c = jnp.split(mod_c, N_MOD, axis=-1)
        lambda_init = 0.8 - 0.6 * math.exp(-0.3 * l)
        lam = (jnp.exp(jnp.sum(lambda_q1[l].astype(jnp.float32) * lambda_k1[l].astype(jnp.float32)))
               - jnp.exp(jnp.sum(lambda_q2[l].astype(jnp.float32) * lambda_k2[l].astype(jnp.float32)))
               + lambda_init)
        proj = (w_in[l], q_norm_w[l], kv_norm_w[l], w_uq[l], w_ukv[l])

        h = _modulate(_rmsnorm(x, norm1_w[l]), sh1, s1)
        hc = _modulate(_rmsnorm(xc, norm1_w[l]), sh1c, s1c)
        q_da, k_da, v_da, q_mla, k_mla, v_mla = _mixer_inputs(h, tabs, *proj)
        qc_da, kc_da, vc_da, qc_mla, kc_mla, vc_mla = _mixer_inputs(hc, None, *proj)
        k_da_all = jnp.concatenate([kc_da, k_da], axis=2)
        v_da_all = jnp.concatenate([vc_da, v_da], axis=2)
        k_mla_all = jnp.concatenate([kc_mla, k_mla], axis=2)
        v_mla_all = jnp.concatenate([vc_mla, v_mla], axis=2)
        o_da = _sweep(lambda qb: _diff_attend(qb, k_da_all, v_da_all, lam), q_da)
        o_mla = _sweep(lambda qb: _softmax_attend(qb, k_mla_all, v_mla_all, MLA_SCALE), q_mla)
        x = x + g1 * (_merge_heads(o_da, o_mla, subln_w[l], lambda_init) @ w_o[l])

        h2 = _modulate(_rmsnorm(x, norm2_w[l]), sh2, s2)
        x = x + g2 * _conv_ffn(h2, w_up[l], conv_w[l], conv_b[l], w_down[l])

        if l < DEPTH - 1:
            oc_da = _diff_attend(qc_da, kc_da, vc_da, lam)
            oc_mla = _softmax_attend(qc_mla, kc_mla, vc_mla, MLA_SCALE)
            xc = xc + g1c * (_merge_heads(oc_da, oc_mla, subln_w[l], lambda_init) @ w_o[l])
            hc2 = _modulate(_rmsnorm(xc, norm2_w[l]), sh2c, s2c)
            xc = xc + g2c * _conv_ffn(hc2, w_up[l], conv_w[l], conv_b[l], w_down[l])
    return _rmsnorm(x, final_w)


def setup_inputs(seed=0):
    out = dict(first_inputs(seed))
    for name, value in second_inputs(seed + 1).items():
        if name != "x":
            out[name + "_2"] = value
    return out


def reference(
    x, c, ada_w, ada_b, norm1_g, w_in, pool_mix, pool_scale, w_attn_branch, w_pool_branch,
    w_out, norm2_g, peer_wq, peer_keys, peer_down, peer_up, final_g, c_2, ctx_2, c_ctx_2,
    w_ada_2, b_ada_2, norm1_w_2, w_in_2, q_norm_w_2, kv_norm_w_2, w_uq_2, w_ukv_2, lambda_q1_2,
    lambda_k1_2, lambda_q2_2, lambda_k2_2, subln_w_2, w_o_2, norm2_w_2, w_up_2, conv_w_2,
    conv_b_2, w_down_2, final_w_2,
):
    x = first_block(
        x, c, ada_w, ada_b, norm1_g, w_in, pool_mix, pool_scale, w_attn_branch, w_pool_branch,
        w_out, norm2_g, peer_wq, peer_keys, peer_down, peer_up, final_g,
    )
    return second_block(
        x, c_2, ctx_2, c_ctx_2, w_ada_2, b_ada_2, norm1_w_2, w_in_2, q_norm_w_2, kv_norm_w_2,
        w_uq_2, w_ukv_2, lambda_q1_2, lambda_k1_2, lambda_q2_2, lambda_k2_2, subln_w_2, w_o_2,
        norm2_w_2, w_up_2, conv_w_2, conv_b_2, w_down_2, final_w_2,
    )


_drawn_inputs = setup_inputs


def setup_inputs(seed=0):
    import zlib

    import numpy as np

    out = dict(_drawn_inputs(seed))
    spreads = {}
    factors = {'ada_b': 3.513,
     'norm1_g': 8.0,
     'pool_scale': 3.372,
     'norm2_g': 6.858,
     'final_g': 2.877,
     'norm1_w_2': 7.817,
     'q_norm_w_2': 8.0,
     'kv_norm_w_2': 8.0,
     'w_uq_2': 3.122,
     'lambda_q1_2': 4.538,
     'lambda_q2_2': 8.0,
     'lambda_k2_2': 8.0,
     'subln_w_2': 17.28,
     'norm2_w_2': 3.768,
     'conv_b_2': 8.0}
    for name, (base, spread) in spreads.items():
        noise = np.random.default_rng([zlib.crc32(name.encode()), seed]).standard_normal(out[name].shape)
        drawn = base * np.exp(spread * noise) if base else spread * noise
        out[name] = jnp.asarray(drawn.astype(out[name].dtype))
    for name, factor in factors.items():
        out[name] = (out[name] * factor).astype(out[name].dtype)
    return out
```

```python
from contextlib import ExitStack

import numpy as np
import concourse.bass as bass
from concourse import mybir

ALU = mybir.AluOpType
ACT = mybir.ActivationFunctionType
AX = mybir.AxisListType.X
F32 = mybir.dt.float32
U32 = mybir.dt.uint32

P = 128
T = 256
D = 2048
KC = D // P
EPS = 1e-6
NEG = -3.0e38
MASKED = -1.0e30

HEADS = 12
SLOTS = 4
GROUPS = ((128, 1), (512, 4), (2048, 16))
SM1 = 128 ** -0.5
POOLS = (2, 4, 8, 16)
PAD = 16
EH = 8
TOPK = 16
NKEY = 128
NG = 8
BLK = 16
NBLK = T // BLK

CTX = 256
TA = CTX + T
H2 = 8
SM_DA = 64 ** -0.5
SM_MLA = 192 ** -0.5
LAMBDA_INIT = 0.8 - 0.6
FF = 5632 // P

RING = 4
BANKS = 4
U = 8
TWO = 2

TILES = {}
_t = 0
for _name, _n in (("qk", 24), ("v", 12), ("gate", 36), ("branch", 8), ("wo", 16), ("wq", 16),
                  ("peer", 256), ("in2", 30), ("ukv", 2), ("uq", 4), ("wo2", 16), ("up", 88), ("down", 64)):
    TILES[_name] = _t
    _t += _n

OUTS = {}
_t = 0
for _name, _n in (("qk", 24), ("v", 12), ("gate", 40), ("branch", 32), ("wo", 16), ("wq", 16), ("key", 8),
                  ("peer", 256), ("q2", 8), ("k2", 8), ("v2", 8), ("c2", 6), ("ukv", 16), ("uq", 16),
                  ("wo2", 16), ("up", 88), ("down", 16), ("end", 0)):
    OUTS[_name] = _t
    _t += _n
MIX_AFTER = 35

CONST = {}
_t = 0
for _name, _n in (("mask0", 3 * P), ("mask1", 3 * T), ("cos1", T), ("sin1", T), ("perm1", P), ("ident", P),
                  ("ones", P), ("cos2", T), ("sin2", T), ("perm2", P), ("iota", P), ("rcount", 4 * T)):
    CONST[_name] = (_t, _t + _n)
    _t += _n
N_CONST = _t
VEC = {}
_t = 0
for _name, _n in (("ada_b", 96), ("norm1_g", 16), ("norm2_g", 16), ("final_g", 16), ("pool_scale", 4),
                  ("b_ada_2", 96), ("norm1_w_2", 16), ("q_norm_w_2", 3), ("kv_norm_w_2", 2), ("subln_w_2", 1),
                  ("norm2_w_2", 16), ("final_w_2", 16), ("conv_w_2", 3 * FF), ("conv_b_2", FF),
                  ("lambda_q1_2", 64), ("lambda_k1_2", 64), ("lambda_q2_2", 64), ("lambda_k2_2", 64)):
    VEC[_name] = (_t, _t + _n)
    _t += _n
N_VEC = _t

NORMS = (("a1", KC, T, D, True), ("b1", KC, T, D, True), ("f1", KC, T, D, False), ("ctx", KC, T, D, True),
         ("a2", KC, T, D, True), ("kv", 2, TA, 2 * P, False), ("q", 3, T, 3 * P, False),
         ("b2", KC, T, D, True), ("f2", KC, T, D, False))
NORM_AT = {n[0]: i for i, n in enumerate(NORMS)}


def before(name, what):
    ahead = NORMS[:NORM_AT[name]]
    if what == "squares":
        return sum(max(1, n[1] // 4) for n in ahead)
    if what == "scaled":
        return sum(n[1] for n in ahead)
    return sum(n[1] for n in ahead if n[4])


class Chain:

    def __init__(self, eng, sem):
        self.eng, self.sem, self.n, self.turn = eng, sem, 0, None

    def tick(self, ins):
        ins.then_inc(self.sem, 1)
        self.n += 1

    def sync(self):
        if self.turn is None:
            self.eng.wait_ge(self.sem, self.n)
        else:
            base, i, per = self.turn
            self.eng.wait_ge(self.sem, i * per + (base + self.n))

    def link(self, ins):
        self.tick(ins)
        self.sync()

    def enter(self, i, per):
        self.turn = (self.n, i, per)
        self.n = 0

    def leave(self, turns):
        base, _, per = self.turn
        assert self.n == per, (self.n, per)
        self.n, self.turn = base + per * turns, None


def build_program(nc, A, out):
    with ExitStack() as ctx:
        def sb(name, shape, dt=F32):
            return ctx.enter_context(nc.sbuf_tensor(name, shape, dt))

        def sem(name):
            return ctx.enter_context(nc.semaphore(name))

        hT = sb("hT", [P, KC, T])
        ring = sb("ring", [P, RING, D])
        ada = sb("ada", [P, 2, D])
        cb = sb("cb", [P, 2, D])
        const = sb("const", [P, N_CONST])
        vec = sb("vec", [P, N_VEC])
        mod1 = sb("mod1", [P, 96])
        mod2 = sb("mod2", [P, 96])
        modc = sb("modc", [P, 32])
        modt = sb("modt", [P, 16])
        coef = sb("coef", [P, KC])
        rs = sb("rs", [P, TA])
        small = sb("small", [P, 16])
        arena = sb("arena", [P, 105 * 256])
        ps = ctx.enter_context(nc.psum_tensor("ps", [P, 8, 512], F32))
        gates_dram = nc.dram_tensor("gates_scratch", (NG, P, NBLK, 16 * BLK), F32, kind="Internal").ap()

        def room(kb, *shape, dt=F32):
            n = int(np.prod(shape))
            at = int(kb * 256)
            assert at + n <= 105 * 256, (kb, shape)
            v = arena[:, at:at + n]
            if dt is not F32:
                v = v.bitcast(dt)
            if len(shape) == 2:
                return v.rearrange("p (a b) -> p a b", a=shape[0])
            if len(shape) == 3:
                return v.rearrange("p (a b c) -> p a b c", a=shape[0], b=shape[1])
            return v

        def cst(name):
            return const[:, CONST[name][0]:CONST[name][1]]

        def vc(name):
            return vec[:, VEC[name][0]:VEC[name][1]]

        X = room(0, KC, T)
        qk = room(16, 24, T)
        v1 = room(40, 2, HEADS * P)
        ga = room(52, KC, T)
        gb = room(68, KC, T)
        pads = [room(84 + 4.25 * j, 4, PAD + T) for j in range(3)]
        attn = room(96.75, SLOTS, T)
        pool = room(100.75, 4, T)
        cbt = cb[:, 1, :]
        rope_a = cbt[:, 0:512].rearrange("p (a b) -> p a b", a=2)
        rope_b = cbt[:, 512:1024].rearrange("p (a b) -> p a b", a=2)
        sc1 = cbt[:, 0:768].rearrange("p (a b) -> p a b", a=3)
        pt1 = cbt[:, 768:1536]
        mixw = cbt[:, 1536:2048].rearrange("p (a b) -> p a b", a=4)
        pq = room(16, KC, T)
        keys = room(32, KC, NKEY)
        score = [room(40, KC, NKEY), room(48, KC, NKEY)]
        cand = cb[:, 0, :].rearrange("p (h i) -> p h i", h=EH)
        eq = cb[:, 1, :].rearrange("p (h k j) -> p h k j", h=EH, k=TOPK)
        oh1 = [room(56 + 8 * j, 8, P) for j in range(2)]
        oh2 = [room(60 + 8 * j, 8, P) for j in range(2)]
        stage = [room(72 + 8 * j, P, BLK) for j in range(2)]
        topv = room(88, KC, TOPK)
        topi = room(89, KC, TOPK, dt=U32)
        topf = room(90, KC, TOPK)
        cv = room(91, EH, TOPK)
        ci = room(91.5, EH, TOPK, dt=U32)
        ca = room(92, EH, TOPK, dt=U32)
        cbi = room(92.5, EH, TOPK, dt=U32)
        caf = room(93, EH, TOPK)
        cbf = room(93.5, EH, TOPK)
        ids = room(94, 3, EH * TOPK)
        idT = room(96, 3, T)
        gsum = room(99, EH)
        G = room(16, NBLK, 16 * BLK)
        AT = room(32, 16, T)
        junk = room(48, D)
        gl = room(99.5, 2, T)
        ctxT = room(56, KC, T)
        X2 = room(72, KC, TA)
        q2 = room(0, H2, T)
        k2 = room(8, H2, TA)
        v2 = room(24, 4, H2 * P)
        cq = room(40, 3, T)
        ckv = room(43, 2, TA)
        kr = room(47, TA)
        vm = room(49, 4, H2 * P)
        sq2 = room(65, 4, T)
        rope2 = [room(65 + 2 * j, 2, T) for j in range(2)]
        kn = room(72, H2, TA)
        qm = room(88, 2 * H2, T)
        mix = cb[:, :, :].rearrange("p a (b c) -> p (a b) c", c=T)
        adaf = ada[:, :, :].rearrange("p a b -> p (a b)")
        prob = [adaf[:, 1024 * j:1024 * j + 1024].rearrange("p (a b) -> p a b", a=2) for j in range(2)]
        wt2 = [adaf[:, 2048 + 512 * j:2560 + 512 * j] for j in range(2)]
        rs8 = room(0, H2, T)
        sq8 = room(8, H2, T)
        hid = room(16, FF, T)
        gp = [room(60 + 1.25 * j, T + 2) for j in range(2)]
        gc = [room(63 + j, T) for j in range(2)]

        def rope_step(n):
            if n < 4:
                return q2[:, 2 * n:2 * n + 2, :], 2 * T
            if n < 8:
                return k2[:, 2 * (n - 4):2 * (n - 4) + 2, CTX:], 2 * T
            if n < 12:
                return qm[:, H2 + 2 * (n - 8):H2 + 2 * (n - 8) + 2, :], 2 * T
            return kr[:, CTX:].unsqueeze(1), T

        w_slot = [sem(f"w_slot{j}") for j in range(RING)]
        quarter_used = sem("quarter_used")
        acc_full = sem("acc_full")
        acc_free = sem("acc_free")
        a_slot = [sem(f"a_slot{j}") for j in range(2)]
        a_free = sem("a_free")
        x_in = sem("x_in")
        c_in = sem("c_in")
        const_in = sem("const_in")
        keys_in = sem("keys_in")
        c2_in = sem("c2_in")
        ctx_in = sem("ctx_in")
        c_silu = sem("c_silu")
        zeroed = sem("zeroed")
        dve_done = sem("dve_done")
        act_done = sem("act_done")
        squared = sem("squared")
        summed = sem("summed")
        var_ready = sem("var_ready")
        std_ready = sem("std_ready")
        scaled = sem("scaled")
        shifted = sem("shifted")
        rotated = sem("rotated")
        roped = sem("roped")
        s_ready = sem("s_ready")
        max_ready = sem("max_ready")
        exp_ready = sem("exp_ready")
        p_ready = sem("p_ready")
        pt_ready = sem("pt_ready")
        pt_copied = sem("pt_copied")
        o_ready = sem("o_ready")
        o_copied = sem("o_copied")
        pooled = sem("pooled")
        merged = sem("merged")
        h_ready = sem("h_ready")
        score_in = sem("score_in")
        cand_ready = sem("cand_ready")
        gate_exp = sem("gate_exp")
        ids_ready = sem("ids_ready")
        ids_turned = sem("ids_turned")
        ids_copied = sem("ids_copied")
        oh_dve = sem("oh_dve")
        oh_pool = sem("oh_pool")
        g_full = sem("g_full")
        g_copied = sem("g_copied")
        g_stored = [sem(f"g_stored{j}") for j in range(2)]
        g_in = sem("g_in")
        gelu_done = sem("gelu_done")
        at_ready = sem("at_ready")
        lam_exp = sem("lam_exp")
        sub_sq = sem("sub_sq")
        sub_sum = sem("sub_sum")
        sub_var = sem("sub_var")
        sub_std = sem("sub_std")
        mixed = sem("mixed")
        g_row = sem("g_row")
        conv_ready = sem("conv_ready")
        silu_done = sem("silu_done")
        out_done = sem("out_done")

        block = ctx.enter_context(nc.Block())

        @block.sync
        def _(sp):
            def load(slot, src, made, n=D):
                if made is not None:
                    sp.wait_ge(acc_full, made)
                sp.dma_start(ring[:, slot % RING, 0:n], src).then_inc(w_slot[slot % RING], 16)

            def stream(name, src, count, n=D, o_name=None):
                o = OUTS[o_name or name]
                with sp.Fori(0, count // U) as i:
                    for u in range(U):
                        load(u, src[i * U + u], i * U + (o + u + 1 - RING), n)

            sp.dma_start(hT[:], A["x"]).then_inc(x_in, 16)
            sp.dma_start(cb[:, 0, :], A["c"]).then_inc(c_in, 16)
            sp.dma_start(const[:], A["const"]).then_inc(const_in, 16)
            sp.dma_start(vec[:], A["vec"]).then_inc(const_in, 16)
            sp.dma_start(mixw, A["pool_mix"]).then_inc(const_in, 16)
            for u in range(RING):
                load(u, A["w_in"][u], None)
            with sp.Fori(0, 72 // RING - 1) as i:
                for u in range(RING):
                    load(u, A["w_in"][i * RING + (RING + u)], i * RING + (u + 1))
            for t in range(8):
                load(t, A["w_branch"][t], 72 - RING + t + 1 if t < RING else OUTS["branch"] + 4 * (t - RING + 1))
            stream("wo", A["w_out"], 16)
            stream("wq", A["peer_wq"], 16)
            with sp.Fori(0, NG) as i:
                for u in range(32):
                    src = A["peer_down"] if u < 16 else A["peer_up"]
                    load(u, src[i * 16 + u % 16], i * 32 + (OUTS["peer"] + u + 1 - RING))
            with sp.Fori(0, 3) as i:
                for u in range(U):
                    load(u, A["w_in_2"][i * U + u], i * U + (OUTS["q2"] + u + 1 - RING))
            for u in range(24, 30):
                load(u, A["w_in_2"][u], OUTS["q2"] + u + 1 - RING)
            for t in range(2):
                load(TILES["ukv"] + t, A["w_ukv_2"][t], OUTS["ukv"] + t + 1 - RING)
            for t in range(4):
                load(TILES["uq"] + t, A["w_uq_2"][t], OUTS["ukv"] + t - 1 if t < 2 else OUTS["ukv"] + 8 * (t - 1),
                     12 * P)
            for t in range(16):
                load(TILES["wo2"] + t, A["w_o_2"][t],
                     OUTS["uq"] + 4 * (t + 1) if t < RING else OUTS["wo2"] + t + 1 - RING)
            stream("up", A["w_up_2"], 88)
            for q in range(4):
                load(q, A["w_down_2"][q], OUTS["down"] + q + 1 - RING, 11 * P)
            with sp.Fori(0, KC - 1) as i:
                for q in range(4):
                    if q < 3:
                        sp.wait_ge(quarter_used, i * 3 + (q + 1))
                    load(q, A["w_down_2"][i * 4 + (4 + q)], i + (OUTS["down"] + 1) if q == 3 else None, 11 * P)
            sp.wait_ge(scaled, before("f2", "scaled") + KC)
            sp.dma_start(out, hT[:]).then_inc(out_done, 16)
            sp.wait_ge(out_done, 16)

        @block.gpsimd
        def _(pool_e):
            def ada_load(tile, slot, src):
                pool_e.wait_ge(a_free, tile + 1)
                pool_e.dma_start(ada[:, slot, :], src).then_inc(a_slot[slot], 16)

            with pool_e.Fori(0, 48) as i:
                for u in range(2):
                    ada_load(i * 2 + u, u, A["ada"][i * 2 + u])
            pool_e.wait_ge(o_ready, 8)
            pool_e.dma_start(keys, A["keys"]).then_inc(keys_in, 16)
            with pool_e.Fori(0, NBLK) as i:
                for j in range(2):
                    pool_e.wait_ge(oh_dve, i * 2 + (j + 1))
                    tok = bass.ds(i * 16 + 8 * j, 8)
                    nc.gpsimd.tensor_tensor(
                        oh2[j], oh2[j], idT[:, 2, tok].unsqueeze(2).broadcast_to([P, 8, P]), ALU.mult,
                    ).then_inc(oh_pool, 1)
            pool_e.wait_ge(ids_ready, 2)
            pool_e.dma_start(cb[:, 0, :], A["c_2"]).then_inc(c2_in, 16)
            pool_e.dma_start(cb[:, 1, :], A["c_ctx_2"]).then_inc(c2_in, 16)
            pool_e.wait_ge(g_full, TWO + 2 * NBLK)
            pool_e.wait_ge(g_copied, TWO + 2 * NBLK)
            pool_e.wait_ge(g_stored[0], 16 + 16 * NBLK // 2)
            pool_e.wait_ge(g_stored[1], 16 + 16 * NBLK // 2)
            pool_e.dma_start(ctxT, A["ctx"]).then_inc(ctx_in, 16)
            with pool_e.Fori(0, NG) as i:
                pool_e.wait_ge(at_ready, i * 16 + TWO)
                pool_e.dma_start(G, gates_dram[i]).then_inc(g_in, 16)
                for u in range(12):
                    ada_load(i * 12 + (96 + u), u % 2, A["ada"][i * 12 + (96 + u)])

        @block.scalar
        def _(act):
            ch = Chain(act, act_done)

            def act_fn(*a, **k):
                return nc.scalar.activation(*a, **k)

            def norm(name, src, sqd, dst, shift=None, cols=T):
                i, n = NORM_AT[name], NORMS[NORM_AT[name]][1]
                for b in range(max(1, n // 4)):
                    w = min(4, n)
                    act_fn(sqd[:, 4 * b:4 * b + w, :], src[:, 4 * b:4 * b + w, :], ACT.Square).then_inc(squared, 1)
                act.wait_ge(var_ready, i + 1)
                act_fn(rs[:, 0:cols], rs[:, 0:cols], ACT.Sqrt).then_inc(std_ready, 1)
                if shift is not None:
                    for k in range(n):
                        act.wait_ge(scaled, before(name, "scaled") + k + 1)
                        act_fn(dst[:, k, :], dst[:, k, :], ACT.Identity, bias=shift[:, k:k + 1]).then_inc(shifted, 1)

            act.wait_ge(c_in, 16)
            act_fn(cb[:, 0, :], cb[:, 0, :], ACT.Silu).then_inc(c_silu, 1)
            act.wait_ge(x_in, 16)
            norm("a1", hT, X, X, mod1[:, 0:KC])

            with act.Fori(0, 24 // U) as i:
                for u in range(U):
                    act.wait_ge(acc_full, i * U + (u + 1))
                    act_fn(qk[:, i * U + u, :], ps[:, u % BANKS, 0:T], ACT.Copy).then_inc(acc_free, 1)
            for n in range(HEADS):
                o = OUTS["v"] + n
                act.wait_ge(acc_full, o + 1)
                act_fn(v1[:, :, n * P:(n + 1) * P], ps[:, o % BANKS, 0:T].rearrange("p (a b) -> p a b", a=2),
                       ACT.Copy).then_inc(acc_free, 1)

            act.wait_ge(zeroed, 1)
            act.wait_ge(const_in, 48)
            for k in range(36):
                o = OUTS["gate"] + k + (4 if k > MIX_AFTER else 0)
                act.wait_ge(acc_full, o + 1)
                if k < 4:
                    act_fn(pads[0][:, k, PAD:], ps[:, o % BANKS, 0:T], ACT.Copy).then_inc(acc_free, 1)
                else:
                    to = ga[:, k - 4, :] if k < 20 else gb[:, k - 20, :]
                    act_fn(to, ps[:, o % BANKS, 0:T], ACT.Sigmoid).then_inc(acc_free, 1)
                if k == MIX_AFTER:
                    for g in range(4):
                        o = OUTS["gate"] + MIX_AFTER + 1 + g
                        act.wait_ge(acc_full, o + 1)
                        act_fn(pool[:, g, :], ps[:, o % BANKS, 0:T], ACT.Copy,
                               scale=vc("pool_scale")[:, g:g + 1]).then_inc(acc_free, 1)
                u = (k - 1) // 4
                if k % 4 == 1 and u < 8:
                    w = 3 * P * (u % 2 + 1)
                    act.wait_ge(max_ready, u + 1)
                    s = sc1[:, :, 0:P * (u % 2 + 1)]
                    act_fn(s, s, ACT.Exp, bias=small[:, 0:1], accum_out=small[:, 1:2]).then_inc(exp_ready, 1)
                if k % 4 == 2 and u < 8:
                    w = 3 * P * (u % 2 + 1)
                    act.wait_ge(pt_ready, u + 1)
                    if u:
                        act.wait_ge(o_ready, u)
                    act_fn(pt1[:, 0:w], ps[:, 6:8, :].rearrange("p a b -> p (a b)")[:, 0:w], ACT.Copy)\
                        .then_inc(pt_copied, 1)
                if k % 4 == 0 and k:
                    u = k // 4 - 1
                    act.wait_ge(o_ready, u + 1)
                    act_fn(attn[:, u // 2, (u % 2) * P:(u % 2 + 1) * P], ps[:, 7, 256:384], ACT.Copy)\
                        .then_inc(o_copied, 1)

            act.wait_ge(h_ready, 1)
            norm("b1", hT, X, X, mod1[:, 48:64])

            with act.Fori(0, 16 // U) as i:
                for u in range(U):
                    act.wait_ge(acc_full, i * U + (OUTS["wq"] + u + 1))
                    act_fn(pq[:, i * U + u, :], ps[:, u % BANKS, 0:T], ACT.Copy).then_inc(acc_free, 1)
            for n in range(8):
                o = OUTS["key"] + n
                act.wait_ge(acc_full, o + 1)
                act_fn(score[n // 4][:, 4 * (n % 4):4 * (n % 4) + 4, :].rearrange("p a b -> p (a b)"),
                       ps[:, o % BANKS, :], ACT.Copy).then_inc(acc_free, 1)
            for tb in range(2):
                act.wait_ge(cand_ready, tb + 1)
                act_fn(ids[:, 2, :].rearrange("p (h k) -> p h k", h=EH), cv, ACT.Exp).then_inc(gate_exp, 1)
                act.wait_ge(ids_turned, tb + 1)
                act_fn(idT[:, :, tb * P:(tb + 1) * P], ps[:, 4, 0:3 * P].rearrange("p (a b) -> p a b", a=3),
                       ACT.Copy).then_inc(ids_copied, 1)
            with act.Fori(0, NBLK // 2) as i:
                for j in range(2):
                    act.wait_ge(g_stored[j], i * 16 + 16)
                    for hv in range(2):
                        act.wait_ge(g_full, i * 4 + (TWO + 2 * j + hv + 1))
                        for q in range(2):
                            t0 = 8 * hv + 4 * q
                            ins = act_fn(stage[j][:, :, t0:t0 + 4],
                                         ps[:, 4 + 2 * hv + q, :].rearrange("p (t c) -> p c t", t=4), ACT.Copy)
                        ins.then_inc(g_copied, 1)
                    act.wait_ge(g_copied, i * 4 + (TWO + 2 * j + 2))
                    act.dma_start(gates_dram[:, :, i * 2 + j, :].rearrange("g p f -> p g f"),
                                  stage[j].rearrange("p (g c) t -> p g (c t)", g=NG)).then_inc(g_stored[j], 16)
            act.wait_ge(c2_in, 32)
            act_fn(cb[:, 0, :], cb[:, 0, :], ACT.Silu).then_inc(c_silu, 1)
            act_fn(cb[:, 1, :], cb[:, 1, :], ACT.Silu).then_inc(c_silu, 1)
            with act.Fori(0, NG) as i:
                for u in range(16):
                    act.wait_ge(acc_full, i * 32 + (OUTS["peer"] + u + 1))
                    act.wait_ge(at_ready, i * 16 + (u + TWO - 1))
                    act_fn(gl[:, u % 2, :], ps[:, u % BANKS, 0:T], ACT.Gelu).then_inc(gelu_done, 1)

            act.wait_ge(h_ready, 2)
            norm("f1", hT, X, None)
            act.wait_ge(ctx_in, 16)
            norm("ctx", ctxT, X2[:, :, 0:CTX], X2[:, :, 0:CTX], modc[:, 0:KC])
            act.wait_ge(scaled, before("f1", "scaled") + KC)
            norm("a2", hT, X2[:, :, CTX:], X2[:, :, CTX:], mod2[:, 0:KC])

            def out_copy(o, to, n=T):
                act.wait_ge(acc_full, o + 1)
                src = ps[:, o % BANKS, 0:n]
                if len(to.shape) == 3:
                    src = src.rearrange("p (a b) -> p a b", a=to.shape[1])
                return act_fn(to, src, ACT.Copy)

            def out_loop(name, to, n):
                with act.Fori(0, 2) as i:
                    for u in range(4):
                        act.wait_ge(acc_full, i * 4 + (OUTS[name] + u + 1))
                        act_fn(to[:, i * 4 + u, :], ps[:, u % BANKS, 0:n], ACT.Copy).then_inc(acc_free, 1)

            out_loop("q2", q2, T)
            out_loop("k2", k2, TA)
            with act.Fori(0, 2) as i:
                for u in range(4):
                    act.wait_ge(acc_full, i * 4 + (OUTS["v2"] + u + 1))
                    act_fn(v2[:, :, bass.ds(i * 512 + u * P, P)],
                           ps[:, u % BANKS, :].rearrange("p (a b) -> p a b", a=4), ACT.Copy).then_inc(acc_free, 1)
            for n in range(2):
                out_copy(OUTS["c2"] + n, ckv[:, n, :], TA).then_inc(acc_free, 1)
            out_copy(OUTS["c2"] + 2, kr, TA).then_inc(acc_free, 1)
            for n in range(3):
                out_copy(OUTS["c2"] + 3 + n, cq[:, n, :], T).then_inc(acc_free, 1)
            act.wait_ge(acc_free, BANKS + OUTS["ukv"])
            norm("kv", ckv, kn[:, 0:2, :], None, cols=TA)
            norm("q", cq, sq2[:, 0:3, :], None)
            for n in range(16):
                to = kn[:, n, :] if n < 8 else vm[:, :, (n - 8) * P:(n - 7) * P]
                out_copy(OUTS["ukv"] + n, to, TA).then_inc(acc_free, 1)
            for n in range(16):
                out_copy(OUTS["uq"] + n, qm[:, n, :], T).then_inc(acc_free, 1)
            act.wait_ge(max_ready, 8 + 1)
            act_fn(small[:, 8:10], small[:, 8:10], ACT.Exp).then_inc(lam_exp, 1)

            def stage_exp(u):
                two = u < 16
                act.wait_ge(max_ready, 8 + 1 + u + 1)
                for j in range(2 if two else 1):
                    ins = act_fn(prob[u % 2][:, j, :], ps[:, 2 * (u % 2) + j, :], ACT.Exp,
                                 bias=small[:, 4 * (u % 2) + j:4 * (u % 2) + j + 1],
                                 scale=SM_DA if two else SM_MLA,
                                 accum_out=small[:, 4 * (u % 2) + 2 + j:4 * (u % 2) + 3 + j])
                ins.then_inc(exp_ready, 1)

            def stage_turn(u):
                act.wait_ge(pt_ready, 8 + u + 1)
                if u >= 2:
                    act.wait_ge(o_ready, 8 + u - 1)
                act_fn(wt2[u % 2], ps[:, 4 + u % 2, :], ACT.Copy).then_inc(pt_copied, 1)

            def stage_out(u):
                head, qb = u // 2, u % 2
                act.wait_ge(o_ready, 8 + u + 1)
                act_fn(mix[:, head, qb * P:(qb + 1) * P], ps[:, 6 + u % 2, 0:P], ACT.Copy).then_inc(o_copied, 1)

            for s in range(32 + 2):
                if s < 32:
                    stage_exp(s)
                if 1 <= s <= 32:
                    stage_turn(s - 1)
                if s >= 2:
                    stage_out(s - 2)
            act.wait_ge(o_copied, 8 + 16)
            for b in range(2):
                act_fn(sq8[:, 4 * b:4 * b + 4, :], mix[:, 4 * b:4 * b + 4, :], ACT.Square).then_inc(sub_sq, 1)
            act.wait_ge(sub_var, 1)
            act_fn(rs8, rs8, ACT.Sqrt).then_inc(sub_std, 1)

            act.wait_ge(h_ready, 3)
            norm("b2", hT, X, X, mod2[:, 48:64])
            with act.Fori(0, FF // 4) as i:
                for p in range(4):
                    act.wait_ge(acc_full, i * U + (OUTS["up"] + 2 * p + 1))
                    act.wait_ge(conv_ready, i * 4 + (p + TWO - 1))
                    act_fn(gp[p % 2][:, 1:T + 1], ps[:, (OUTS["up"] + 2 * p) % BANKS, 0:T], ACT.Copy)\
                        .then_inc(g_row, 1)
                    act.wait_ge(conv_ready, i * 4 + (p + TWO + 1))
                    act_fn(gc[p % 2], gc[p % 2], ACT.Silu).then_inc(silu_done, 1)
            act.wait_ge(h_ready, 4)
            norm("f2", hT, X, None)

        @block.tensor
        def _(pe):
            mm = nc.tensor.matmul
            ones, ident = cst("ones"), cst("ident")

            def bank(o):
                pe.wait_ge(acc_free, o + 1)

            def norm_sum(name, sqd, n, cols=T):
                for k in range(n):
                    if k % 4 == 0:
                        pe.wait_ge(squared, before(name, "squares") + k // 4 + 1)
                    ins = mm(ps[:, 4, 0:cols], ones, sqd[:, k, :], start=(k == 0), stop=(k == n - 1))
                ins.then_inc(summed, 1)

            def blocks(to, slot, n, moving, at=0):
                for k in range(n):
                    ins = mm(to, ring[:, slot % RING, (at + k) * P:(at + k + 1) * P], moving(k),
                             start=(k == 0), stop=(k == n - 1))
                return ins

            def loop(name, turns, moving, out_name=None, cols=T, u_n=U):
                o0, t0 = OUTS[out_name or name], TILES[name]
                with pe.Fori(0, turns) as i:
                    for u in range(u_n):
                        pe.wait_ge(w_slot[u % RING], i * (16 * u_n // RING) + 16 * ((t0 + u) // RING + 1))
                        pe.wait_ge(acc_free, i * u_n + (o0 + u + 1))
                        blocks(ps[:, (o0 + u) % BANKS, 0:cols], u, KC, moving).then_inc(acc_full, 1)

            def one(tile, o, emit):
                pe.wait_ge(w_slot[tile % RING], 16 * (tile // RING + 1))
                bank(o)
                emit(tile % RING, o % BANKS)

            def tokens_first(slot, b, src, n, tbs, at=0):
                for tb in range(tbs):
                    for k in range(n):
                        ins = mm(ps[:, b, tb * P:(tb + 1) * P], src[:, k, tb * P:(tb + 1) * P],
                                 ring[:, slot, (at + k) * P:(at + k + 1) * P], start=(k == 0), stop=(k == n - 1))
                return ins

            pe.wait_ge(const_in, 48)
            norm_sum("a1", X, KC)
            pe.wait_ge(shifted, before("a1", "shifted") + KC)
            loop("qk", 24 // U, lambda k: X[:, k, :])
            pe.wait_ge(acc_free, BANKS + OUTS["v"])
            for n in range(HEADS):
                one(TILES["v"] + n, OUTS["v"] + n,
                    lambda s, b: tokens_first(s, b, X, KC, 2).then_inc(acc_full, 1))
                if n >= 2:
                    pe.wait_ge(roped, n - 1)
                mm(ps[:, 4 + n % 2, :], cst("perm1"), qk[:, 2 * n:2 * n + 2, :], start=True, stop=True)\
                    .then_inc(rotated, 1)

            def s1(u):
                hs, qb = u // 2, u % 2
                if u == 0:
                    pe.wait_ge(roped, 12)
                else:
                    pe.wait_ge(max_ready, u)
                nk = P * (qb + 1)
                for g in range(3):
                    h = g * SLOTS + hs
                    ins = mm(ps[:, 4 + g // 2, (g % 2) * T:(g % 2) * T + nk], qk[:, h, qb * P:(qb + 1) * P],
                             qk[:, HEADS + h, 0:nk], start=True, stop=True)
                ins.then_inc(s_ready, 1)

            def t1(u):
                pe.wait_ge(p_ready, u + 1)
                if u:
                    pe.wait_ge(pt_copied, u)
                    pe.wait_ge(o_copied, u)
                nb = u % 2 + 1
                for g in range(3):
                    for kb in range(nb):
                        n = g * nb + kb
                        ins = nc.tensor.transpose(ps[:, 6 + n // 4, (n % 4) * P:(n % 4 + 1) * P],
                                                  sc1[:, g, kb * P:(kb + 1) * P], ident)
                ins.then_inc(pt_ready, 1)

            def y1(u):
                hs, nb = u // 2, u % 2 + 1
                pe.wait_ge(pt_copied, u + 1)
                for g in range(3):
                    h = g * SLOTS + hs
                    for kb in range(nb):
                        n = g * nb + kb
                        ins = mm(ps[:, 7, 256:384], v1[:, kb, h * P:(h + 1) * P], pt1[:, n * P:(n + 1) * P],
                                 start=(n == 0), stop=(n == 3 * nb - 1))
                ins.then_inc(o_ready, 1)

            for k in range(36):
                o = OUTS["gate"] + k + (4 if k > MIX_AFTER else 0)
                one(TILES["gate"] + k, o,
                    lambda s, b: blocks(ps[:, b, 0:T], s, KC, lambda c: X[:, c, :]).then_inc(acc_full, 1))
                if k == MIX_AFTER:
                    pe.wait_ge(pooled, 1)
                    for g in range(4):
                        o = OUTS["gate"] + MIX_AFTER + 1 + g
                        bank(o)
                        mm(ps[:, o % BANKS, 0:T], mixw[:, g, :], pads[2][:, g, PAD:], start=True, stop=True)\
                            .then_inc(acc_full, 1)
                u = k // 4
                if u < 8:
                    if k % 4 == 0:
                        s1(u)
                    if k % 4 == 2:
                        t1(u)
                    if k % 4 == 3:
                        y1(u)
            pe.wait_ge(acc_free, BANKS + OUTS["branch"])
            pe.wait_ge(o_copied, 8)
            for t in range(8):
                src = attn if t % 2 == 0 else pool
                pe.wait_ge(w_slot[t % RING], 16 * ((TILES["branch"] + t) // RING + 1))
                for n in range(4):
                    o = OUTS["branch"] + 4 * t + n
                    bank(o)
                    blocks(ps[:, o % BANKS, 0:T], t, 4, lambda c: src[:, c, :], at=4 * n).then_inc(acc_full, 1)
            pe.wait_ge(merged, 4)
            loop("wo", 16 // U, lambda k: ga[:, k, :])
            norm_sum("b1", X, KC)
            pe.wait_ge(shifted, before("b1", "shifted") + KC)
            loop("wq", 16 // U, lambda k: X[:, k, :])
            pe.wait_ge(acc_free, BANKS + OUTS["key"])
            pe.wait_ge(keys_in, 16)
            for n in range(8):
                o, tb = OUTS["key"] + n, n // 4
                bank(o)
                for j in range(4):
                    c = 4 * (n % 4) + j
                    ins = mm(ps[:, o % BANKS, j * P:(j + 1) * P], pq[:, c, tb * P:(tb + 1) * P], keys[:, c, :],
                             start=True, stop=True)
                ins.then_inc(acc_full, 1)
            for tb in range(2):
                pe.wait_ge(ids_ready, tb + 1)
                if tb:
                    pe.wait_ge(ids_copied, tb)
                for j in range(3):
                    ins = nc.tensor.transpose(ps[:, 4, j * P:(j + 1) * P], ids[:, j, :], ident)
                ins.then_inc(ids_turned, 1)
            pe.wait_ge(ids_copied, 2)
            with pe.Fori(0, NBLK) as i:
                for j in range(2):
                    pe.wait_ge(oh_pool, i * 2 + (j + 1))
                    pe.wait_ge(g_copied, i * 2 + (j - 1 + TWO))
                    for q in range(8):
                        ins = mm(ps[:, 4 + 2 * j + q // 4, (q % 4) * P:(q % 4 + 1) * P], oh1[j][:, q, :],
                                 oh2[j][:, q, :], start=True, stop=True)
                    ins.then_inc(g_full, 1)
            with pe.Fori(0, NG) as i:
                for u in range(32):
                    pe.wait_ge(w_slot[u % RING], i * (16 * 32 // RING) + 16 * ((TILES["peer"] + u) // RING + 1))
                    pe.wait_ge(acc_free, i * 32 + (OUTS["peer"] + u + 1))
                    if u < 16:
                        blocks(ps[:, u % BANKS, 0:T], u, KC, lambda k: X[:, k, :]).then_inc(acc_full, 1)
                    else:
                        for k in range(16):
                            if u == 16:
                                pe.wait_ge(at_ready, i * 16 + (k + TWO + 1))
                            ins = mm(ps[:, u % BANKS, 0:T], ring[:, u % RING, k * P:(k + 1) * P], AT[:, k, :],
                                     start=(k == 0), stop=(k == 15))
                        ins.then_inc(acc_full, 1)

            norm_sum("f1", X, KC)
            pe.wait_ge(var_ready, NORM_AT["f1"] + 1)
            norm_sum("ctx", X2[:, :, 0:CTX], KC)
            pe.wait_ge(var_ready, NORM_AT["ctx"] + 1)
            norm_sum("a2", X2[:, :, CTX:], KC)
            pe.wait_ge(shifted, before("a2", "shifted") + KC)

            def loop_in2(name, skip, turn):
                with pe.Fori(0, 2) as i:
                    for u in range(4):
                        t, o = TILES["in2"] + skip + u, OUTS[name] + u
                        pe.wait_ge(w_slot[u % RING], i * 16 + 16 * (t // RING + 1))
                        pe.wait_ge(acc_free, i * 4 + (o + 1))
                        turn(u % RING, u % BANKS).then_inc(acc_full, 1)

            loop_in2("q2", 0, lambda s, b: blocks(ps[:, b, 0:T], s, KC, lambda k: X2[:, k, CTX:]))
            loop_in2("k2", 8, lambda s, b: blocks(ps[:, b, :], s, KC, lambda k: X2[:, k, :]))
            loop_in2("v2", 16, lambda s, b: tokens_first(s, b, X2, KC, 4))
            for n in range(6):
                one(TILES["in2"] + 24 + n, OUTS["c2"] + n,
                    (lambda s, b: blocks(ps[:, b, :], s, KC, lambda k: X2[:, k, :]).then_inc(acc_full, 1)) if n < 3
                    else (lambda s, b: blocks(ps[:, b, 0:T], s, KC, lambda k: X2[:, k, CTX:]).then_inc(acc_full, 1)))
            norm_sum("kv", kn[:, 0:2, :], 2, TA)
            pe.wait_ge(var_ready, NORM_AT["kv"] + 1)
            norm_sum("q", sq2, 3)
            pe.wait_ge(scaled, before("q", "scaled"))
            for t in range(2):
                tile = TILES["ukv"] + t
                pe.wait_ge(w_slot[tile % RING], 16 * (tile // RING + 1))
                for n in range(8):
                    o = OUTS["ukv"] + 8 * t + n
                    bank(o)
                    if t == 0:
                        ins = blocks(ps[:, o % BANKS, :], tile, 2, lambda k: ckv[:, k, :], at=2 * n)
                    else:
                        ins = tokens_first(tile % RING, o % BANKS, ckv, 2, 4, at=2 * n)
                    ins.then_inc(acc_full, 1)
            pe.wait_ge(scaled, before("q", "scaled") + 3)
            for t in range(4):
                tile = TILES["uq"] + t
                pe.wait_ge(w_slot[tile % RING], 16 * (tile // RING + 1))
                for n in range(4):
                    o = OUTS["uq"] + 4 * t + n
                    bank(o)
                    blocks(ps[:, o % BANKS, 0:T], tile, 3, lambda k: cq[:, k, :], at=3 * n).then_inc(acc_full, 1)
            pe.wait_ge(acc_free, BANKS + OUTS["wo2"])
            for n in range(13):
                if n >= 2:
                    pe.wait_ge(roped, 12 + n - 1)
                src, w = rope_step(n)
                mm(ps[:, 4 + n % 2, 0:w], cst("perm2"), src, start=True, stop=True).then_inc(rotated, 1)

            def s2(u):
                h, qb = (u // 2) % 8, u % 2
                if u == 0:
                    pe.wait_ge(roped, 12 + 13)
                if u >= 2:
                    pe.wait_ge(exp_ready, 8 + u - 1)
                cols = slice(qb * P, (qb + 1) * P)
                if u < 16:
                    for j in range(2):
                        rows = slice(64 * j, 64 * j + 64)
                        ins = mm(ps[:, 2 * (u % 2) + j, :], q2[rows, h, cols], k2[rows, h, :], start=True, stop=True)
                else:
                    mm(ps[:, 2 * (u % 2), :], qm[:, h, cols], kn[:, h, :], start=True, stop=False)
                    ins = mm(ps[:, 2 * (u % 2), :], qm[:, 8 + h, cols], kr, start=False, stop=True)
                ins.then_inc(s_ready, 1)

            def t2(u):
                pe.wait_ge(p_ready, 8 + u + 1)
                if u >= 2:
                    pe.wait_ge(pt_copied, 8 + u - 1)
                for kb in range(4):
                    ins = nc.tensor.transpose(ps[:, 4 + u % 2, kb * P:(kb + 1) * P],
                                              prob[u % 2][:, 0, kb * P:(kb + 1) * P], ident)
                ins.then_inc(pt_ready, 1)

            def o2(u):
                h = (u // 2) % 8
                pe.wait_ge(pt_copied, 8 + u + 1)
                if u >= 2:
                    pe.wait_ge(o_copied, 8 + u - 1)
                vv = v2 if u < 16 else vm
                for kb in range(4):
                    ins = mm(ps[:, 6 + u % 2, 0:P], vv[:, kb, h * P:(h + 1) * P], wt2[u % 2][:, kb * P:(kb + 1) * P],
                             start=(kb == 0), stop=(kb == 3))
                ins.then_inc(o_ready, 1)

            s2(0)
            for s in range(32 + 1):
                if s + 1 < 32:
                    s2(s + 1)
                if s < 32:
                    t2(s)
                if s >= 1:
                    o2(s - 1)
            for b in range(2):
                pe.wait_ge(sub_sq, b + 1)
                for j in range(2):
                    ins = mm(ps[:, 2 * b + j, :], ones, sq8[:, 4 * b + 2 * j:4 * b + 2 * j + 2, :],
                             start=True, stop=True)
            ins.then_inc(sub_sum, 1)
            pe.wait_ge(mixed, 1)
            pe.wait_ge(o_copied, 8 + 32)
            loop("wo2", 16 // U, lambda k: mix[:, k, :])
            norm_sum("b2", X, KC)
            pe.wait_ge(shifted, before("b2", "shifted") + KC)
            with pe.Fori(0, FF // 4) as i:
                for u in range(U):
                    o0, t0 = OUTS["up"], TILES["up"]
                    pe.wait_ge(w_slot[u % RING], i * (16 * U // RING) + 16 * ((t0 + u) // RING + 1))
                    pe.wait_ge(acc_free, i * U + (o0 + 2 * (u // 2) + 2))
                    blocks(ps[:, (o0 + u) % BANKS, 0:T], u, KC, lambda k: X[:, k, :]).then_inc(acc_full, 1)
            pe.wait_ge(acc_free, BANKS + OUTS["down"])
            with pe.Fori(0, 4) as i:
                for n in range(4):
                    o0, t0 = OUTS["down"], TILES["down"]
                    pe.wait_ge(acc_free, i * 4 + (o0 + n + 1))
                    for q in range(4):
                        u = 4 * n + q
                        pe.wait_ge(w_slot[u % RING], i * (16 * 16 // RING) + 16 * ((t0 + u) // RING + 1))
                        for k in range(11):
                            kk = 11 * q + k
                            ins = mm(ps[:, (o0 + n) % BANKS, 0:T], ring[:, u % RING, k * P:(k + 1) * P],
                                     hid[:, kk, :], start=(kk == 0), stop=(kk == FF - 1))
                        if q < 3:
                            ins.then_inc(quarter_used, 1)
                    ins.then_inc(acc_full, 1)
            norm_sum("f2", X, KC)

        @block.vector
        def _(dve):
            ch = Chain(dve, dve_done)
            vv = nc.vector

            def ada_row(slot, wait, c_row, to):
                dve.wait_ge(a_slot[slot], wait)
                vv.tensor_tensor_reduce(ada[:, slot, :], ada[:, slot, :], c_row, 1.0, 0.0, ALU.mult, ALU.add,
                                        to).then_inc(a_free, 1)

            def ada_static(tile, to):
                ada_row(tile % 2, 16 * (tile // 2 + 1), cb[:, 0, :], to)

            def norm(name, src, dst, gain, shift_cols=None, cols=T):
                i = NORM_AT[name]
                _, n, _, width, _ = NORMS[i]
                dve.wait_ge(summed, i + 1)
                vv.tensor_scalar(rs[:, 0:cols], ps[:, 4, 0:cols], 1.0 / width, EPS, ALU.mult, ALU.add)\
                    .then_inc(var_ready, 1)
                dve.wait_ge(std_ready, i + 1)
                ch.link(vv.reciprocal(rs[:, 0:cols], rs[:, 0:cols]))
                for k in range(n):
                    vv.scalar_tensor_tensor(dst[:, k, :], src[:, k, :], gain[:, k:k + 1], rs[:, 0:cols],
                                            ALU.mult, ALU.mult).then_inc(scaled, 1)
                dve.wait_ge(scaled, before(name, "scaled") + n)

            def gain_of(scale, g):
                ch.link(vv.scalar_tensor_tensor(coef[:], scale, 1.0, g, ALU.add, ALU.mult))

            dve.sem_inc(acc_free, BANKS)
            dve.sem_inc(a_free, TWO)
            dve.sem_inc(at_ready, TWO)
            dve.sem_inc(g_copied, TWO)
            dve.sem_inc(g_full, TWO)
            for j in range(2):
                dve.sem_inc(g_stored[j], 16)
            for j in range(3):
                ins = vv.memset(pads[j], 0.0)
            ins.then_inc(zeroed, 1)

            dve.wait_ge(c_silu, 1)
            for t in range(32):
                ada_static(t, mod1[:, t:t + 1])
            dve.wait_ge(a_free, 2 + 32)
            dve.wait_ge(const_in, 48)
            ch.link(vv.tensor_tensor(mod1[:, 0:32], mod1[:, 0:32], vc("ada_b")[:, 0:32], ALU.add))
            gain_of(mod1[:, 16:32], vc("norm1_g"))
            norm("a1", hT, X, coef)

            with dve.Fori(0, 3) as i:
                ch.enter(i, 1)
                for u in range(8):
                    ada_row(u % 2, i * 64 + 16 * ((32 + u) // 2 + 1), cb[:, 0, :], modt[:, u:u + 1])
                dve.wait_ge(a_free, i * 8 + (2 + 32 + 8))
                ch.link(vv.tensor_copy(mod1[:, bass.ds(i * 8 + 32, 8)], modt[:, 0:8]))
            ch.leave(3)

            def rope(step, rot_n, bankn, chunk, w, a, b, cos, sin):
                dve.wait_ge(rotated, rot_n + 1)
                ch.tick(vv.tensor_tensor(a, ps[:, bankn, 0:w].rearrange("p (a b) -> p a b", b=T), sin, ALU.mult))
                ch.link(vv.tensor_tensor(b, chunk, cos, ALU.mult))
                vv.tensor_tensor(chunk, a, b, ALU.add).then_inc(roped, 1)
                dve.wait_ge(roped, rot_n + 1)

            def both(name, n):
                return cst(name).unsqueeze(1).broadcast_to([P, n, T])

            at = 56
            for n in range(HEADS):
                ada_static(at, mod1[:, at:at + 1])
                at += 1
                rope(n, n, 4 + n % 2, qk[:, 2 * n:2 * n + 2, :], 512, rope_a, rope_b, both("cos1", 2), both("sin1", 2))

            def pool_rows():
                dve.wait_ge(acc_free, BANKS + OUTS["gate"] + 4)
                w = 1
                src = pads[0]
                for level in range(4):
                    to = pads[1 + level % 2]
                    ch.link(vv.tensor_tensor(to[:, level:4, PAD:], src[:, level:4, PAD:],
                                             src[:, level:4, PAD - w:PAD + T - w], ALU.add))
                    src, w = to, 2 * w
                rc = cst("rcount").rearrange("p (a b) -> p a b", a=4)
                for g in range(4):
                    s = pads[1 + g % 2]
                    ch.tick(vv.tensor_tensor(s[:, g, PAD:], s[:, g, PAD:], rc[:, g, :], ALU.mult))
                ch.sync()
                for g in range(4):
                    s = pads[1 + g % 2]
                    ins = vv.tensor_tensor(pads[2][:, g, PAD:], s[:, g, PAD:], pads[0][:, g, PAD:], ALU.subtract)
                ins.then_inc(pooled, 1)

            for u in range(8):
                qb = u % 2
                nk = P * (qb + 1)
                s = sc1[:, :, 0:nk]
                mask = cst(f"mask{qb}").rearrange("p (a b) -> p a b", a=3)
                dve.wait_ge(s_ready, u + 1)
                if u:
                    dve.wait_ge(pt_ready, u)
                scores = ps[:, 4:6, :].rearrange("p a (b c) -> p (a b) c", c=T)[:, 0:3, 0:nk]
                ch.link(vv.scalar_tensor_tensor(s, scores, SM1, mask, ALU.mult, ALU.add))
                ch.link(vv.tensor_reduce(small[:, 2:3], s, mybir.AxisListType.XY, ALU.max))
                vv.tensor_scalar(small[:, 0:1], small[:, 2:3], -1.0, None, ALU.mult).then_inc(max_ready, 1)
                if at < 96:
                    ada_static(at, mod1[:, at:at + 1])
                    at += 1
                if u == 2:
                    pool_rows()
                dve.wait_ge(exp_ready, u + 1)
                ch.link(vv.reciprocal(small[:, 3:4], small[:, 1:2]))
                vv.tensor_scalar(s, s, small[:, 3:4], None, ALU.mult).then_inc(p_ready, 1)
                for _ in range(3):
                    if at < 96:
                        ada_static(at, mod1[:, at:at + 1])
                        at += 1
            assert at == 96, at
            dve.wait_ge(a_free, 2 + 96)
            ch.link(vv.tensor_tensor(mod1[:, 32:96], mod1[:, 32:96], vc("ada_b")[:, 32:96], ALU.add))

            for t in range(8):
                g = ga if t % 2 == 0 else gb
                for n in range(4):
                    o, c = OUTS["branch"] + 4 * t + n, 4 * (t // 2) + n
                    dve.wait_ge(acc_full, o + 1)
                    vv.tensor_tensor(g[:, c, :], g[:, c, :], ps[:, o % BANKS, 0:T], ALU.mult).then_inc(acc_free, 1)
                if t % 2:
                    c = 4 * (t // 2)
                    dve.wait_ge(acc_free, BANKS + OUTS["branch"] + 4 * (t + 1))
                    vv.tensor_tensor(ga[:, c:c + 4, :], ga[:, c:c + 4, :], gb[:, c:c + 4, :], ALU.add)\
                        .then_inc(merged, 1)

            def residual(name, turns, gate, gate_at):
                with dve.Fori(0, turns) as i:
                    for u in range(U):
                        dve.wait_ge(acc_full, i * U + (OUTS[name] + u + 1))
                        c = i * U + u
                        vv.scalar_tensor_tensor(hT[:, c, :], ps[:, (OUTS[name] + u) % BANKS, 0:T],
                                                gate[:, bass.ds(i * U + (gate_at + u), 1)], hT[:, c, :],
                                                ALU.mult, ALU.add).then_inc(acc_free, 1)

            residual("wo", 2, mod1, 32)
            dve.wait_ge(acc_free, BANKS + OUTS["wq"])
            dve.sem_inc(h_ready, 1)
            gain_of(mod1[:, 64:80], vc("norm2_g"))
            norm("b1", hT, X, coef)

            def best(to_v, to_i, rows, n):
                for r in range(n):
                    ins = vv.max(to_v[:, r, 0:8], rows[:, r, :])
                ch.link(ins)
                for r in range(n):
                    ins = vv.max_index(to_i[:, r, 0:8], to_v[:, r, 0:8], rows[:, r, :])
                ch.link(ins)
                for r in range(n):
                    ins = vv.match_replace(rows[:, r, :], to_v[:, r, 0:8], rows[:, r, :], NEG)
                ch.link(ins)
                for r in range(n):
                    ins = vv.max(to_v[:, r, 8:16], rows[:, r, :])
                ch.link(ins)
                for r in range(n):
                    ins = vv.max_index(to_i[:, r, 8:16], to_v[:, r, 8:16], rows[:, r, :])
                ch.link(ins)

            iota = cst("iota")
            for tb in range(2):
                dve.wait_ge(acc_free, BANKS + OUTS["key"] + 4 * (tb + 1))
                best(topv, topi, score[tb], KC)
                ch.tick(vv.tensor_copy(topf, topi))
                pairs = topv.rearrange("p (h s) k -> p h s k", s=2)
                c4 = cand.rearrange("p h (i j) -> p h i j", i=TOPK)
                ch.link(vv.tensor_tensor(c4, pairs[:, :, 0, :].unsqueeze(3).broadcast_to([P, EH, TOPK, TOPK]),
                                         pairs[:, :, 1, :].unsqueeze(2).broadcast_to([P, EH, TOPK, TOPK]), ALU.add))
                best(cv, ci, cand, EH)
                ch.tick(vv.tensor_scalar(ca, ci, 4, None, ALU.logical_shift_right))
                ch.link(vv.tensor_scalar(cbi, ci, 15, None, ALU.bitwise_and))
                ch.tick(vv.tensor_copy(caf, ca))
                ch.tick(vv.tensor_copy(cbf, cbi))
                ch.link(vv.tensor_tensor(gsum, cv[:, :, 0], cv[:, :, 0], ALU.max))
                if tb:
                    dve.wait_ge(ids_turned, tb)
                vv.tensor_tensor(cv, cv, gsum.unsqueeze(2).broadcast_to([P, EH, TOPK]), ALU.subtract)\
                    .then_inc(cand_ready, 1)
                ff = topf.rearrange("p (h s) k -> p h s k", s=2)
                for j, pos in enumerate((caf, cbf)):
                    ch.link(vv.tensor_tensor(eq, pos.unsqueeze(3).broadcast_to([P, EH, TOPK, TOPK]),
                                             iota[:, 0:TOPK].unsqueeze(1).unsqueeze(1).broadcast_to([P, EH, TOPK, TOPK]),
                                             ALU.is_equal))
                    ch.link(vv.tensor_tensor(eq, eq, ff[:, :, j, :].unsqueeze(2).broadcast_to([P, EH, TOPK, TOPK]),
                                             ALU.mult))
                    ch.link(vv.tensor_reduce(ids[:, j, :], eq.rearrange("p h k j -> p (h k) j"), AX, ALU.add))
                dve.wait_ge(gate_exp, tb + 1)
                gt = ids[:, 2, :].rearrange("p (h k) -> p h k", h=EH)
                ch.link(vv.tensor_reduce(gsum, gt, AX, ALU.add))
                ch.link(vv.reciprocal(gsum, gsum))
                vv.tensor_tensor(gt, gt, gsum.unsqueeze(2).broadcast_to([P, EH, TOPK]), ALU.mult)\
                    .then_inc(ids_ready, 1)
                dve.wait_ge(ids_ready, tb + 1)

            dve.wait_ge(ids_copied, 2)
            with dve.Fori(0, NBLK) as i:
                for j in range(2):
                    tok = bass.ds(i * 16 + 8 * j, 8)
                    dve.wait_ge(g_full, i * 2 + (j + TWO - 1))
                    many = iota.unsqueeze(1).broadcast_to([P, 8, P])
                    vv.tensor_tensor(oh1[j], many, idT[:, 0, tok].unsqueeze(2).broadcast_to([P, 8, P]), ALU.is_equal)
                    vv.tensor_tensor(oh2[j], many, idT[:, 1, tok].unsqueeze(2).broadcast_to([P, 8, P]), ALU.is_equal)\
                        .then_inc(oh_dve, 1)

            dve.wait_ge(c_silu, 3)
            with dve.Fori(0, NG) as i:
                ch.enter(i, 7)
                dve.wait_ge(g_in, i * 16 + 16)
                for u in range(16):
                    if u < 12:
                        slot = u % 2
                        dve.wait_ge(a_slot[slot], i * 96 + 16 * ((96 + u) // 2 + 1))
                        if u < 4:
                            ch.link(vv.tensor_tensor_reduce(junk, ada[:, slot, :], cb[:, 1, :], 1.0, 0.0, ALU.mult,
                                                            ALU.add, modt[:, 12 + u:13 + u]))
                        vv.tensor_tensor_reduce(ada[:, slot, :], ada[:, slot, :], cb[:, 0, :], 1.0, 0.0, ALU.mult,
                                                ALU.add, modt[:, u:u + 1]).then_inc(a_free, 1)
                    dve.wait_ge(gelu_done, i * 16 + (u + 1))
                    vv.tensor_tensor(AT[:, u, :].rearrange("p (a b) -> p a b", a=NBLK),
                                     gl[:, u % 2, :].rearrange("p (a b) -> p a b", a=NBLK),
                                     G[:, :, u * BLK:(u + 1) * BLK], ALU.mult).then_inc(at_ready, 1)
                    dve.wait_ge(at_ready, i * 16 + (u + TWO + 1))
                    dve.sem_inc(acc_free, 1)
                dve.wait_ge(a_free, i * 12 + (2 + 96 + 12))
                ch.tick(vv.tensor_copy(mod2[:, bass.ds(i * 4, 4)], modt[:, 0:4]))
                ch.tick(vv.tensor_copy(mod2[:, bass.ds(i * 8 + 32, 8)], modt[:, 4:12]))
                ch.link(vv.tensor_copy(modc[:, bass.ds(i * 4, 4)], modt[:, 12:16]))
                for u in range(16):
                    dve.wait_ge(acc_full, i * 32 + (OUTS["peer"] + 16 + u + 1))
                    vv.scalar_tensor_tensor(hT[:, u, :], ps[:, u % BANKS, 0:T], mod1[:, 80 + u:81 + u], hT[:, u, :],
                                            ALU.mult, ALU.add).then_inc(acc_free, 1)
                dve.wait_ge(acc_free, i * 32 + (BANKS + OUTS["peer"] + 32))
            ch.leave(NG)
            ch.link(vv.tensor_tensor(mod2[:], mod2[:], vc("b_ada_2"), ALU.add))
            ch.link(vv.tensor_tensor(modc[:], modc[:], vc("b_ada_2")[:, 0:32], ALU.add))
            dve.sem_inc(h_ready, 1)
            norm("f1", hT, hT, vc("final_g"))
            gain_of(modc[:, 16:32], vc("norm1_w_2"))
            norm("ctx", ctxT, X2[:, :, 0:CTX], coef)
            gain_of(mod2[:, 16:32], vc("norm1_w_2"))
            norm("a2", hT, X2[:, :, CTX:], coef)

            norm("kv", ckv, ckv, vc("kv_norm_w_2"), cols=TA)
            norm("q", cq, cq, vc("q_norm_w_2"))
            for j in range(2):
                ch.tick(vv.tensor_tensor_reduce(vc(f"lambda_q{j + 1}_2"), vc(f"lambda_q{j + 1}_2"),
                                                vc(f"lambda_k{j + 1}_2"), 1.0, 0.0, ALU.mult, ALU.add,
                                                small[:, 8 + j:9 + j]))
            ch.sync()
            dve.sem_inc(max_ready, 1)
            dve.wait_ge(lam_exp, 1)
            ch.link(vv.tensor_tensor(small[:, 10:11], small[:, 9:10], small[:, 8:9], ALU.subtract))
            ch.link(vv.tensor_scalar(small[:, 10:11], small[:, 10:11], -LAMBDA_INIT, None, ALU.add))
            dve.wait_ge(acc_free, BANKS + OUTS["wo2"])
            for n in range(13):
                src, w = rope_step(n)
                m = w // T
                rope(n, 12 + n, 4 + n % 2, src, w, rope2[0][:, 0:m, :], rope2[1][:, 0:m, :],
                     both("cos2", m), both("sin2", m))

            def max2(u):
                two = 2 if u < 16 else 1
                b = 2 * (u % 2)
                dve.wait_ge(s_ready, 8 + u + 1)
                if u >= 2:
                    dve.wait_ge(p_ready, 8 + u - 1)
                m = small[:, 4 * (u % 2):4 * (u % 2) + two]
                ch.link(vv.tensor_reduce(m, ps[:, b:b + two, :], AX, ALU.max))
                vv.tensor_scalar(m, m, -(SM_DA if two == 2 else SM_MLA), None, ALU.mult).then_inc(max_ready, 1)

            def prob2(u):
                two = 2 if u < 16 else 1
                s0 = 4 * (u % 2) + 2
                dve.wait_ge(exp_ready, 8 + u + 1)
                ch.link(vv.reciprocal(small[:, s0:s0 + two], small[:, s0:s0 + two]))
                w = prob[u % 2]
                if two == 2:
                    ch.tick(vv.tensor_scalar(w[:, 1, :], w[:, 1, :], small[:, s0 + 1:s0 + 2], small[:, 10:11],
                                             ALU.mult, ALU.mult))
                    ch.sync()
                    vv.scalar_tensor_tensor(w[:, 0, :], w[:, 0, :], small[:, s0:s0 + 1], w[:, 1, :],
                                            ALU.mult, ALU.add).then_inc(p_ready, 1)
                else:
                    vv.tensor_scalar(w[:, 0, :], w[:, 0, :], small[:, s0:s0 + 1], None, ALU.mult)\
                        .then_inc(p_ready, 1)

            max2(0)
            for s in range(32):
                if s + 1 < 32:
                    max2(s + 1)
                prob2(s)
            dve.wait_ge(sub_sum, 1)
            vv.tensor_scalar(rs8.rearrange("p a b -> p (a b)"), ps[:, 0:4, :].rearrange("p a b -> p (a b)"),
                             1.0 / P, EPS, ALU.mult, ALU.add).then_inc(sub_var, 1)
            dve.wait_ge(sub_std, 1)
            ch.link(vv.reciprocal(rs8, rs8))
            ch.link(vv.tensor_scalar(small[:, 11:12], vc("subln_w_2"), 1.0 - LAMBDA_INIT, None, ALU.mult))
            vv.scalar_tensor_tensor(mix[:, 0:H2, :], mix[:, 0:H2, :], small[:, 11:12], rs8, ALU.mult, ALU.mult)\
                .then_inc(mixed, 1)
            residual("wo2", 2, mod2, 32)
            dve.wait_ge(acc_free, BANKS + OUTS["up"])
            dve.sem_inc(h_ready, 1)
            gain_of(mod2[:, 64:80], vc("norm2_w_2"))
            norm("b2", hT, X, coef)

            for j in range(2):
                ch.tick(vv.memset(gp[j], 0.0))
            ch.sync()
            dve.sem_inc(conv_ready, TWO)
            cw = vc("conv_w_2").rearrange("p (j f) -> p j f", j=3)
            with dve.Fori(0, FF // 4) as i:
                ch.enter(i, 8)
                for p in range(4):
                    f = bass.ds(i * 4 + p, 1)
                    g, c = gp[p % 2], gc[p % 2]
                    dve.wait_ge(g_row, i * 4 + (p + 1))
                    dve.wait_ge(acc_free, i * U + (OUTS["up"] + 2 * p + 2))
                    ch.link(vv.tensor_scalar(c, g[:, 1:T + 1], cw[:, 1, f], vc("conv_b_2")[:, f], ALU.mult, ALU.add))
                    ch.link(vv.scalar_tensor_tensor(c, g[:, 0:T], cw[:, 0, f], c, ALU.mult, ALU.add))
                    vv.scalar_tensor_tensor(c, g[:, 2:T + 2], cw[:, 2, f], c, ALU.mult, ALU.add)\
                        .then_inc(conv_ready, 1)
                    dve.wait_ge(silu_done, i * 4 + (p + 1))
                    o = OUTS["up"] + 2 * p + 1
                    dve.wait_ge(acc_full, i * U + (o + 1))
                    vv.tensor_tensor(hid[:, i * 4 + p, :], c, ps[:, o % BANKS, 0:T], ALU.mult)\
                        .then_inc(acc_free, 2)
            ch.leave(FF // 4)
            with dve.Fori(0, 4) as i:
                for u in range(4):
                    o = OUTS["down"] + u
                    dve.wait_ge(acc_full, i * 4 + (o + 1))
                    c = i * 4 + u
                    vv.scalar_tensor_tensor(hT[:, c, :], ps[:, o % BANKS, 0:T], mod2[:, bass.ds(i * 4 + 80 + u, 1)],
                                            hT[:, c, :], ALU.mult, ALU.add).then_inc(acc_free, 1)
            dve.wait_ge(acc_free, BANKS + OUTS["end"])
            dve.sem_inc(h_ready, 1)
            norm("f2", hT, hT, vc("final_w_2"))


def tiled(w):
    k, n = w.shape
    return w.reshape(k // P, P, n // P, P).transpose(2, 1, 0, 3).reshape(n // P, P, k)


def chunks(x):
    n, f = x.shape
    return x.reshape(n, f // P, P).transpose(2, 1, 0)


def columns(v):
    return v.reshape(-1, P).T


def constants():
    c = np.zeros((P, N_CONST), np.float32)

    def put(name, v):
        c[:, CONST[name][0]:CONST[name][1]] = v.reshape(P, -1)

    p = np.arange(P)
    for qb, n in ((0, P), (1, T)):
        dist = (qb * P + p)[:, None] - np.arange(n)[None, :]
        ok = np.stack([(dist >= 0) & (dist % dil == 0) & (dist // dil <= window // dil)
                       for window, dil in GROUPS], axis=1)
        put(f"mask{qb}", np.where(ok, 0.0, MASKED))
    inv = np.power(np.float32(10000.0), -np.arange(64, dtype=np.float32) / np.float32(64)).astype(np.float32)
    ang = (np.arange(T, dtype=np.float32)[None, :] * inv[p % 64][:, None]).astype(np.float32).astype(np.float64)
    put("cos1", np.cos(ang))
    put("sin1", np.sin(ang))
    perm = np.zeros((P, P))
    perm[(p + 64) % P, p] = np.where(p < 64, -1.0, 1.0)
    put("perm1", perm)
    put("ident", np.eye(P))
    put("ones", np.ones((P, P)))
    inv = np.power(np.float32(10000.0), -np.arange(16, dtype=np.float32) / np.float32(16)).astype(np.float32)
    t = np.arange(T)
    pos = np.where((p % 64 < 32)[:, None], (t // 64)[None, :], (t % 64)[None, :]).astype(np.float32)
    ang = (pos * inv[p % 16][:, None]).astype(np.float32).astype(np.float64)
    put("cos2", np.cos(ang))
    put("sin2", np.sin(ang))
    perm = np.zeros((P, P))
    low = p % 32 < 16
    perm[np.where(low, p + 16, p - 16), p] = np.where(low, -1.0, 1.0)
    put("perm2", perm)
    put("iota", np.broadcast_to(np.arange(P), (P, P)))
    count = np.stack([1.0 / np.minimum(t + 1, w) for w in POOLS])
    put("rcount", np.broadcast_to(count, (P, 4, T)).copy())
    return c


def kernel(**inputs):
    import concourse.bacc as bacc
    from concourse.bass_utils import run_bass_kernel_spmd

    a = {k: np.asarray(v) for k, v in inputs.items()}

    def spread(v):
        return np.broadcast_to(v.reshape(1, -1), (P, v.size))

    vectors = []
    for name, (lo, hi) in VEC.items():
        if name.startswith("lambda"):
            vectors.append(spread(a[name]))
        else:
            vectors.append(columns(a[name].reshape(-1)))

    rows1 = a["ada_w"][0].T.reshape(96, P, D)
    rows2 = a["w_ada_2"][0].T.reshape(96, P, D)
    order = [j for g in range(NG) for j in (*range(4 * g, 4 * g + 4), *range(32 + 8 * g, 40 + 8 * g))]

    def wide(w, n):
        t = tiled(w)
        return t.reshape(t.shape[0] // n, n, P, t.shape[2]).transpose(0, 2, 1, 3).reshape(-1, P, n * t.shape[2])

    wa, wp = wide(a["w_attn_branch"][0], 4), wide(a["w_pool_branch"][0], 4)
    w2 = a["w_in_2"][0]
    zeros = np.zeros((D, 64), np.float32)
    w2 = np.concatenate([w2[:, :3072], w2[:, 3456:3712], w2[:, 3712:], zeros, w2[:, 3072:3456]], axis=1)
    uq = a["w_uq_2"][0].reshape(384, H2, 192)
    uq_rope = np.concatenate([uq[:, :, P:], np.zeros((384, H2, 64), np.float32)], axis=2)
    uq = np.concatenate([uq[:, :, :P].reshape(384, -1), uq_rope.reshape(384, -1)], axis=1)
    ukv = a["w_ukv_2"][0].reshape(256, H2, 2, P).transpose(0, 2, 1, 3).reshape(256, 2 * D // 2)
    up = a["w_up_2"][0].reshape(D, 2, FF, P).transpose(0, 2, 1, 3).reshape(D, 2 * FF * P)
    down = tiled(a["w_down_2"][0]).reshape(KC, P, 4, 11 * P).transpose(0, 2, 1, 3).reshape(4 * KC, P, 11 * P)
    arrays = {
        "x": chunks(a["x"][0]),
        "ctx": chunks(a["ctx_2"][0]),
        "c": spread(a["c"]),
        "c_2": spread(a["c_2"]),
        "c_ctx_2": spread(a["c_ctx_2"]),
        "const": constants(),
        "vec": np.concatenate(vectors, axis=1),
        "pool_mix": a["pool_mix"][0].transpose(1, 0, 2),
        "ada": np.concatenate([rows1, rows2[order]], axis=0),
        "w_in": tiled(a["w_in"][0]),
        "w_branch": np.stack([wa, wp], axis=1).reshape(8, P, D),
        "w_out": tiled(a["w_out"][0]),
        "peer_wq": tiled(a["peer_wq"][0]),
        "keys": a["peer_keys"][0].transpose(3, 0, 1, 2).reshape(P, KC, NKEY),
        "peer_down": a["peer_down"][0].reshape(NKEY, NKEY, KC, P).transpose(1, 3, 2, 0).reshape(NKEY, P, D),
        "peer_up": a["peer_up"][0].reshape(NKEY, NG, 16, KC, P).transpose(1, 3, 0, 2, 4).reshape(NKEY, P, D),
        "w_in_2": tiled(w2),
        "w_ukv_2": wide(ukv, 8),
        "w_uq_2": wide(uq, 4),
        "w_o_2": tiled(a["w_o_2"][0]),
        "w_up_2": tiled(up),
        "w_down_2": down,
    }
    arrays = {k: np.ascontiguousarray(v) for k, v in arrays.items()}
    nc = bacc.Bacc("TRN2", target_bir_lowering=False, num_devices=1)
    A = {k: nc.dram_tensor(f"in_{k}", v.shape, F32, kind="ExternalInput").ap() for k, v in arrays.items()}
    out = nc.dram_tensor("out", (P, KC, T), F32, kind="ExternalOutput").ap()
    build_program(nc, A, out)
    r = run_bass_kernel_spmd(nc, [{f"in_{k}": v for k, v in arrays.items()}], core_ids=[0])
    return r.results[0]["out"].transpose(2, 1, 0).reshape(1, T, D)
```

```python
from contextlib import ExitStack

import numpy as np
import concourse.bass as bass
from concourse import mybir

ALU = mybir.AluOpType
ACT = mybir.ActivationFunctionType
AX = mybir.AxisListType.X
F32 = mybir.dt.float32
F32R = mybir.dt.float32r
U32 = mybir.dt.uint32

P = 128
T = 256
D = 2048
KC = D // P
EPS = 1e-6
NEG = -3.0e38
MASKED = -1.0e30

HEADS = 12
SLOTS = 4
GROUPS = ((128, 1), (512, 4), (2048, 16))
SM1 = 128 ** -0.5
POOLS = (2, 4, 8, 16)
PAD = 16
EH = 8
TOPK = 16
NKEY = 128
NG = 8
BLK = 16
NBLK = T // BLK

CTX = 256
TA = CTX + T
H2 = 8
SM_DA = 64 ** -0.5
SM_MLA = 192 ** -0.5
LAMBDA_INIT = 0.8 - 0.6
FF = 5632 // P

RING = 4
BANKS = 4
U = 8
PIECES = 4
PB = 4
TWO = 2

TILES = {}
_t = 0
for _name, _n in (("qk", 24), ("v", 12), ("gate", 36), ("branch", 8), ("wo", 16), ("wq", 16),
                  ("peer", 256), ("in2", 30), ("ukv", 2), ("uq", 4), ("wo2", 16), ("up", 88), ("down", 64)):
    TILES[_name] = _t
    _t += _n

OUTS = {}
_t = 0
for _name, _n in (("qk", 24), ("v", 12), ("gate", 40), ("branch", 32), ("wo", 16), ("wq", 16), ("key", 8),
                  ("peer", 256), ("q2", 8), ("k2", 8), ("v2", 8), ("c2", 6), ("ukv", 16), ("uq", 16),
                  ("wo2", 16), ("up", 88), ("down", 16), ("end", 0)):
    OUTS[_name] = _t
    _t += _n
MIX_AFTER = 35

SPLIT = {"peer": 0, "up": 256 * PIECES, "down": (256 + 88) * PIECES}
USED = {"peer": 0, "up": 256 * (PIECES - 1), "down": (256 + 88) * (PIECES - 1)}

CONST = {}
_t = 0
for _name, _n in (("mask0", 3 * P), ("mask1", 3 * T), ("cos1", T), ("sin1", T), ("perm1", P), ("ident", P),
                  ("ones", P), ("cos2", T), ("sin2", T), ("perm2", P), ("iota", P), ("rcount", 4 * T)):
    CONST[_name] = (_t, _t + _n)
    _t += _n
N_CONST = _t
VEC = {}
_t = 0
for _name, _n in (("ada_b", 96), ("norm1_g", 16), ("norm2_g", 16), ("final_g", 16), ("pool_scale", 4),
                  ("b_ada_2", 96), ("norm1_w_2", 16), ("q_norm_w_2", 3), ("kv_norm_w_2", 2), ("subln_w_2", 1),
                  ("norm2_w_2", 16), ("final_w_2", 16), ("conv_w_2", 3 * FF), ("conv_b_2", FF),
                  ("lambda_q1_2", 64), ("lambda_k1_2", 64), ("lambda_q2_2", 64), ("lambda_k2_2", 64)):
    VEC[_name] = (_t, _t + _n)
    _t += _n
N_VEC = _t

NORMS = (("a1", KC, T, D, True), ("b1", KC, T, D, True), ("f1", KC, T, D, False), ("ctx", KC, T, D, True),
         ("a2", KC, T, D, True), ("kv", 2, TA, 2 * P, False), ("q", 3, T, 3 * P, False),
         ("b2", KC, T, D, True), ("f2", KC, T, D, False))
NORM_AT = {n[0]: i for i, n in enumerate(NORMS)}


def before(name, what):
    ahead = NORMS[:NORM_AT[name]]
    if what == "squares":
        return sum(max(1, n[1] // 4) for n in ahead)
    if what == "scaled":
        return sum(n[1] for n in ahead)
    return sum(n[1] for n in ahead if n[4])


class Chain:

    def __init__(self, eng, sem):
        self.eng, self.sem, self.n, self.turn = eng, sem, 0, None

    def tick(self, ins):
        ins.then_inc(self.sem, 1)
        self.n += 1

    def sync(self):
        if self.turn is None:
            self.eng.wait_ge(self.sem, self.n)
        else:
            base, i, per = self.turn
            self.eng.wait_ge(self.sem, i * per + (base + self.n))

    def link(self, ins):
        self.tick(ins)
        self.sync()

    def enter(self, i, per):
        self.turn = (self.n, i, per)
        self.n = 0

    def leave(self, turns):
        base, _, per = self.turn
        assert self.n == per, (self.n, per)
        self.n, self.turn = base + per * turns, None


def build_program(nc, A, out):
    with ExitStack() as ctx:
        def sb(name, shape, dt=F32):
            return ctx.enter_context(nc.sbuf_tensor(name, shape, dt))

        def sem(name):
            return ctx.enter_context(nc.semaphore(name))

        hT = sb("hT", [P, KC, T])
        ring = sb("ring", [P, RING, D])
        const = sb("const", [P, N_CONST])
        vec = sb("vec", [P, N_VEC])
        mod1 = sb("mod1", [P, 96])
        mod2 = sb("mod2", [P, 96])
        modc = sb("modc", [P, 32])
        modt = sb("modt", [P, 16])
        coef = sb("coef", [P, KC])
        rs = sb("rs", [P, TA])
        small = sb("small", [P, 16])
        arena = sb("arena", [P, 105 * 256])
        ada = sb("ada", [P, 2, D])
        cb = sb("cb", [P, 2, D])
        arena_at = nc.lookup_mloc("arena").addr
        assert nc.lookup_mloc("ada").addr == arena_at + 105 * 1024
        assert nc.lookup_mloc("cb").addr == arena_at + 121 * 1024

        def split_room(name, kb, *shape):
            return nc.alloc_sbuf_tensor_at(name, [P, *shape], F32R, offset=arena_at + int(kb * 1024))[:]
        ps = ctx.enter_context(nc.psum_tensor("ps", [P, 8, 512], F32))
        gates_dram = nc.dram_tensor("gates_scratch", (NG, P, NBLK, 16 * BLK), F32, kind="Internal").ap()

        def room(kb, *shape, dt=F32):
            n = int(np.prod(shape))
            at = int(kb * 256)
            assert at + n <= 105 * 256, (kb, shape)
            v = arena[:, at:at + n]
            if dt is not F32:
                v = v.bitcast(dt)
            if len(shape) == 2:
                return v.rearrange("p (a b) -> p a b", a=shape[0])
            if len(shape) == 3:
                return v.rearrange("p (a b c) -> p a b c", a=shape[0], b=shape[1])
            return v

        def cst(name):
            return const[:, CONST[name][0]:CONST[name][1]]

        def vc(name):
            return vec[:, VEC[name][0]:VEC[name][1]]

        X = room(0, KC, T)
        qk = room(16, 24, T)
        v1 = room(40, 2, HEADS * P)
        ga = room(52, KC, T)
        gb = room(68, KC, T)
        pads = [room(84 + 4.25 * j, 4, PAD + T) for j in range(3)]
        attn = room(96.75, SLOTS, T)
        pool = room(100.75, 4, T)
        cbt = cb[:, 1, :]
        rope_a = cbt[:, 0:512].rearrange("p (a b) -> p a b", a=2)
        rope_b = cbt[:, 512:1024].rearrange("p (a b) -> p a b", a=2)
        sc1 = cbt[:, 0:768].rearrange("p (a b) -> p a b", a=3)
        pt1 = cbt[:, 768:1536]
        mixw = cbt[:, 1536:2048].rearrange("p (a b) -> p a b", a=4)
        pq = room(16, KC, T)
        keys = room(32, KC, NKEY)
        score = [room(40, KC, NKEY), room(48, KC, NKEY)]
        cand = cb[:, 0, :].rearrange("p (h i) -> p h i", h=EH)
        eq = cb[:, 1, :].rearrange("p (h k j) -> p h k j", h=EH, k=TOPK)
        oh1 = [room(56 + 8 * j, 8, P) for j in range(2)]
        oh2 = [room(60 + 8 * j, 8, P) for j in range(2)]
        stage = [room(72 + 8 * j, P, BLK) for j in range(2)]
        topv = room(88, KC, TOPK)
        topi = room(89, KC, TOPK, dt=U32)
        topf = room(90, KC, TOPK)
        cv = room(91, EH, TOPK)
        ci = room(91.5, EH, TOPK, dt=U32)
        ca = room(92, EH, TOPK, dt=U32)
        cbi = room(92.5, EH, TOPK, dt=U32)
        caf = room(93, EH, TOPK)
        cbf = room(93.5, EH, TOPK)
        ids = room(94, 3, EH * TOPK)
        idT = room(96, 3, T)
        gsum = room(99, EH)
        XL, XH = split_room("x_low", 0, KC, T), split_room("x_high", 16, KC, T)
        ATH, ATL = split_room("at_high", 32, 16, T), split_room("at_low", 48, 16, T)
        G = room(64, NBLK, 16 * BLK)
        WP = split_room("w_parts", 80, PIECES, 2, PB * P)
        junk = ps[:, 4:8, :].rearrange("p a b -> p (a b)")
        gl = room(99.5, 2, T)
        ctxT = room(32, KC, T)
        X2 = room(72, KC, TA)
        q2 = room(0, H2, T)
        k2 = room(8, H2, TA)
        v2 = room(24, 4, H2 * P)
        cq = room(40, 3, T)
        ckv = room(43, 2, TA)
        kr = room(47, TA)
        vm = room(49, 4, H2 * P)
        sq2 = room(65, 4, T)
        rope2 = [room(65 + 2 * j, 2, T) for j in range(2)]
        kn = room(72, H2, TA)
        qm = room(88, 2 * H2, T)
        mix = cb[:, :, :].rearrange("p a (b c) -> p (a b) c", c=T)
        adaf = ada[:, :, :].rearrange("p a b -> p (a b)")
        prob = [adaf[:, 1024 * j:1024 * j + 1024].rearrange("p (a b) -> p a b", a=2) for j in range(2)]
        wt2 = [adaf[:, 2048 + 512 * j:2560 + 512 * j] for j in range(2)]
        rs8 = room(0, H2, T)
        sq8 = room(8, H2, T)
        HH, HL = split_room("hidden_high", 32, FF, T), split_room("hidden_low", 92, FF, T)
        WF = split_room("w_parts_ff", 76, PIECES, 2, PB * P)
        gp = [const[:, 264 * j:264 * j + T + 2] for j in range(2)]
        gc = [const[:, 528 + T * j:528 + T * (j + 1)] for j in range(2)]

        def rope_step(n):
            if n < 4:
                return q2[:, 2 * n:2 * n + 2, :], 2 * T
            if n < 8:
                return k2[:, 2 * (n - 4):2 * (n - 4) + 2, CTX:], 2 * T
            if n < 12:
                return qm[:, H2 + 2 * (n - 8):H2 + 2 * (n - 8) + 2, :], 2 * T
            return kr[:, CTX:].unsqueeze(1), T

        def at_free(stage_name, i, per, u, j):
            if stage_name == "down":
                n, p = u // 4, 3 * (u % 4) + j
                if p == 3:
                    return None, i * (per // 4) + (OUTS["down"] + n)
                ahead = 3 + USED["down"] + 11 * n + (p - 3 if p >= 4 else p - 2)
                return i * (11 * per // 4) + ahead, None
            if j == PIECES - 1:
                return None, i * per + (OUTS[stage_name] + u)
            return i * (3 * per) + (USED[stage_name] + 3 * u + j + 1), None

        w_slot = [sem(f"w_slot{j}") for j in range(RING)]
        acc_full = sem("acc_full")
        acc_free = sem("acc_free")
        a_slot = [sem(f"a_slot{j}") for j in range(2)]
        a_free = sem("a_free")
        x_in = sem("x_in")
        c_in = sem("c_in")
        const_in = sem("const_in")
        keys_in = sem("keys_in")
        c2_in = sem("c2_in")
        ctx_in = sem("ctx_in")
        c_silu = sem("c_silu")
        zeroed = sem("zeroed")
        dve_done = sem("dve_done")
        act_done = sem("act_done")
        squared = sem("squared")
        summed = sem("summed")
        var_ready = sem("var_ready")
        std_ready = sem("std_ready")
        scaled = sem("scaled")
        shifted = sem("shifted")
        rotated = sem("rotated")
        roped = sem("roped")
        s_ready = sem("s_ready")
        max_ready = sem("max_ready")
        exp_ready = sem("exp_ready")
        p_ready = sem("p_ready")
        pt_ready = sem("pt_ready")
        pt_copied = sem("pt_copied")
        o_ready = sem("o_ready")
        o_copied = sem("o_copied")
        pooled = sem("pooled")
        merged = sem("merged")
        h_ready = sem("h_ready")
        score_in = sem("score_in")
        cand_ready = sem("cand_ready")
        gate_exp = sem("gate_exp")
        ids_ready = sem("ids_ready")
        ids_turned = sem("ids_turned")
        ids_copied = sem("ids_copied")
        oh_dve = sem("oh_dve")
        oh_pool = sem("oh_pool")
        g_full = sem("g_full")
        g_copied = sem("g_copied")
        g_stored = [sem(f"g_stored{j}") for j in range(2)]
        g_in = sem("g_in")
        gelu_done = sem("gelu_done")
        at_ready = sem("at_ready")
        lam_exp = sem("lam_exp")
        sub_sq = sem("sub_sq")
        sub_sum = sem("sub_sum")
        sub_var = sem("sub_var")
        sub_std = sem("sub_std")
        mixed = sem("mixed")
        g_row = sem("g_row")
        conv_ready = sem("conv_ready")
        silu_done = sem("silu_done")
        out_done = sem("out_done")
        hi_ready = sem("hi_ready")
        lo_ready = sem("lo_ready")
        piece_used = sem("piece_used")
        xh_ready = sem("xh_ready")
        xl_ready = sem("xl_ready")
        hid_done = sem("hid_done")

        block = ctx.enter_context(nc.Block())

        @block.sync
        def _(sp):
            def load(slot, src, made, n=D, split=None):
                if made is not None:
                    sp.wait_ge(acc_full, made)
                if split is not None:
                    sp.wait_ge(lo_ready, split)
                sp.dma_start(ring[:, slot % RING, 0:n], src).then_inc(w_slot[slot % RING], 16)

            def stream(name, src, count, n=D, o_name=None):
                o = OUTS[o_name or name]
                with sp.Fori(0, count // U) as i:
                    for u in range(U):
                        load(u, src[i * U + u], i * U + (o + u + 1 - RING), n)

            sp.dma_start(hT[:], A["x"]).then_inc(x_in, 16)
            sp.dma_start(cb[:, 0, :], A["c"]).then_inc(c_in, 16)
            sp.dma_start(const[:], A["const"]).then_inc(const_in, 16)
            sp.dma_start(vec[:], A["vec"]).then_inc(const_in, 16)
            sp.dma_start(mixw, A["pool_mix"]).then_inc(const_in, 16)
            for u in range(RING):
                load(u, A["w_in"][u], None)
            with sp.Fori(0, 72 // RING - 1) as i:
                for u in range(RING):
                    load(u, A["w_in"][i * RING + (RING + u)], i * RING + (u + 1))
            for t in range(8):
                load(t, A["w_branch"][t], 72 - RING + t + 1 if t < RING else OUTS["branch"] + 4 * (t - RING + 1))
            stream("wo", A["w_out"], 16)
            stream("wq", A["peer_wq"], 16)
            sp.wait_ge(acc_full, OUTS["key"])
            with sp.Fori(0, NG) as i:
                for u in range(32):
                    src = A["peer_down"] if u < 16 else A["peer_up"]
                    load(u, src[i * 16 + u % 16], None, split=i * (32 * PIECES) + PIECES * (u + 1))
            with sp.Fori(0, 3) as i:
                for u in range(U):
                    load(u, A["w_in_2"][i * U + u], i * U + (OUTS["q2"] + u + 1 - RING))
            for u in range(24, 30):
                load(u, A["w_in_2"][u], OUTS["q2"] + u + 1 - RING)
            for t in range(2):
                load(TILES["ukv"] + t, A["w_ukv_2"][t], OUTS["ukv"] + t + 1 - RING)
            for t in range(4):
                load(TILES["uq"] + t, A["w_uq_2"][t], OUTS["ukv"] + t - 1 if t < 2 else OUTS["ukv"] + 8 * (t - 1),
                     12 * P)
            for t in range(16):
                load(TILES["wo2"] + t, A["w_o_2"][t],
                     OUTS["uq"] + 4 * (t + 1) if t < RING else OUTS["wo2"] + t + 1 - RING)
            for u in range(RING):
                load(u, A["w_up_2"][u], OUTS["up"] + u + 1 - RING)
            with sp.Fori(0, 88 // RING - 1) as i:
                for u in range(RING):
                    load(u, A["w_up_2"][i * RING + (RING + u)], None,
                         split=i * (RING * PIECES) + (16 + SPLIT["up"] + PIECES * (u + 1)))
            for u in range(RING):
                load(u, A["w_down_2"][u], None, 11 * P, split=16 + SPLIT["down"] - PIECES * (RING - 1 - u))
            with sp.Fori(0, KC - 1) as i:
                for u in range(RING):
                    load(u, A["w_down_2"][i * 4 + (4 + u)], None, 11 * P,
                         split=i * 12 + (16 + SPLIT["down"] + 3 * (u + 1)))
            sp.wait_ge(scaled, before("f2", "scaled") + KC)
            sp.dma_start(out, hT[:]).then_inc(out_done, 16)
            sp.wait_ge(out_done, 16)

        @block.gpsimd
        def _(pool_e):
            def ada_load(tile, slot, src):
                pool_e.wait_ge(a_free, tile + 1)
                pool_e.dma_start(ada[:, slot, :], src).then_inc(a_slot[slot], 16)

            with pool_e.Fori(0, 48) as i:
                for u in range(2):
                    ada_load(i * 2 + u, u, A["ada"][i * 2 + u])
            pool_e.wait_ge(o_ready, 8)
            pool_e.dma_start(keys, A["keys"]).then_inc(keys_in, 16)
            with pool_e.Fori(0, NBLK) as i:
                for j in range(2):
                    pool_e.wait_ge(oh_dve, i * 2 + (j + 1))
                    tok = bass.ds(i * 16 + 8 * j, 8)
                    nc.gpsimd.tensor_tensor(
                        oh2[j], oh2[j], idT[:, 2, tok].unsqueeze(2).broadcast_to([P, 8, P]), ALU.mult,
                    ).then_inc(oh_pool, 1)
            pool_e.wait_ge(ids_ready, 2)
            pool_e.dma_start(cb[:, 0, :], A["c_2"]).then_inc(c2_in, 16)
            pool_e.dma_start(cb[:, 1, :], A["c_ctx_2"]).then_inc(c2_in, 16)
            pool_e.wait_ge(g_full, TWO + 2 * NBLK)
            pool_e.wait_ge(g_copied, TWO + 2 * NBLK)
            pool_e.wait_ge(g_stored[0], 16 + 16 * NBLK // 2)
            pool_e.wait_ge(g_stored[1], 16 + 16 * NBLK // 2)
            with pool_e.Fori(0, NG) as i:
                pool_e.wait_ge(at_ready, i * 16 + TWO)
                pool_e.dma_start(G, gates_dram[i]).then_inc(g_in, 16)
                for u in range(12):
                    ada_load(i * 12 + (96 + u), u % 2, A["ada"][i * 12 + (96 + u)])
            pool_e.wait_ge(h_ready, 2)
            pool_e.dma_start(ctxT, A["ctx"]).then_inc(ctx_in, 16)

        @block.scalar
        def _(act):
            ch = Chain(act, act_done)

            def act_fn(*a, **k):
                return nc.scalar.activation(*a, **k)

            def norm(name, src, sqd, dst, shift=None, cols=T, high_to=None):
                i, n = NORM_AT[name], NORMS[NORM_AT[name]][1]
                for b in range(max(1, n // 4)):
                    w = min(4, n)
                    act_fn(sqd[:, 4 * b:4 * b + w, :], src[:, 4 * b:4 * b + w, :], ACT.Square).then_inc(squared, 1)
                act.wait_ge(var_ready, i + 1)
                act_fn(rs[:, 0:cols], rs[:, 0:cols], ACT.Sqrt).then_inc(std_ready, 1)
                if shift is not None:
                    for k in range(n):
                        act.wait_ge(scaled, before(name, "scaled") + k + 1)
                        act_fn(dst[:, k, :] if high_to is None else high_to[:, k, :], dst[:, k, :], ACT.Identity,
                               bias=shift[:, k:k + 1]).then_inc(shifted, 1)

            act.wait_ge(c_in, 16)
            act_fn(cb[:, 0, :], cb[:, 0, :], ACT.Silu).then_inc(c_silu, 1)
            act.wait_ge(x_in, 16)
            norm("a1", hT, X, X, mod1[:, 0:KC])

            with act.Fori(0, 24 // U) as i:
                for u in range(U):
                    act.wait_ge(acc_full, i * U + (u + 1))
                    act_fn(qk[:, i * U + u, :], ps[:, u % BANKS, 0:T], ACT.Copy).then_inc(acc_free, 1)
            for n in range(HEADS):
                o = OUTS["v"] + n
                act.wait_ge(acc_full, o + 1)
                act_fn(v1[:, :, n * P:(n + 1) * P], ps[:, o % BANKS, 0:T].rearrange("p (a b) -> p a b", a=2),
                       ACT.Copy).then_inc(acc_free, 1)

            act.wait_ge(zeroed, 1)
            act.wait_ge(const_in, 48)
            for k in range(36):
                o = OUTS["gate"] + k + (4 if k > MIX_AFTER else 0)
                act.wait_ge(acc_full, o + 1)
                if k < 4:
                    act_fn(pads[0][:, k, PAD:], ps[:, o % BANKS, 0:T], ACT.Copy).then_inc(acc_free, 1)
                else:
                    to = ga[:, k - 4, :] if k < 20 else gb[:, k - 20, :]
                    act_fn(to, ps[:, o % BANKS, 0:T], ACT.Sigmoid).then_inc(acc_free, 1)
                if k == MIX_AFTER:
                    for g in range(4):
                        o = OUTS["gate"] + MIX_AFTER + 1 + g
                        act.wait_ge(acc_full, o + 1)
                        act_fn(pool[:, g, :], ps[:, o % BANKS, 0:T], ACT.Copy,
                               scale=vc("pool_scale")[:, g:g + 1]).then_inc(acc_free, 1)
                u = (k - 1) // 4
                if k % 4 == 1 and u < 8:
                    w = 3 * P * (u % 2 + 1)
                    act.wait_ge(max_ready, u + 1)
                    s = sc1[:, :, 0:P * (u % 2 + 1)]
                    act_fn(s, s, ACT.Exp, bias=small[:, 0:1], accum_out=small[:, 1:2]).then_inc(exp_ready, 1)
                if k % 4 == 2 and u < 8:
                    w = 3 * P * (u % 2 + 1)
                    act.wait_ge(pt_ready, u + 1)
                    if u:
                        act.wait_ge(o_ready, u)
                    act_fn(pt1[:, 0:w], ps[:, 6:8, :].rearrange("p a b -> p (a b)")[:, 0:w], ACT.Copy)\
                        .then_inc(pt_copied, 1)
                if k % 4 == 0 and k:
                    u = k // 4 - 1
                    act.wait_ge(o_ready, u + 1)
                    act_fn(attn[:, u // 2, (u % 2) * P:(u % 2 + 1) * P], ps[:, 7, 256:384], ACT.Copy)\
                        .then_inc(o_copied, 1)

            act.wait_ge(h_ready, 1)
            norm("b1", hT, X, X, mod1[:, 48:64])

            with act.Fori(0, 16 // U) as i:
                for u in range(U):
                    act.wait_ge(acc_full, i * U + (OUTS["wq"] + u + 1))
                    act_fn(pq[:, i * U + u, :], ps[:, u % BANKS, 0:T], ACT.Copy).then_inc(acc_free, 1)
            for n in range(8):
                o = OUTS["key"] + n
                act.wait_ge(acc_full, o + 1)
                act_fn(score[n // 4][:, 4 * (n % 4):4 * (n % 4) + 4, :].rearrange("p a b -> p (a b)"),
                       ps[:, o % BANKS, :], ACT.Copy).then_inc(acc_free, 1)
            for tb in range(2):
                act.wait_ge(cand_ready, tb + 1)
                act_fn(ids[:, 2, :].rearrange("p (h k) -> p h k", h=EH), cv, ACT.Exp).then_inc(gate_exp, 1)
                act.wait_ge(ids_turned, tb + 1)
                act_fn(idT[:, :, tb * P:(tb + 1) * P], ps[:, 4, 0:3 * P].rearrange("p (a b) -> p a b", a=3),
                       ACT.Copy).then_inc(ids_copied, 1)
            with act.Fori(0, NBLK // 2) as i:
                for j in range(2):
                    act.wait_ge(g_stored[j], i * 16 + 16)
                    for hv in range(2):
                        act.wait_ge(g_full, i * 4 + (TWO + 2 * j + hv + 1))
                        for q in range(2):
                            t0 = 8 * hv + 4 * q
                            ins = act_fn(stage[j][:, :, t0:t0 + 4],
                                         ps[:, 4 + 2 * hv + q, :].rearrange("p (t c) -> p c t", t=4), ACT.Copy)
                        ins.then_inc(g_copied, 1)
                    act.wait_ge(g_copied, i * 4 + (TWO + 2 * j + 2))
                    act.dma_start(gates_dram[:, :, i * 2 + j, :].rearrange("g p f -> p g f"),
                                  stage[j].rearrange("p (g c) t -> p g (c t)", g=NG)).then_inc(g_stored[j], 16)
            act.wait_ge(c2_in, 32)
            act_fn(cb[:, 0, :], cb[:, 0, :], ACT.Silu).then_inc(c_silu, 1)
            act_fn(cb[:, 1, :], cb[:, 1, :], ACT.Silu).then_inc(c_silu, 1)
            for b in range(4):
                act_fn(XH[:, 4 * b:4 * b + 4, :], X[:, 4 * b:4 * b + 4, :], ACT.Copy).then_inc(xh_ready, 1)

            def high(parts, stage_name, i, per, u, slot, n=PIECES * PB, at=0, pieces=PIECES):
                for j in range(pieces):
                    w = min(PB, n - PB * j) * P
                    used, full = at_free(stage_name, i, per, u, j)
                    if full is None:
                        act.wait_ge(piece_used, used)
                    else:
                        act.wait_ge(acc_full, full)
                    m = (pieces * u + j) % PIECES
                    act_fn(parts[:, m, 0, 0:w], ring[:, slot, j * PB * P:j * PB * P + w], ACT.Copy)\
                        .then_inc(hi_ready, 1)

            act.wait_ge(g_stored[0], 16 + 16 * NBLK // 2)
            act.wait_ge(g_stored[1], 16 + 16 * NBLK // 2)

            def gelu(i, u):
                act.wait_ge(acc_full, i * 32 + (OUTS["peer"] + u + 1))
                act.wait_ge(at_ready, i * 16 + (u + TWO - 1))
                act_fn(gl[:, u % 2, :], ps[:, u % BANKS, 0:T], ACT.Gelu).then_inc(gelu_done, 1)

            with act.Fori(0, NG) as i:
                for u in range(32):
                    act.wait_ge(w_slot[u % RING], i * (16 * 32 // RING) + 16 * ((TILES["peer"] + u) // RING + 1))
                    high(WP, "peer", i, 32, u, u % RING)
                    if 1 <= u <= 16:
                        gelu(i, u - 1)

            act.wait_ge(h_ready, 2)
            norm("f1", hT, X, None)
            act.wait_ge(ctx_in, 16)
            norm("ctx", ctxT, X2[:, :, 0:CTX], X2[:, :, 0:CTX], modc[:, 0:KC])
            act.wait_ge(scaled, before("f1", "scaled") + KC)
            norm("a2", hT, X2[:, :, CTX:], X2[:, :, CTX:], mod2[:, 0:KC])

            def out_copy(o, to, n=T):
                act.wait_ge(acc_full, o + 1)
                src = ps[:, o % BANKS, 0:n]
                if len(to.shape) == 3:
                    src = src.rearrange("p (a b) -> p a b", a=to.shape[1])
                return act_fn(to, src, ACT.Copy)

            def out_loop(name, to, n):
                with act.Fori(0, 2) as i:
                    for u in range(4):
                        act.wait_ge(acc_full, i * 4 + (OUTS[name] + u + 1))
                        act_fn(to[:, i * 4 + u, :], ps[:, u % BANKS, 0:n], ACT.Copy).then_inc(acc_free, 1)

            out_loop("q2", q2, T)
            out_loop("k2", k2, TA)
            with act.Fori(0, 2) as i:
                for u in range(4):
                    act.wait_ge(acc_full, i * 4 + (OUTS["v2"] + u + 1))
                    act_fn(v2[:, :, bass.ds(i * 512 + u * P, P)],
                           ps[:, u % BANKS, :].rearrange("p (a b) -> p a b", a=4), ACT.Copy).then_inc(acc_free, 1)
            for n in range(2):
                out_copy(OUTS["c2"] + n, ckv[:, n, :], TA).then_inc(acc_free, 1)
            out_copy(OUTS["c2"] + 2, kr, TA).then_inc(acc_free, 1)
            for n in range(3):
                out_copy(OUTS["c2"] + 3 + n, cq[:, n, :], T).then_inc(acc_free, 1)
            act.wait_ge(acc_free, BANKS + OUTS["ukv"])
            norm("kv", ckv, kn[:, 0:2, :], None, cols=TA)
            norm("q", cq, sq2[:, 0:3, :], None)
            for n in range(16):
                to = kn[:, n, :] if n < 8 else vm[:, :, (n - 8) * P:(n - 7) * P]
                out_copy(OUTS["ukv"] + n, to, TA).then_inc(acc_free, 1)
            for n in range(16):
                out_copy(OUTS["uq"] + n, qm[:, n, :], T).then_inc(acc_free, 1)
            act.wait_ge(max_ready, 8 + 1)
            act_fn(small[:, 8:10], small[:, 8:10], ACT.Exp).then_inc(lam_exp, 1)

            def stage_exp(u):
                two = u < 16
                act.wait_ge(max_ready, 8 + 1 + u + 1)
                for j in range(2 if two else 1):
                    ins = act_fn(prob[u % 2][:, j, :], ps[:, 2 * (u % 2) + j, :], ACT.Exp,
                                 bias=small[:, 4 * (u % 2) + j:4 * (u % 2) + j + 1],
                                 scale=SM_DA if two else SM_MLA,
                                 accum_out=small[:, 4 * (u % 2) + 2 + j:4 * (u % 2) + 3 + j])
                ins.then_inc(exp_ready, 1)

            def stage_turn(u):
                act.wait_ge(pt_ready, 8 + u + 1)
                if u >= 2:
                    act.wait_ge(o_ready, 8 + u - 1)
                act_fn(wt2[u % 2], ps[:, 4 + u % 2, :], ACT.Copy).then_inc(pt_copied, 1)

            def stage_out(u):
                head, qb = u // 2, u % 2
                act.wait_ge(o_ready, 8 + u + 1)
                act_fn(mix[:, head, qb * P:(qb + 1) * P], ps[:, 6 + u % 2, 0:P], ACT.Copy).then_inc(o_copied, 1)

            for s in range(32 + 2):
                if s < 32:
                    stage_exp(s)
                if 1 <= s <= 32:
                    stage_turn(s - 1)
                if s >= 2:
                    stage_out(s - 2)
            act.wait_ge(o_copied, 8 + 16)
            for b in range(2):
                act_fn(sq8[:, 4 * b:4 * b + 4, :], mix[:, 4 * b:4 * b + 4, :], ACT.Square).then_inc(sub_sq, 1)
            act.wait_ge(sub_var, 1)
            act_fn(rs8, rs8, ACT.Sqrt).then_inc(sub_std, 1)

            act.wait_ge(h_ready, 3)
            norm("b2", hT, X, X, mod2[:, 48:64], high_to=XH)

            def gate_row(i, p):
                act.wait_ge(acc_full, i * U + (OUTS["up"] + 2 * p + 1))
                act.wait_ge(conv_ready, i * 4 + (p + TWO - 1))
                act_fn(gp[p % 2][:, 1:T + 1], ps[:, (OUTS["up"] + 2 * p) % BANKS, 0:T], ACT.Copy)\
                    .then_inc(g_row, 1)

            def gate_silu(i, p):
                act.wait_ge(conv_ready, i * 4 + (p + TWO + 1))
                act_fn(gc[p % 2], gc[p % 2], ACT.Silu).then_inc(silu_done, 1)

            with act.Fori(0, FF // 4) as i:
                for u in range(U):
                    act.wait_ge(w_slot[u % RING], i * (16 * U // RING) + 16 * ((TILES["up"] + u) // RING + 1))
                    high(WF, "up", i, U, u, u % RING)
                    if u % 2:
                        gate_row(i, u // 2)
                    elif u:
                        gate_silu(i, u // 2 - 1)
                gate_silu(i, 3)
            with act.Fori(0, 4) as i:
                for u in range(16):
                    act.wait_ge(w_slot[u % RING], i * (16 * 16 // RING) + 16 * ((TILES["down"] + u) // RING + 1))
                    high(WF, "down", i, 16, u, u % RING, n=11, pieces=3)
            act.wait_ge(h_ready, 4)
            norm("f2", hT, X, None)

        @block.tensor
        def _(pe):
            mm = nc.tensor.matmul
            ones, ident = cst("ones"), cst("ident")

            def bank(o):
                pe.wait_ge(acc_free, o + 1)

            def norm_sum(name, sqd, n, cols=T):
                for k in range(n):
                    if k % 4 == 0:
                        pe.wait_ge(squared, before(name, "squares") + k // 4 + 1)
                    ins = mm(ps[:, 4, 0:cols], ones, sqd[:, k, :], start=(k == 0), stop=(k == n - 1))
                ins.then_inc(summed, 1)

            def blocks(to, slot, n, moving, at=0):
                for k in range(n):
                    ins = mm(to, ring[:, slot % RING, (at + k) * P:(at + k + 1) * P], moving(k),
                             start=(k == 0), stop=(k == n - 1))
                return ins

            def loop(name, turns, moving, out_name=None, cols=T, u_n=U):
                o0, t0 = OUTS[out_name or name], TILES[name]
                with pe.Fori(0, turns) as i:
                    for u in range(u_n):
                        pe.wait_ge(w_slot[u % RING], i * (16 * u_n // RING) + 16 * ((t0 + u) // RING + 1))
                        pe.wait_ge(acc_free, i * u_n + (o0 + u + 1))
                        blocks(ps[:, (o0 + u) % BANKS, 0:cols], u, KC, moving).then_inc(acc_full, 1)

            def one(tile, o, emit):
                pe.wait_ge(w_slot[tile % RING], 16 * (tile // RING + 1))
                bank(o)
                emit(tile % RING, o % BANKS)

            def tokens_first(slot, b, src, n, tbs, at=0):
                for tb in range(tbs):
                    for k in range(n):
                        ins = mm(ps[:, b, tb * P:(tb + 1) * P], src[:, k, tb * P:(tb + 1) * P],
                                 ring[:, slot, (at + k) * P:(at + k + 1) * P], start=(k == 0), stop=(k == n - 1))
                return ins

            pe.wait_ge(const_in, 48)
            norm_sum("a1", X, KC)
            pe.wait_ge(shifted, before("a1", "shifted") + KC)
            loop("qk", 24 // U, lambda k: X[:, k, :])
            pe.wait_ge(acc_free, BANKS + OUTS["v"])
            for n in range(HEADS):
                one(TILES["v"] + n, OUTS["v"] + n,
                    lambda s, b: tokens_first(s, b, X, KC, 2).then_inc(acc_full, 1))
                if n >= 2:
                    pe.wait_ge(roped, n - 1)
                mm(ps[:, 4 + n % 2, :], cst("perm1"), qk[:, 2 * n:2 * n + 2, :], start=True, stop=True)\
                    .then_inc(rotated, 1)

            def s1(u):
                hs, qb = u // 2, u % 2
                if u == 0:
                    pe.wait_ge(roped, 12)
                else:
                    pe.wait_ge(max_ready, u)
                nk = P * (qb + 1)
                for g in range(3):
                    h = g * SLOTS + hs
                    ins = mm(ps[:, 4 + g // 2, (g % 2) * T:(g % 2) * T + nk], qk[:, h, qb * P:(qb + 1) * P],
                             qk[:, HEADS + h, 0:nk], start=True, stop=True)
                ins.then_inc(s_ready, 1)

            def t1(u):
                pe.wait_ge(p_ready, u + 1)
                if u:
                    pe.wait_ge(pt_copied, u)
                    pe.wait_ge(o_copied, u)
                nb = u % 2 + 1
                for g in range(3):
                    for kb in range(nb):
                        n = g * nb + kb
                        ins = nc.tensor.transpose(ps[:, 6 + n // 4, (n % 4) * P:(n % 4 + 1) * P],
                                                  sc1[:, g, kb * P:(kb + 1) * P], ident)
                ins.then_inc(pt_ready, 1)

            def y1(u):
                hs, nb = u // 2, u % 2 + 1
                pe.wait_ge(pt_copied, u + 1)
                for g in range(3):
                    h = g * SLOTS + hs
                    for kb in range(nb):
                        n = g * nb + kb
                        ins = mm(ps[:, 7, 256:384], v1[:, kb, h * P:(h + 1) * P], pt1[:, n * P:(n + 1) * P],
                                 start=(n == 0), stop=(n == 3 * nb - 1))
                ins.then_inc(o_ready, 1)

            for k in range(36):
                o = OUTS["gate"] + k + (4 if k > MIX_AFTER else 0)
                one(TILES["gate"] + k, o,
                    lambda s, b: blocks(ps[:, b, 0:T], s, KC, lambda c: X[:, c, :]).then_inc(acc_full, 1))
                if k == MIX_AFTER:
                    pe.wait_ge(pooled, 1)
                    for g in range(4):
                        o = OUTS["gate"] + MIX_AFTER + 1 + g
                        bank(o)
                        mm(ps[:, o % BANKS, 0:T], mixw[:, g, :], pads[2][:, g, PAD:], start=True, stop=True)\
                            .then_inc(acc_full, 1)
                u = k // 4
                if u < 8:
                    if k % 4 == 0:
                        s1(u)
                    if k % 4 == 2:
                        t1(u)
                    if k % 4 == 3:
                        y1(u)
            pe.wait_ge(acc_free, BANKS + OUTS["branch"])
            pe.wait_ge(o_copied, 8)
            for t in range(8):
                src = attn if t % 2 == 0 else pool
                pe.wait_ge(w_slot[t % RING], 16 * ((TILES["branch"] + t) // RING + 1))
                for n in range(4):
                    o = OUTS["branch"] + 4 * t + n
                    bank(o)
                    blocks(ps[:, o % BANKS, 0:T], t, 4, lambda c: src[:, c, :], at=4 * n).then_inc(acc_full, 1)
            pe.wait_ge(merged, 4)
            loop("wo", 16 // U, lambda k: ga[:, k, :])
            norm_sum("b1", X, KC)
            pe.wait_ge(shifted, before("b1", "shifted") + KC)
            loop("wq", 16 // U, lambda k: X[:, k, :])
            pe.wait_ge(acc_free, BANKS + OUTS["key"])
            pe.wait_ge(keys_in, 16)
            for n in range(8):
                o, tb = OUTS["key"] + n, n // 4
                bank(o)
                for j in range(4):
                    c = 4 * (n % 4) + j
                    ins = mm(ps[:, o % BANKS, j * P:(j + 1) * P], pq[:, c, tb * P:(tb + 1) * P], keys[:, c, :],
                             start=True, stop=True)
                ins.then_inc(acc_full, 1)
            for tb in range(2):
                pe.wait_ge(ids_ready, tb + 1)
                if tb:
                    pe.wait_ge(ids_copied, tb)
                for j in range(3):
                    ins = nc.tensor.transpose(ps[:, 4, j * P:(j + 1) * P], ids[:, j, :], ident)
                ins.then_inc(ids_turned, 1)
            pe.wait_ge(ids_copied, 2)
            with pe.Fori(0, NBLK) as i:
                for j in range(2):
                    pe.wait_ge(oh_pool, i * 2 + (j + 1))
                    pe.wait_ge(g_copied, i * 2 + (j - 1 + TWO))
                    for q in range(8):
                        ins = mm(ps[:, 4 + 2 * j + q // 4, (q % 4) * P:(q % 4 + 1) * P], oh1[j][:, q, :],
                                 oh2[j][:, q, :], start=True, stop=True)
                    ins.then_inc(g_full, 1)
            def piece(to, parts, m, wait, first, n, high, low, k_all):
                pe.wait_ge(lo_ready, wait)
                for b in range(n):
                    k = first + b
                    w_high, w_low = (parts[:, m, h, b * P:(b + 1) * P] for h in range(2))
                    mm(to, w_high, high(k), start=(k == 0), stop=False)
                    mm(to, w_high, low(k), start=False, stop=False)
                    ins = mm(to, w_low, high(k), start=False, stop=(k == k_all - 1))
                return ins

            pe.wait_ge(xl_ready, 4)
            with pe.Fori(0, NG) as i:
                for u in range(32):
                    pe.wait_ge(acc_free, i * 32 + (OUTS["peer"] + u + 1))
                    xh, xl = (XH, XL) if u < 16 else (ATH, ATL)
                    for j in range(PIECES):
                        if u == 16:
                            pe.wait_ge(at_ready, i * 16 + (PB * (j + 1) + TWO))
                        ins = piece(ps[:, u % BANKS, 0:T], WP, j, i * (32 * PIECES) + (16 + PIECES * u + j + 1),
                                    PB * j, PB, lambda k: xh[:, k, :], lambda k: xl[:, k, :], KC)
                        ins.then_inc(piece_used if j < PIECES - 1 else acc_full, 1)

            norm_sum("f1", X, KC)
            pe.wait_ge(var_ready, NORM_AT["f1"] + 1)
            norm_sum("ctx", X2[:, :, 0:CTX], KC)
            pe.wait_ge(var_ready, NORM_AT["ctx"] + 1)
            norm_sum("a2", X2[:, :, CTX:], KC)
            pe.wait_ge(shifted, before("a2", "shifted") + KC)

            def loop_in2(name, skip, turn):
                with pe.Fori(0, 2) as i:
                    for u in range(4):
                        t, o = TILES["in2"] + skip + u, OUTS[name] + u
                        pe.wait_ge(w_slot[u % RING], i * 16 + 16 * (t // RING + 1))
                        pe.wait_ge(acc_free, i * 4 + (o + 1))
                        turn(u % RING, u % BANKS).then_inc(acc_full, 1)

            loop_in2("q2", 0, lambda s, b: blocks(ps[:, b, 0:T], s, KC, lambda k: X2[:, k, CTX:]))
            loop_in2("k2", 8, lambda s, b: blocks(ps[:, b, :], s, KC, lambda k: X2[:, k, :]))
            loop_in2("v2", 16, lambda s, b: tokens_first(s, b, X2, KC, 4))
            for n in range(6):
                one(TILES["in2"] + 24 + n, OUTS["c2"] + n,
                    (lambda s, b: blocks(ps[:, b, :], s, KC, lambda k: X2[:, k, :]).then_inc(acc_full, 1)) if n < 3
                    else (lambda s, b: blocks(ps[:, b, 0:T], s, KC, lambda k: X2[:, k, CTX:]).then_inc(acc_full, 1)))
            norm_sum("kv", kn[:, 0:2, :], 2, TA)
            pe.wait_ge(var_ready, NORM_AT["kv"] + 1)
            norm_sum("q", sq2, 3)
            pe.wait_ge(scaled, before("q", "scaled"))
            for t in range(2):
                tile = TILES["ukv"] + t
                pe.wait_ge(w_slot[tile % RING], 16 * (tile // RING + 1))
                for n in range(8):
                    o = OUTS["ukv"] + 8 * t + n
                    bank(o)
                    if t == 0:
                        ins = blocks(ps[:, o % BANKS, :], tile, 2, lambda k: ckv[:, k, :], at=2 * n)
                    else:
                        ins = tokens_first(tile % RING, o % BANKS, ckv, 2, 4, at=2 * n)
                    ins.then_inc(acc_full, 1)
            pe.wait_ge(scaled, before("q", "scaled") + 3)
            for t in range(4):
                tile = TILES["uq"] + t
                pe.wait_ge(w_slot[tile % RING], 16 * (tile // RING + 1))
                for n in range(4):
                    o = OUTS["uq"] + 4 * t + n
                    bank(o)
                    blocks(ps[:, o % BANKS, 0:T], tile, 3, lambda k: cq[:, k, :], at=3 * n).then_inc(acc_full, 1)
            pe.wait_ge(acc_free, BANKS + OUTS["wo2"])
            for n in range(13):
                if n >= 2:
                    pe.wait_ge(roped, 12 + n - 1)
                src, w = rope_step(n)
                mm(ps[:, 4 + n % 2, 0:w], cst("perm2"), src, start=True, stop=True).then_inc(rotated, 1)

            def s2(u):
                h, qb = (u // 2) % 8, u % 2
                if u == 0:
                    pe.wait_ge(roped, 12 + 13)
                if u >= 2:
                    pe.wait_ge(exp_ready, 8 + u - 1)
                cols = slice(qb * P, (qb + 1) * P)
                if u < 16:
                    for j in range(2):
                        rows = slice(64 * j, 64 * j + 64)
                        ins = mm(ps[:, 2 * (u % 2) + j, :], q2[rows, h, cols], k2[rows, h, :], start=True, stop=True)
                else:
                    mm(ps[:, 2 * (u % 2), :], qm[:, h, cols], kn[:, h, :], start=True, stop=False)
                    ins = mm(ps[:, 2 * (u % 2), :], qm[:, 8 + h, cols], kr, start=False, stop=True)
                ins.then_inc(s_ready, 1)

            def t2(u):
                pe.wait_ge(p_ready, 8 + u + 1)
                if u >= 2:
                    pe.wait_ge(pt_copied, 8 + u - 1)
                for kb in range(4):
                    ins = nc.tensor.transpose(ps[:, 4 + u % 2, kb * P:(kb + 1) * P],
                                              prob[u % 2][:, 0, kb * P:(kb + 1) * P], ident)
                ins.then_inc(pt_ready, 1)

            def o2(u):
                h = (u // 2) % 8
                pe.wait_ge(pt_copied, 8 + u + 1)
                if u >= 2:
                    pe.wait_ge(o_copied, 8 + u - 1)
                vv = v2 if u < 16 else vm
                for kb in range(4):
                    ins = mm(ps[:, 6 + u % 2, 0:P], vv[:, kb, h * P:(h + 1) * P], wt2[u % 2][:, kb * P:(kb + 1) * P],
                             start=(kb == 0), stop=(kb == 3))
                ins.then_inc(o_ready, 1)

            s2(0)
            for s in range(32 + 1):
                if s + 1 < 32:
                    s2(s + 1)
                if s < 32:
                    t2(s)
                if s >= 1:
                    o2(s - 1)
            for b in range(2):
                pe.wait_ge(sub_sq, b + 1)
                for j in range(2):
                    ins = mm(ps[:, 2 * b + j, :], ones, sq8[:, 4 * b + 2 * j:4 * b + 2 * j + 2, :],
                             start=True, stop=True)
            ins.then_inc(sub_sum, 1)
            pe.wait_ge(mixed, 1)
            pe.wait_ge(o_copied, 8 + 32)
            loop("wo2", 16 // U, lambda k: mix[:, k, :])
            norm_sum("b2", X, KC)
            pe.wait_ge(xl_ready, 4 + KC)
            with pe.Fori(0, FF // 4) as i:
                for u in range(U):
                    pe.wait_ge(acc_free, i * U + (OUTS["up"] + 2 * (u // 2) + 2))
                    for j in range(PIECES):
                        ins = piece(ps[:, (OUTS["up"] + u) % BANKS, 0:T], WF, j,
                                    i * (U * PIECES) + (16 + SPLIT["up"] + PIECES * u + j + 1),
                                    PB * j, PB, lambda k: XH[:, k, :], lambda k: XL[:, k, :], KC)
                        ins.then_inc(piece_used if j < PIECES - 1 else acc_full, 1)
            pe.wait_ge(hid_done, 1)
            with pe.Fori(0, 4) as i:
                for n in range(4):
                    pe.wait_ge(acc_free, i * 4 + (OUTS["down"] + n + 1))
                    for p in range(12):
                        blocks_n = PB if p % 3 < 2 else 3
                        ins = piece(ps[:, (OUTS["down"] + n) % BANKS, 0:T], WF, p % PIECES,
                                    i * 48 + (16 + SPLIT["down"] + 12 * n + p + 1),
                                    11 * (p // 3) + PB * (p % 3), blocks_n,
                                    lambda k: HH[:, k, :], lambda k: HL[:, k, :], FF)
                        ins.then_inc(piece_used if p < 11 else acc_full, 1)
            norm_sum("f2", X, KC)

        @block.vector
        def _(dve):
            ch = Chain(dve, dve_done)
            vv = nc.vector

            def ada_row(slot, wait, c_row, to):
                dve.wait_ge(a_slot[slot], wait)
                vv.tensor_tensor_reduce(ada[:, slot, :], ada[:, slot, :], c_row, 1.0, 0.0, ALU.mult, ALU.add,
                                        to).then_inc(a_free, 1)

            def ada_static(tile, to):
                ada_row(tile % 2, 16 * (tile // 2 + 1), cb[:, 0, :], to)

            def norm(name, src, dst, gain, shift_cols=None, cols=T):
                i = NORM_AT[name]
                _, n, _, width, _ = NORMS[i]
                dve.wait_ge(summed, i + 1)
                vv.tensor_scalar(rs[:, 0:cols], ps[:, 4, 0:cols], 1.0 / width, EPS, ALU.mult, ALU.add)\
                    .then_inc(var_ready, 1)
                dve.wait_ge(std_ready, i + 1)
                ch.link(vv.reciprocal(rs[:, 0:cols], rs[:, 0:cols]))
                for k in range(n):
                    vv.scalar_tensor_tensor(dst[:, k, :], src[:, k, :], gain[:, k:k + 1], rs[:, 0:cols],
                                            ALU.mult, ALU.mult).then_inc(scaled, 1)
                dve.wait_ge(scaled, before(name, "scaled") + n)

            def gain_of(scale, g):
                ch.link(vv.scalar_tensor_tensor(coef[:], scale, 1.0, g, ALU.add, ALU.mult))

            dve.sem_inc(acc_free, BANKS)
            dve.sem_inc(lo_ready, 16)
            dve.sem_inc(piece_used, PIECES - 1)
            dve.sem_inc(a_free, TWO)
            dve.sem_inc(at_ready, TWO)
            dve.sem_inc(g_copied, TWO)
            dve.sem_inc(g_full, TWO)
            for j in range(2):
                dve.sem_inc(g_stored[j], 16)
            for j in range(3):
                ins = vv.memset(pads[j], 0.0)
            ins.then_inc(zeroed, 1)

            dve.wait_ge(c_silu, 1)
            for t in range(32):
                ada_static(t, mod1[:, t:t + 1])
            dve.wait_ge(a_free, 2 + 32)
            dve.wait_ge(const_in, 48)
            ch.link(vv.tensor_tensor(mod1[:, 0:32], mod1[:, 0:32], vc("ada_b")[:, 0:32], ALU.add))
            gain_of(mod1[:, 16:32], vc("norm1_g"))
            norm("a1", hT, X, coef)

            with dve.Fori(0, 3) as i:
                ch.enter(i, 1)
                for u in range(8):
                    ada_row(u % 2, i * 64 + 16 * ((32 + u) // 2 + 1), cb[:, 0, :], modt[:, u:u + 1])
                dve.wait_ge(a_free, i * 8 + (2 + 32 + 8))
                ch.link(vv.tensor_copy(mod1[:, bass.ds(i * 8 + 32, 8)], modt[:, 0:8]))
            ch.leave(3)

            def rope(step, rot_n, bankn, chunk, w, a, b, cos, sin):
                dve.wait_ge(rotated, rot_n + 1)
                ch.tick(vv.tensor_tensor(a, ps[:, bankn, 0:w].rearrange("p (a b) -> p a b", b=T), sin, ALU.mult))
                ch.link(vv.tensor_tensor(b, chunk, cos, ALU.mult))
                vv.tensor_tensor(chunk, a, b, ALU.add).then_inc(roped, 1)
                dve.wait_ge(roped, rot_n + 1)

            def both(name, n):
                return cst(name).unsqueeze(1).broadcast_to([P, n, T])

            at = 56
            for n in range(HEADS):
                ada_static(at, mod1[:, at:at + 1])
                at += 1
                rope(n, n, 4 + n % 2, qk[:, 2 * n:2 * n + 2, :], 512, rope_a, rope_b, both("cos1", 2), both("sin1", 2))

            def pool_rows():
                dve.wait_ge(acc_free, BANKS + OUTS["gate"] + 4)
                w = 1
                src = pads[0]
                for level in range(4):
                    to = pads[1 + level % 2]
                    ch.link(vv.tensor_tensor(to[:, level:4, PAD:], src[:, level:4, PAD:],
                                             src[:, level:4, PAD - w:PAD + T - w], ALU.add))
                    src, w = to, 2 * w
                rc = cst("rcount").rearrange("p (a b) -> p a b", a=4)
                for g in range(4):
                    s = pads[1 + g % 2]
                    ch.tick(vv.tensor_tensor(s[:, g, PAD:], s[:, g, PAD:], rc[:, g, :], ALU.mult))
                ch.sync()
                for g in range(4):
                    s = pads[1 + g % 2]
                    ins = vv.tensor_tensor(pads[2][:, g, PAD:], s[:, g, PAD:], pads[0][:, g, PAD:], ALU.subtract)
                ins.then_inc(pooled, 1)

            for u in range(8):
                qb = u % 2
                nk = P * (qb + 1)
                s = sc1[:, :, 0:nk]
                mask = cst(f"mask{qb}").rearrange("p (a b) -> p a b", a=3)
                dve.wait_ge(s_ready, u + 1)
                if u:
                    dve.wait_ge(pt_ready, u)
                scores = ps[:, 4:6, :].rearrange("p a (b c) -> p (a b) c", c=T)[:, 0:3, 0:nk]
                ch.link(vv.scalar_tensor_tensor(s, scores, SM1, mask, ALU.mult, ALU.add))
                ch.link(vv.tensor_reduce(small[:, 2:3], s, mybir.AxisListType.XY, ALU.max))
                vv.tensor_scalar(small[:, 0:1], small[:, 2:3], -1.0, None, ALU.mult).then_inc(max_ready, 1)
                if at < 96:
                    ada_static(at, mod1[:, at:at + 1])
                    at += 1
                if u == 2:
                    pool_rows()
                dve.wait_ge(exp_ready, u + 1)
                ch.link(vv.reciprocal(small[:, 3:4], small[:, 1:2]))
                vv.tensor_scalar(s, s, small[:, 3:4], None, ALU.mult).then_inc(p_ready, 1)
                for _ in range(3):
                    if at < 96:
                        ada_static(at, mod1[:, at:at + 1])
                        at += 1
            assert at == 96, at
            dve.wait_ge(a_free, 2 + 96)
            ch.link(vv.tensor_tensor(mod1[:, 32:96], mod1[:, 32:96], vc("ada_b")[:, 32:96], ALU.add))

            for t in range(8):
                g = ga if t % 2 == 0 else gb
                for n in range(4):
                    o, c = OUTS["branch"] + 4 * t + n, 4 * (t // 2) + n
                    dve.wait_ge(acc_full, o + 1)
                    vv.tensor_tensor(g[:, c, :], g[:, c, :], ps[:, o % BANKS, 0:T], ALU.mult).then_inc(acc_free, 1)
                if t % 2:
                    c = 4 * (t // 2)
                    dve.wait_ge(acc_free, BANKS + OUTS["branch"] + 4 * (t + 1))
                    vv.tensor_tensor(ga[:, c:c + 4, :], ga[:, c:c + 4, :], gb[:, c:c + 4, :], ALU.add)\
                        .then_inc(merged, 1)

            def residual(name, turns, gate, gate_at):
                with dve.Fori(0, turns) as i:
                    for u in range(U):
                        dve.wait_ge(acc_full, i * U + (OUTS[name] + u + 1))
                        c = i * U + u
                        vv.scalar_tensor_tensor(hT[:, c, :], ps[:, (OUTS[name] + u) % BANKS, 0:T],
                                                gate[:, bass.ds(i * U + (gate_at + u), 1)], hT[:, c, :],
                                                ALU.mult, ALU.add).then_inc(acc_free, 1)

            residual("wo", 2, mod1, 32)
            dve.wait_ge(acc_free, BANKS + OUTS["wq"])
            dve.sem_inc(h_ready, 1)
            gain_of(mod1[:, 64:80], vc("norm2_g"))
            norm("b1", hT, X, coef)

            def best(to_v, to_i, rows, n):
                for r in range(n):
                    ins = vv.max(to_v[:, r, 0:8], rows[:, r, :])
                ch.link(ins)
                for r in range(n):
                    ins = vv.max_index(to_i[:, r, 0:8], to_v[:, r, 0:8], rows[:, r, :])
                ch.link(ins)
                for r in range(n):
                    ins = vv.match_replace(rows[:, r, :], to_v[:, r, 0:8], rows[:, r, :], NEG)
                ch.link(ins)
                for r in range(n):
                    ins = vv.max(to_v[:, r, 8:16], rows[:, r, :])
                ch.link(ins)
                for r in range(n):
                    ins = vv.max_index(to_i[:, r, 8:16], to_v[:, r, 8:16], rows[:, r, :])
                ch.link(ins)

            iota = cst("iota")
            for tb in range(2):
                dve.wait_ge(acc_free, BANKS + OUTS["key"] + 4 * (tb + 1))
                best(topv, topi, score[tb], KC)
                ch.tick(vv.tensor_copy(topf, topi))
                pairs = topv.rearrange("p (h s) k -> p h s k", s=2)
                c4 = cand.rearrange("p h (i j) -> p h i j", i=TOPK)
                ch.link(vv.tensor_tensor(c4, pairs[:, :, 0, :].unsqueeze(3).broadcast_to([P, EH, TOPK, TOPK]),
                                         pairs[:, :, 1, :].unsqueeze(2).broadcast_to([P, EH, TOPK, TOPK]), ALU.add))
                best(cv, ci, cand, EH)
                ch.tick(vv.tensor_scalar(ca, ci, 4, None, ALU.logical_shift_right))
                ch.link(vv.tensor_scalar(cbi, ci, 15, None, ALU.bitwise_and))
                ch.tick(vv.tensor_copy(caf, ca))
                ch.tick(vv.tensor_copy(cbf, cbi))
                ch.link(vv.tensor_tensor(gsum, cv[:, :, 0], cv[:, :, 0], ALU.max))
                if tb:
                    dve.wait_ge(ids_turned, tb)
                vv.tensor_tensor(cv, cv, gsum.unsqueeze(2).broadcast_to([P, EH, TOPK]), ALU.subtract)\
                    .then_inc(cand_ready, 1)
                ff = topf.rearrange("p (h s) k -> p h s k", s=2)
                for j, pos in enumerate((caf, cbf)):
                    ch.link(vv.tensor_tensor(eq, pos.unsqueeze(3).broadcast_to([P, EH, TOPK, TOPK]),
                                             iota[:, 0:TOPK].unsqueeze(1).unsqueeze(1).broadcast_to([P, EH, TOPK, TOPK]),
                                             ALU.is_equal))
                    ch.link(vv.tensor_tensor(eq, eq, ff[:, :, j, :].unsqueeze(2).broadcast_to([P, EH, TOPK, TOPK]),
                                             ALU.mult))
                    ch.link(vv.tensor_reduce(ids[:, j, :], eq.rearrange("p h k j -> p (h k) j"), AX, ALU.add))
                dve.wait_ge(gate_exp, tb + 1)
                gt = ids[:, 2, :].rearrange("p (h k) -> p h k", h=EH)
                ch.link(vv.tensor_reduce(gsum, gt, AX, ALU.add))
                ch.link(vv.reciprocal(gsum, gsum))
                vv.tensor_tensor(gt, gt, gsum.unsqueeze(2).broadcast_to([P, EH, TOPK]), ALU.mult)\
                    .then_inc(ids_ready, 1)
                dve.wait_ge(ids_ready, tb + 1)

            dve.wait_ge(ids_copied, 2)
            with dve.Fori(0, NBLK) as i:
                for j in range(2):
                    tok = bass.ds(i * 16 + 8 * j, 8)
                    dve.wait_ge(g_full, i * 2 + (j + TWO - 1))
                    many = iota.unsqueeze(1).broadcast_to([P, 8, P])
                    vv.tensor_tensor(oh1[j], many, idT[:, 0, tok].unsqueeze(2).broadcast_to([P, 8, P]), ALU.is_equal)
                    vv.tensor_tensor(oh2[j], many, idT[:, 1, tok].unsqueeze(2).broadcast_to([P, 8, P]), ALU.is_equal)\
                        .then_inc(oh_dve, 1)

            def low(parts, ready, u, slot, n=PIECES * PB, pieces=PIECES):
                for j in range(pieces):
                    w = min(PB, n - PB * j) * P
                    m = (pieces * u + j) % PIECES
                    dve.wait_ge(hi_ready, ready + j)
                    vv.tensor_tensor(parts[:, m, 1, 0:w], ring[:, slot, j * PB * P:j * PB * P + w],
                                     parts[:, m, 0, 0:w].bitcast(F32), ALU.subtract).then_inc(lo_ready, 1)

            for b in range(4):
                dve.wait_ge(xh_ready, b + 1)
                vv.tensor_tensor(XL[:, 4 * b:4 * b + 4, :], X[:, 4 * b:4 * b + 4, :],
                                 XH[:, 4 * b:4 * b + 4, :].bitcast(F32), ALU.subtract).then_inc(xl_ready, 1)
            dve.wait_ge(c_silu, 3)

            def gated(i, u):
                dve.wait_ge(gelu_done, i * 16 + (u + 1))
                g = gl[:, u % 2, :]
                ch.link(vv.tensor_tensor(g.rearrange("p (a b) -> p a b", a=NBLK),
                                         g.rearrange("p (a b) -> p a b", a=NBLK),
                                         G[:, :, u * BLK:(u + 1) * BLK], ALU.mult))
                ch.link(vv.tensor_copy(ATH[:, u, :], g))
                vv.tensor_tensor(ATL[:, u, :], g, ATH[:, u, :].bitcast(F32), ALU.subtract).then_inc(at_ready, 1)
                dve.wait_ge(at_ready, i * 16 + (u + TWO + 1))
                dve.sem_inc(acc_free, 1)

            def expert_out(i, u):
                dve.wait_ge(acc_full, i * 32 + (OUTS["peer"] + 16 + u + 1))
                vv.scalar_tensor_tensor(hT[:, u, :], ps[:, u % BANKS, 0:T], mod1[:, 80 + u:81 + u], hT[:, u, :],
                                        ALU.mult, ALU.add).then_inc(acc_free, 1)

            with dve.Fori(0, NG) as i:
                ch.enter(i, 39)
                for u in range(32):
                    low(WP, i * (32 * PIECES) + (PIECES * u + 1), u, u % RING)
                    if u == 1:
                        dve.wait_ge(g_in, i * 16 + 16)
                    if 1 <= u <= 16:
                        gated(i, u - 1)
                    elif u > 16:
                        expert_out(i, u - 17)
                    m, slot = u // 2, (u // 2) % 2
                    if m < 4 and u % 2 == 0:
                        dve.wait_ge(a_slot[slot], i * 96 + 16 * ((96 + m) // 2 + 1))
                        ch.link(vv.tensor_tensor_reduce(junk, ada[:, slot, :], cb[:, 1, :], 1.0, 0.0, ALU.mult,
                                                        ALU.add, modt[:, 12 + m:13 + m]))
                    if m < 12 and u % 2:
                        dve.wait_ge(a_slot[slot], i * 96 + 16 * ((96 + m) // 2 + 1))
                        vv.tensor_tensor_reduce(ada[:, slot, :], ada[:, slot, :], cb[:, 0, :], 1.0, 0.0, ALU.mult,
                                                ALU.add, modt[:, m:m + 1]).then_inc(a_free, 1)
                dve.wait_ge(a_free, i * 12 + (2 + 96 + 12))
                ch.tick(vv.tensor_copy(mod2[:, bass.ds(i * 4, 4)], modt[:, 0:4]))
                ch.tick(vv.tensor_copy(mod2[:, bass.ds(i * 8 + 32, 8)], modt[:, 4:12]))
                ch.link(vv.tensor_copy(modc[:, bass.ds(i * 4, 4)], modt[:, 12:16]))
                expert_out(i, 15)
                dve.wait_ge(acc_free, i * 32 + (BANKS + OUTS["peer"] + 32))
            ch.leave(NG)
            ch.link(vv.tensor_tensor(mod2[:], mod2[:], vc("b_ada_2"), ALU.add))
            ch.link(vv.tensor_tensor(modc[:], modc[:], vc("b_ada_2")[:, 0:32], ALU.add))
            dve.sem_inc(h_ready, 1)
            norm("f1", hT, hT, vc("final_g"))
            gain_of(modc[:, 16:32], vc("norm1_w_2"))
            norm("ctx", ctxT, X2[:, :, 0:CTX], coef)
            gain_of(mod2[:, 16:32], vc("norm1_w_2"))
            norm("a2", hT, X2[:, :, CTX:], coef)

            norm("kv", ckv, ckv, vc("kv_norm_w_2"), cols=TA)
            norm("q", cq, cq, vc("q_norm_w_2"))
            for j in range(2):
                ch.tick(vv.tensor_tensor_reduce(vc(f"lambda_q{j + 1}_2"), vc(f"lambda_q{j + 1}_2"),
                                                vc(f"lambda_k{j + 1}_2"), 1.0, 0.0, ALU.mult, ALU.add,
                                                small[:, 8 + j:9 + j]))
            ch.sync()
            dve.sem_inc(max_ready, 1)
            dve.wait_ge(lam_exp, 1)
            ch.link(vv.tensor_tensor(small[:, 10:11], small[:, 9:10], small[:, 8:9], ALU.subtract))
            ch.link(vv.tensor_scalar(small[:, 10:11], small[:, 10:11], -LAMBDA_INIT, None, ALU.add))
            dve.wait_ge(acc_free, BANKS + OUTS["wo2"])
            for n in range(13):
                src, w = rope_step(n)
                m = w // T
                rope(n, 12 + n, 4 + n % 2, src, w, rope2[0][:, 0:m, :], rope2[1][:, 0:m, :],
                     both("cos2", m), both("sin2", m))

            def max2(u):
                two = 2 if u < 16 else 1
                b = 2 * (u % 2)
                dve.wait_ge(s_ready, 8 + u + 1)
                if u >= 2:
                    dve.wait_ge(p_ready, 8 + u - 1)
                m = small[:, 4 * (u % 2):4 * (u % 2) + two]
                ch.link(vv.tensor_reduce(m, ps[:, b:b + two, :], AX, ALU.max))
                vv.tensor_scalar(m, m, -(SM_DA if two == 2 else SM_MLA), None, ALU.mult).then_inc(max_ready, 1)

            def prob2(u):
                two = 2 if u < 16 else 1
                s0 = 4 * (u % 2) + 2
                dve.wait_ge(exp_ready, 8 + u + 1)
                ch.link(vv.reciprocal(small[:, s0:s0 + two], small[:, s0:s0 + two]))
                w = prob[u % 2]
                if two == 2:
                    ch.tick(vv.tensor_scalar(w[:, 1, :], w[:, 1, :], small[:, s0 + 1:s0 + 2], small[:, 10:11],
                                             ALU.mult, ALU.mult))
                    ch.sync()
                    vv.scalar_tensor_tensor(w[:, 0, :], w[:, 0, :], small[:, s0:s0 + 1], w[:, 1, :],
                                            ALU.mult, ALU.add).then_inc(p_ready, 1)
                else:
                    vv.tensor_scalar(w[:, 0, :], w[:, 0, :], small[:, s0:s0 + 1], None, ALU.mult)\
                        .then_inc(p_ready, 1)

            max2(0)
            for s in range(32):
                if s + 1 < 32:
                    max2(s + 1)
                prob2(s)
            dve.wait_ge(sub_sum, 1)
            vv.tensor_scalar(rs8.rearrange("p a b -> p (a b)"), ps[:, 0:4, :].rearrange("p a b -> p (a b)"),
                             1.0 / P, EPS, ALU.mult, ALU.add).then_inc(sub_var, 1)
            dve.wait_ge(sub_std, 1)
            ch.link(vv.reciprocal(rs8, rs8))
            ch.link(vv.tensor_scalar(small[:, 11:12], vc("subln_w_2"), 1.0 - LAMBDA_INIT, None, ALU.mult))
            vv.scalar_tensor_tensor(mix[:, 0:H2, :], mix[:, 0:H2, :], small[:, 11:12], rs8, ALU.mult, ALU.mult)\
                .then_inc(mixed, 1)
            residual("wo2", 2, mod2, 32)
            dve.wait_ge(acc_free, BANKS + OUTS["up"])
            dve.sem_inc(h_ready, 1)
            gain_of(mod2[:, 64:80], vc("norm2_w_2"))
            norm("b2", hT, X, coef)

            for k in range(KC):
                dve.wait_ge(shifted, before("b2", "shifted") + k + 1)
                vv.scalar_tensor_tensor(XL[:, k, :], X[:, k, :], mod2[:, 48 + k:49 + k], XH[:, k, :].bitcast(F32),
                                        ALU.add, ALU.subtract).then_inc(xl_ready, 1)

            for j in range(2):
                ch.tick(vv.memset(gp[j], 0.0))
            ch.sync()
            dve.sem_inc(conv_ready, TWO)
            cw = vc("conv_w_2").rearrange("p (j f) -> p j f", j=3)

            def conv(i, p):
                f = bass.ds(i * 4 + p, 1)
                g, c = gp[p % 2], gc[p % 2]
                dve.wait_ge(g_row, i * 4 + (p + 1))
                ch.link(vv.tensor_scalar(c, g[:, 1:T + 1], cw[:, 1, f], vc("conv_b_2")[:, f], ALU.mult, ALU.add))
                ch.link(vv.scalar_tensor_tensor(c, g[:, 0:T], cw[:, 0, f], c, ALU.mult, ALU.add))
                vv.scalar_tensor_tensor(c, g[:, 2:T + 2], cw[:, 2, f], c, ALU.mult, ALU.add)\
                    .then_inc(conv_ready, 1)

            def hidden(i, p):
                c, f = gc[p % 2], i * 4 + p
                o = OUTS["up"] + 2 * p + 1
                dve.wait_ge(silu_done, i * 4 + (p + 1))
                dve.wait_ge(acc_full, i * U + (o + 1))
                vv.tensor_tensor(c, c, ps[:, o % BANKS, 0:T], ALU.mult).then_inc(acc_free, 2)
                dve.wait_ge(acc_free, i * U + (BANKS + OUTS["up"] + 2 * p + 2))
                ch.link(vv.tensor_copy(HH[:, f, :], c))
                ch.link(vv.tensor_tensor(HL[:, f, :], c, HH[:, f, :].bitcast(F32), ALU.subtract))

            with dve.Fori(0, FF // 4) as i:
                ch.enter(i, 16)
                for u in range(U):
                    low(WF, i * (U * PIECES) + (SPLIT["up"] + PIECES * u + 1), u, u % RING)
                    if u % 2:
                        conv(i, u // 2)
                    elif u:
                        hidden(i, u // 2 - 1)
                hidden(i, 3)
            ch.leave(FF // 4)
            dve.sem_inc(hid_done, 1)

            def down_out(i, n):
                dve.wait_ge(acc_full, i * 4 + (OUTS["down"] + n + 1))
                c = i * 4 + n
                vv.scalar_tensor_tensor(hT[:, c, :], ps[:, (OUTS["down"] + n) % BANKS, 0:T],
                                        mod2[:, bass.ds(i * 4 + 80 + n, 1)], hT[:, c, :],
                                        ALU.mult, ALU.add).then_inc(acc_free, 1)

            with dve.Fori(0, 4) as i:
                for u in range(16):
                    low(WF, i * 48 + (SPLIT["down"] + 3 * u + 1), u, u % RING, n=11, pieces=3)
                    if u % 4 == 0 and u:
                        down_out(i, u // 4 - 1)
                down_out(i, 3)
            dve.wait_ge(acc_free, BANKS + OUTS["end"])
            dve.sem_inc(h_ready, 1)
            norm("f2", hT, hT, vc("final_w_2"))


def tiled(w):
    k, n = w.shape
    return w.reshape(k // P, P, n // P, P).transpose(2, 1, 0, 3).reshape(n // P, P, k)


def chunks(x):
    n, f = x.shape
    return x.reshape(n, f // P, P).transpose(2, 1, 0)


def columns(v):
    return v.reshape(-1, P).T


def constants():
    c = np.zeros((P, N_CONST), np.float32)

    def put(name, v):
        c[:, CONST[name][0]:CONST[name][1]] = v.reshape(P, -1)

    p = np.arange(P)
    for qb, n in ((0, P), (1, T)):
        dist = (qb * P + p)[:, None] - np.arange(n)[None, :]
        ok = np.stack([(dist >= 0) & (dist % dil == 0) & (dist // dil <= window // dil)
                       for window, dil in GROUPS], axis=1)
        put(f"mask{qb}", np.where(ok, 0.0, MASKED))
    inv = np.power(np.float32(10000.0), -np.arange(64, dtype=np.float32) / np.float32(64)).astype(np.float32)
    ang = (np.arange(T, dtype=np.float32)[None, :] * inv[p % 64][:, None]).astype(np.float32).astype(np.float64)
    put("cos1", np.cos(ang))
    put("sin1", np.sin(ang))
    perm = np.zeros((P, P))
    perm[(p + 64) % P, p] = np.where(p < 64, -1.0, 1.0)
    put("perm1", perm)
    put("ident", np.eye(P))
    put("ones", np.ones((P, P)))
    inv = np.power(np.float32(10000.0), -np.arange(16, dtype=np.float32) / np.float32(16)).astype(np.float32)
    t = np.arange(T)
    pos = np.where((p % 64 < 32)[:, None], (t // 64)[None, :], (t % 64)[None, :]).astype(np.float32)
    ang = (pos * inv[p % 16][:, None]).astype(np.float32).astype(np.float64)
    put("cos2", np.cos(ang))
    put("sin2", np.sin(ang))
    perm = np.zeros((P, P))
    low = p % 32 < 16
    perm[np.where(low, p + 16, p - 16), p] = np.where(low, -1.0, 1.0)
    put("perm2", perm)
    put("iota", np.broadcast_to(np.arange(P), (P, P)))
    count = np.stack([1.0 / np.minimum(t + 1, w) for w in POOLS])
    put("rcount", np.broadcast_to(count, (P, 4, T)).copy())
    return c


def kernel(**inputs):
    import concourse.bacc as bacc
    from concourse.bass_utils import run_bass_kernel_spmd

    a = {k: np.asarray(v) for k, v in inputs.items()}

    def spread(v):
        return np.broadcast_to(v.reshape(1, -1), (P, v.size))

    vectors = []
    for name, (lo, hi) in VEC.items():
        if name.startswith("lambda"):
            vectors.append(spread(a[name]))
        else:
            vectors.append(columns(a[name].reshape(-1)))

    rows1 = a["ada_w"][0].T.reshape(96, P, D)
    rows2 = a["w_ada_2"][0].T.reshape(96, P, D)
    order = [j for g in range(NG) for j in (*range(4 * g, 4 * g + 4), *range(32 + 8 * g, 40 + 8 * g))]

    def wide(w, n):
        t = tiled(w)
        return t.reshape(t.shape[0] // n, n, P, t.shape[2]).transpose(0, 2, 1, 3).reshape(-1, P, n * t.shape[2])

    wa, wp = wide(a["w_attn_branch"][0], 4), wide(a["w_pool_branch"][0], 4)
    w2 = a["w_in_2"][0]
    zeros = np.zeros((D, 64), np.float32)
    w2 = np.concatenate([w2[:, :3072], w2[:, 3456:3712], w2[:, 3712:], zeros, w2[:, 3072:3456]], axis=1)
    uq = a["w_uq_2"][0].reshape(384, H2, 192)
    uq_rope = np.concatenate([uq[:, :, P:], np.zeros((384, H2, 64), np.float32)], axis=2)
    uq = np.concatenate([uq[:, :, :P].reshape(384, -1), uq_rope.reshape(384, -1)], axis=1)
    ukv = a["w_ukv_2"][0].reshape(256, H2, 2, P).transpose(0, 2, 1, 3).reshape(256, 2 * D // 2)
    up = a["w_up_2"][0].reshape(D, 2, FF, P).transpose(0, 2, 1, 3).reshape(D, 2 * FF * P)
    down = tiled(a["w_down_2"][0]).reshape(KC, P, 4, 11 * P).transpose(0, 2, 1, 3).reshape(4 * KC, P, 11 * P)
    arrays = {
        "x": chunks(a["x"][0]),
        "ctx": chunks(a["ctx_2"][0]),
        "c": spread(a["c"]),
        "c_2": spread(a["c_2"]),
        "c_ctx_2": spread(a["c_ctx_2"]),
        "const": constants(),
        "vec": np.concatenate(vectors, axis=1),
        "pool_mix": a["pool_mix"][0].transpose(1, 0, 2),
        "ada": np.concatenate([rows1, rows2[order]], axis=0),
        "w_in": tiled(a["w_in"][0]),
        "w_branch": np.stack([wa, wp], axis=1).reshape(8, P, D),
        "w_out": tiled(a["w_out"][0]),
        "peer_wq": tiled(a["peer_wq"][0]),
        "keys": a["peer_keys"][0].transpose(3, 0, 1, 2).reshape(P, KC, NKEY),
        "peer_down": a["peer_down"][0].reshape(NKEY, NKEY, KC, P).transpose(1, 3, 2, 0).reshape(NKEY, P, D),
        "peer_up": a["peer_up"][0].reshape(NKEY, NG, 16, KC, P).transpose(1, 3, 0, 2, 4).reshape(NKEY, P, D),
        "w_in_2": tiled(w2),
        "w_ukv_2": wide(ukv, 8),
        "w_uq_2": wide(uq, 4),
        "w_o_2": tiled(a["w_o_2"][0]),
        "w_up_2": tiled(up),
        "w_down_2": down,
    }
    arrays = {k: np.ascontiguousarray(v) for k, v in arrays.items()}
    nc = bacc.Bacc("TRN2", target_bir_lowering=False, num_devices=1)
    A = {k: nc.dram_tensor(f"in_{k}", v.shape, F32, kind="ExternalInput").ap() for k, v in arrays.items()}
    out = nc.dram_tensor("out", (P, KC, T), F32, kind="ExternalOutput").ap()
    build_program(nc, A, out)
    r = run_bass_kernel_spmd(nc, [{f"in_{k}": v for k, v in arrays.items()}], core_ids=[0])
    return r.results[0]["out"].transpose(2, 1, 0).reshape(1, T, D)
```

```python
from contextlib import ExitStack

import numpy as np
import concourse.bass as bass
from concourse import mybir

ALU = mybir.AluOpType
ACT = mybir.ActivationFunctionType
AX = mybir.AxisListType.X
F32 = mybir.dt.float32
F32R = mybir.dt.float32r
U32 = mybir.dt.uint32

P = 128
T = 256
D = 2048
KC = D // P
EPS = 1e-6
NEG = -3.0e38
MASKED = -1.0e30

HEADS = 12
SLOTS = 4
GROUPS = ((128, 1), (512, 4), (2048, 16))
SM1 = 128 ** -0.5
POOLS = (2, 4, 8, 16)
PAD = 16
EH = 8
TOPK = 16
NKEY = 128
NG = 8
BLK = 16
NBLK = T // BLK

CTX = 256
TA = CTX + T
H2 = 8
SM_DA = 64 ** -0.5
SM_MLA = 192 ** -0.5
LAMBDA_INIT = 0.8 - 0.6
FF = 5632 // P

RING = 4
BANKS = 4
U = 8
PIECES = 4
PB = 4
OHT, OHB = 4, 4
TWO = 2

TILES = {}
_t = 0
for _name, _n in (("qk", 24), ("v", 12), ("gate", 36), ("branch", 8), ("wo", 16), ("wq", 16),
                  ("peer", 256), ("in2", 30), ("ukv", 2), ("uq", 4), ("wo2", 16), ("up", 88), ("down", 64)):
    TILES[_name] = _t
    _t += _n

OUTS = {}
_t = 0
for _name, _n in (("qk", 24), ("v", 12), ("gate", 40), ("branch", 32), ("wo", 16), ("wq", 16),
                  ("peer", 256), ("q2", 8), ("k2", 8), ("v2", 8), ("c2", 6), ("ukv", 16), ("uq", 16),
                  ("wo2", 16), ("up", 88), ("down", 16), ("end", 0)):
    OUTS[_name] = _t
    _t += _n
MIX_AFTER = 35

SPLIT, USED = {}, {}
_t = _n = 0
for _name, _tiles, _pieces, _outs in (("qk", 24, 4, 24), ("v", 12, 4, 12), ("wo", 16, 4, 16),
                                      ("wq", 16, 4, 16), ("peer", 256, 4, 256), ("q2", 8, 4, 8),
                                      ("k2", 8, 4, 8), ("v2", 8, 4, 8), ("c2", 6, 4, 6), ("wo2", 16, 4, 16),
                                      ("up", 88, 4, 88),
                                      ("down", 64, 3, 16)):
    SPLIT[_name], USED[_name] = _t, _n
    _t += _tiles * _pieces
    _n += _tiles * _pieces - _outs

CONST = {}
_t = 0
for _name, _n in (("mask0", 3 * P), ("mask1", 3 * T), ("cos1", T), ("sin1", T), ("perm1", P),
                  ("ident", P), ("cos2", T), ("sin2", T), ("perm2", P), ("iota", P), ("rcount", 4 * T), ("ones", P)):
    CONST[_name] = (_t, _t + _n)
    _t += _n
N_CONST = _t
VEC = {}
_t = 0
for _name, _n in (("ada_b", 96), ("norm1_g", 16), ("norm2_g", 16), ("final_g", 16), ("pool_scale", 4),
                  ("b_ada_2", 96), ("norm1_w_2", 16), ("q_norm_w_2", 3), ("kv_norm_w_2", 2), ("subln_w_2", 1),
                  ("norm2_w_2", 16), ("final_w_2", 16), ("conv_w_2", 3 * FF), ("conv_b_2", FF),
                  ("lambda_q1_2", 64), ("lambda_k1_2", 64), ("lambda_q2_2", 64), ("lambda_k2_2", 64)):
    VEC[_name] = (_t, _t + _n)
    _t += _n
N_VEC = _t

NORMS = (("a1", KC, T, D, True), ("b1", KC, T, D, True), ("f1", KC, T, D, False), ("ctx", KC, T, D, True),
         ("a2", KC, T, D, True), ("kv", 2, TA, 2 * P, False), ("q", 3, T, 3 * P, False),
         ("b2", KC, T, D, True), ("f2", KC, T, D, False))
NORM_AT = {n[0]: i for i, n in enumerate(NORMS)}


def before(name, what):
    ahead = NORMS[:NORM_AT[name]]
    if what == "squares":
        return sum(max(1, n[1] // 4) for n in ahead)
    if what == "scaled":
        return sum(n[1] for n in ahead)
    return sum(n[1] for n in ahead if n[4])


class Chain:

    def __init__(self, eng, sem):
        self.eng, self.sem, self.n, self.turn = eng, sem, 0, None

    def tick(self, ins):
        ins.then_inc(self.sem, 1)
        self.n += 1

    def sync(self):
        if self.turn is None:
            self.eng.wait_ge(self.sem, self.n)
        else:
            base, i, per = self.turn
            self.eng.wait_ge(self.sem, i * per + (base + self.n))

    def link(self, ins):
        self.tick(ins)
        self.sync()

    def enter(self, i, per):
        self.turn = (self.n, i, per)
        self.n = 0

    def leave(self, turns):
        base, _, per = self.turn
        assert self.n == per, (self.n, per)
        self.n, self.turn = base + per * turns, None


def build_program(nc, A, out):
    with ExitStack() as ctx:
        def sb(name, shape, dt=F32):
            return ctx.enter_context(nc.sbuf_tensor(name, shape, dt))

        def sem(name):
            return ctx.enter_context(nc.semaphore(name))

        hT = sb("hT", [P, KC, T])
        ring = sb("ring", [P, RING, D])
        const = sb("const", [P, N_CONST])
        vec = sb("vec", [P, N_VEC])
        mod1 = sb("mod1", [P, 96])
        mod2 = sb("mod2", [P, 96])
        modc = sb("modc", [P, 32])
        modt = sb("modt", [P, 16])
        coef = sb("coef", [P, KC])
        rs = sb("rs", [P, TA])
        small = sb("small", [P, 16])
        arena = sb("arena", [P, 105 * 256])
        ada = sb("ada", [P, 2, D])
        cb = sb("cb", [P, 2, D])
        arena_at = nc.lookup_mloc("arena").addr
        assert nc.lookup_mloc("ada").addr == arena_at + 105 * 1024
        assert nc.lookup_mloc("cb").addr == arena_at + 121 * 1024

        def split_room(name, kb, *shape):
            return nc.alloc_sbuf_tensor_at(name, [P, *shape], F32R, offset=arena_at + int(kb * 1024))[:]
        ps = ctx.enter_context(nc.psum_tensor("ps", [P, 8, 512], F32))
        gates_dram = nc.dram_tensor("gates_scratch", (NG, P, NBLK, 16 * BLK), F32, kind="Internal").ap()

        def room(kb, *shape, dt=F32):
            n = int(np.prod(shape))
            at = int(kb * 256)
            assert at + n <= 105 * 256, (kb, shape)
            v = arena[:, at:at + n]
            if dt is not F32:
                v = v.bitcast(dt)
            if len(shape) == 2:
                return v.rearrange("p (a b) -> p a b", a=shape[0])
            if len(shape) == 3:
                return v.rearrange("p (a b c) -> p a b c", a=shape[0], b=shape[1])
            return v

        def cst(name):
            return const[:, CONST[name][0]:CONST[name][1]]

        def vc(name):
            return vec[:, VEC[name][0]:VEC[name][1]]

        ada0 = [room(16 + 8 * j, D) for j in range(8)]
        X = room(0, KC, T)
        qk = room(16, 24, T)
        v1 = room(40, 2, HEADS * P)
        ga = room(52, KC, T)
        gb = room(68, KC, T)
        pads = [room(84 + 4.25 * j, 4, PAD + T) for j in range(3)]
        attn = room(96.75, SLOTS, T)
        pool = room(100.75, 4, T)
        cbt = cb[:, 1, :]
        rope_a = cbt[:, 0:512].rearrange("p (a b) -> p a b", a=2)
        rope_b = cbt[:, 512:1024].rearrange("p (a b) -> p a b", a=2)
        sc1 = cbt[:, 0:768].rearrange("p (a b) -> p a b", a=3)
        pt1 = cbt[:, 768:1536]
        mixw = cbt[:, 1536:2048].rearrange("p (a b) -> p a b", a=4)
        XL1, XH1 = split_room("x_low_1", 52, KC, T), split_room("x_high_1", 68, KC, T)
        W1 = split_room("w_parts_1", 84, PIECES, 2, PB * P)
        GH, GL = split_room("merged_high", 0, KC, T), split_room("merged_low", 16, KC, T)
        WO = split_room("w_parts_out", 32, PIECES, 2, PB * P)
        pq = room(56, KC, T)
        keys = room(32, KC, NKEY)
        score = room(40, 2 * KC, NKEY)
        cand = cb[:, 0, :].rearrange("p (h i) -> p h i", h=EH)
        eq = cb[:, 1, :].rearrange("p (h k j) -> p h k j", h=EH, k=TOPK)
        oh1 = [room(56 + 4 * j, OHT, P) for j in range(OHB)]
        oh2 = [room(58 + 4 * j, OHT, P) for j in range(OHB)]
        stage = [room(72 + 8 * j, P, BLK) for j in range(2)]
        topv = room(72, 2 * KC, TOPK)
        topi = room(74, 2 * KC, TOPK, dt=U32)
        topf = room(90, KC, TOPK)
        cv = room(91, EH, TOPK)
        ci = room(91.5, EH, TOPK, dt=U32)
        ca = room(92, EH, TOPK, dt=U32)
        cbi = room(92.5, EH, TOPK, dt=U32)
        caf = room(93, EH, TOPK)
        cbf = room(93.5, EH, TOPK)
        ids = room(94, 3, EH * TOPK)
        idT = room(96, 3, T)
        gsum = room(99, EH)
        XL, XH = split_room("x_low", 0, KC, T), split_room("x_high", 16, KC, T)
        ATH, ATL = split_room("at_high", 32, 16, T), split_room("at_low", 48, 16, T)
        G = room(64, NBLK, 16 * BLK)
        WP = split_room("w_parts", 80, PIECES, 2, PB * P)
        junk = ps[:, 4:8, :].rearrange("p a b -> p (a b)")
        gl = room(99.5, 2, T)
        ctxT = room(32, KC, T)
        X2 = nc.alloc_sbuf_tensor_at("x2", [P, KC, TA], F32, offset=arena_at + 81 * 1024)[:]
        X2L, X2H = split_room("x2_low", 81, KC, TA), split_room("x2_high", 49, KC, TA)
        W2 = split_room("w_parts_2", 113, PIECES, 2, PB * P)
        q2 = room(0, H2, T)
        k2 = room(8, H2, TA)
        v2 = room(24, 4, H2 * P)
        cq = room(40, 3, T)
        ckv = room(43, 2, TA)
        kr = room(47, TA)
        vm = room(49, 4, H2 * P)
        sq2 = room(65, 4, T)
        rope2 = [room(65 + 2 * j, 2, T) for j in range(2)]
        kn = room(72, H2, TA)
        qm = room(88, 2 * H2, T)
        mix = cb[:, :, :].rearrange("p a (b c) -> p (a b) c", c=T)
        adaf = ada[:, :, :].rearrange("p a b -> p (a b)")
        prob = [adaf[:, 1024 * j:1024 * j + 1024].rearrange("p (a b) -> p a b", a=2) for j in range(3)]
        wt2 = [adaf[:, 3072 + 512 * j:3584 + 512 * j] for j in range(2)]
        rs8 = room(0, H2, T)
        sq8 = room(8, H2, T)
        ML, MH = split_room("heads_low", 16, KC, T), split_room("heads_high", 32, KC, T)
        WO2 = split_room("w_parts_out_2", 0, PIECES, 2, PB * P)
        HH, HL = split_room("hidden_high", 32, FF, T), split_room("hidden_low", 92, FF, T)
        WF = split_room("w_parts_ff", 76, PIECES, 2, PB * P)
        gp = [const[:, 264 * j:264 * j + T + 2] for j in range(2)]
        gc = [const[:, 528 + T * j:528 + T * (j + 1)] for j in range(2)]

        def rope_step(n):
            if n < 4:
                return q2[:, 2 * n:2 * n + 2, :], 2 * T
            if n < 8:
                return k2[:, 2 * (n - 4):2 * (n - 4) + 2, CTX:], 2 * T
            if n < 12:
                return qm[:, H2 + 2 * (n - 8):H2 + 2 * (n - 8) + 2, :], 2 * T
            return kr[:, CTX:].unsqueeze(1), T

        def in2_tile(n):
            return ("q2", "k2", "v2", "c2")[n // 8], n % 8

        def at_free(stage_name, i, per, u, j):
            if stage_name == "down":
                n, p = u // 4, 3 * (u % 4) + j
                if p == 3:
                    return None, i * (per // 4) + (OUTS["down"] + n)
                ahead = 3 + USED["down"] + 11 * n + (p - 3 if p >= 4 else p - 2)
                return i * (11 * per // 4) + ahead, None
            if j == PIECES - 1:
                return None, i * per + (OUTS[stage_name] + u)
            return i * (3 * per) + (USED[stage_name] + 3 * u + j + 1), None

        w_slot = [sem(f"w_slot{j}") for j in range(RING)]
        acc_full = sem("acc_full")
        acc_free = sem("acc_free")
        a_slot = [sem(f"a_slot{j}") for j in range(2)]
        a_free = sem("a_free")
        x_in = sem("x_in")
        c_in = sem("c_in")
        const_in = sem("const_in")
        tables_in = sem("tables_in")
        keys_in = sem("keys_in")
        c2_in = sem("c2_in")
        ctx_in = sem("ctx_in")
        c_silu = sem("c_silu")
        a0_slot = [sem(f"a0_slot{j}") for j in range(8)]
        a0_used = sem("a0_used")
        zeroed = sem("zeroed")
        dve_done = sem("dve_done")
        act_done = sem("act_done")
        squared = sem("squared")
        summed = sem("summed")
        var_ready = sem("var_ready")
        std_ready = sem("std_ready")
        scaled = sem("scaled")
        shifted = sem("shifted")
        rotated = sem("rotated")
        roped = sem("roped")
        s_ready = sem("s_ready")
        max_ready = sem("max_ready")
        exp_ready = sem("exp_ready")
        p_ready = sem("p_ready")
        pt_ready = sem("pt_ready")
        pt_copied = sem("pt_copied")
        o_ready = sem("o_ready")
        o_copied = sem("o_copied")
        pooled = sem("pooled")
        merged = sem("merged")
        h_ready = sem("h_ready")
        score_ready = sem("score_ready")
        score_copied = sem("score_copied")
        cand_ready = sem("cand_ready")
        gate_exp = sem("gate_exp")
        ids_ready = sem("ids_ready")
        ids_turned = sem("ids_turned")
        ids_copied = sem("ids_copied")
        oh_dve = sem("oh_dve")
        oh_pool = sem("oh_pool")
        g_full = sem("g_full")
        g_copied = sem("g_copied")
        g_stored = [sem(f"g_stored{j}") for j in range(2)]
        g_in = sem("g_in")
        gelu_done = sem("gelu_done")
        at_ready = sem("at_ready")
        lam_exp = sem("lam_exp")
        sub_sq = sem("sub_sq")
        sub_sum = sem("sub_sum")
        sub_var = sem("sub_var")
        sub_std = sem("sub_std")
        mixed = sem("mixed")
        mix_high = sem("mix_high")
        mix_raw = sem("mix_raw")
        g_row = sem("g_row")
        conv_ready = sem("conv_ready")
        silu_done = sem("silu_done")
        out_done = sem("out_done")
        hi_ready = sem("hi_ready")
        lo_ready = sem("lo_ready")
        piece_used = sem("piece_used")
        xh_ready = sem("xh_ready")
        xl_ready = sem("xl_ready")
        hid_done = sem("hid_done")

        block = ctx.enter_context(nc.Block())

        @block.sync
        def _(sp):
            def load(slot, src, made, n=D, split=None):
                if made is not None:
                    sp.wait_ge(acc_full, made)
                if split is not None:
                    sp.wait_ge(lo_ready, split)
                sp.dma_start(ring[:, slot % RING, 0:n], src).then_inc(w_slot[slot % RING], 16)

            def stream(name, src, count, n=D, o_name=None):
                o = OUTS[o_name or name]
                with sp.Fori(0, count // U) as i:
                    for u in range(U):
                        load(u, src[i * U + u], i * U + (o + u + 1 - RING), n)

            sp.dma_start(cb[:, 0, :], A["c"]).then_inc(c_in, 16)
            for t in range(32):
                if t >= 8:
                    sp.wait_ge(a0_used, t - 7)
                sp.dma_start(ada0[t % 8], A["ada"][t]).then_inc(a0_slot[t % 8], 16)
                if t == 8:
                    sp.dma_start(hT[:], A["x"]).then_inc(x_in, 16)
                if t == 16:
                    sp.dma_start(cst("ones"), A["const"][:, CONST["ones"][0]:]).then_inc(const_in, 16)
                    sp.dma_start(vec[:], A["vec"]).then_inc(const_in, 16)
            for u in range(RING):
                load(u, A["w_in"][u], None)
            sp.dma_start(const[:, 0:CONST["ones"][0]], A["const"][:, 0:CONST["ones"][0]]).then_inc(tables_in, 16)
            sp.dma_start(mixw, A["pool_mix"]).then_inc(tables_in, 16)
            with sp.Fori(0, 36 // RING) as i:
                for u in range(RING):
                    load(u, A["w_in"][i * RING + (RING + u)], None, split=i * (RING * PIECES) + (16 + PIECES * (u + 1)))
            with sp.Fori(0, 36 // RING - 1) as i:
                for u in range(RING):
                    load(u, A["w_in"][i * RING + (36 + RING + u)], i * RING + (36 + u + 1))
            for t in range(8):
                load(t, A["w_branch"][t], 72 - RING + t + 1 if t < RING else OUTS["branch"] + 4 * (t - RING + 1))
            for name, src in (("wo", A["w_out"]), ("wq", A["peer_wq"])):
                for t in range(16):
                    if name == "wo" and t < RING:
                        load(t, src[t], OUTS["branch"] + 4 * (t + RING + 1))
                    else:
                        load(t, src[t], None, split=16 + SPLIT[name] + PIECES * (t + 1 - RING))
            with sp.Fori(0, NG) as i:
                for u in range(32):
                    src = A["peer_down"] if u < 16 else A["peer_up"]
                    load(u, src[i * 16 + u % 16], None,
                         split=i * (32 * PIECES) + (16 + SPLIT["peer"] + PIECES * (u + 1 - RING)))
            with sp.Fori(0, 3) as i:
                for u in range(U):
                    load(u, A["w_in_2"][i * U + u], None,
                         split=i * (U * PIECES) + (16 + SPLIT["q2"] + PIECES * (u + 1 - RING)))
            for u in range(24, 30):
                load(u, A["w_in_2"][u], None, split=16 + SPLIT["q2"] + PIECES * (u + 1 - RING))
            for t in range(2):
                load(TILES["ukv"] + t, A["w_ukv_2"][t], None, split=16 + SPLIT["q2"] + PIECES * (30 + t + 1 - RING))
            for t in range(4):
                load(TILES["uq"] + t, A["w_uq_2"][t], OUTS["ukv"] if t < 2 else OUTS["ukv"] + 8 * (t - 1), 12 * P)
            for t in range(16):
                if t < RING:
                    load(TILES["wo2"] + t, A["w_o_2"][t], OUTS["uq"] + 4 * (t + 1))
                else:
                    load(TILES["wo2"] + t, A["w_o_2"][t], None, split=16 + SPLIT["wo2"] + PIECES * (t + 1 - RING))
            for u in range(RING):
                load(u, A["w_up_2"][u], None, split=16 + SPLIT["up"] + PIECES * (u + 1 - RING))
            with sp.Fori(0, 88 // RING - 1) as i:
                for u in range(RING):
                    load(u, A["w_up_2"][i * RING + (RING + u)], None,
                         split=i * (RING * PIECES) + (16 + SPLIT["up"] + PIECES * (u + 1)))
            for u in range(RING):
                load(u, A["w_down_2"][u], None, 11 * P, split=16 + SPLIT["down"] - PIECES * (RING - 1 - u))
            with sp.Fori(0, KC - 1) as i:
                for u in range(RING):
                    load(u, A["w_down_2"][i * 4 + (4 + u)], None, 11 * P,
                         split=i * 12 + (16 + SPLIT["down"] + 3 * (u + 1)))
            sp.wait_ge(scaled, before("f2", "scaled") + KC)
            sp.dma_start(out, hT[:]).then_inc(out_done, 16)
            sp.wait_ge(out_done, 16)

        @block.gpsimd
        def _(pool_e):
            def ada_load(tile, slot, src):
                pool_e.wait_ge(a_free, tile + 1)
                pool_e.dma_start(ada[:, slot, :], src).then_inc(a_slot[slot], 16)

            pool_e.wait_ge(a0_used, 24)
            with pool_e.Fori(0, 32) as i:
                for u in range(2):
                    ada_load(i * 2 + u, u, A["ada"][i * 2 + (32 + u)])
            pool_e.wait_ge(acc_full, OUTS["wq"])
            pool_e.dma_start(keys, A["keys"]).then_inc(keys_in, 16)
            with pool_e.Fori(0, NBLK) as i:
                for j in range(OHB):
                    pool_e.wait_ge(oh_dve, i * OHB + (j + 1))
                    tok = bass.ds(i * 16 + OHT * j, OHT)
                    nc.gpsimd.tensor_tensor(
                        oh2[j], oh2[j], idT[:, 2, tok].unsqueeze(2).broadcast_to([P, OHT, P]), ALU.mult,
                    ).then_inc(oh_pool, 1)
            pool_e.wait_ge(ids_ready, 2)
            pool_e.dma_start(cb[:, 0, :], A["c_2"]).then_inc(c2_in, 16)
            pool_e.dma_start(cb[:, 1, :], A["c_ctx_2"]).then_inc(c2_in, 16)
            pool_e.wait_ge(g_full, OHB + OHB * NBLK)
            pool_e.wait_ge(g_copied, OHB + OHB * NBLK)
            pool_e.wait_ge(g_stored[0], 16 + 16 * NBLK // 2)
            pool_e.wait_ge(g_stored[1], 16 + 16 * NBLK // 2)
            with pool_e.Fori(0, NG) as i:
                pool_e.wait_ge(at_ready, i * 16 + TWO)
                pool_e.dma_start(G, gates_dram[i]).then_inc(g_in, 16)
                for u in range(12):
                    ada_load(i * 12 + (64 + u), u % 2, A["ada"][i * 12 + (96 + u)])
            pool_e.wait_ge(h_ready, 2)
            pool_e.dma_start(ctxT, A["ctx"]).then_inc(ctx_in, 16)

        @block.scalar
        def _(act):
            ch = Chain(act, act_done)

            def act_fn(*a, **k):
                return nc.scalar.activation(*a, **k)

            def norm(name, src, sqd, dst, shift=None, cols=T, high_to=None, also_high=None):
                i, n = NORM_AT[name], NORMS[NORM_AT[name]][1]
                for b in range(max(1, n // 4)):
                    w = min(4, n)
                    act_fn(sqd[:, 4 * b:4 * b + w, :], src[:, 4 * b:4 * b + w, :], ACT.Square).then_inc(squared, 1)
                act.wait_ge(var_ready, i + 1)
                act_fn(rs[:, 0:cols], rs[:, 0:cols], ACT.Sqrt).then_inc(std_ready, 1)
                if shift is not None:
                    for k in range(n):
                        act.wait_ge(scaled, before(name, "scaled") + k + 1)
                        act_fn(dst[:, k, :] if high_to is None else high_to[:, k, :], dst[:, k, :], ACT.Identity,
                               bias=shift[:, k:k + 1]).then_inc(shifted, 1)
                if also_high is not None:
                    act.wait_ge(shifted, before(name, "shifted") + n)
                    for b in range(4):
                        act_fn(also_high[:, 4 * b:4 * b + 4, :], dst[:, 4 * b:4 * b + 4, :], ACT.Copy)\
                            .then_inc(xh_ready, 1)

            def high(parts, stage_name, i, per, u, slot, n=PIECES * PB, at=0, pieces=PIECES):
                for j in range(pieces):
                    w = min(PB, n - PB * j) * P
                    used, full = at_free(stage_name, i, per, u, j)
                    if full is None:
                        act.wait_ge(piece_used, used)
                    else:
                        act.wait_ge(acc_full, full)
                    m = (pieces * u + j) % PIECES
                    act_fn(parts[:, m, 0, 0:w], ring[:, slot, j * PB * P:j * PB * P + w], ACT.Copy)\
                        .then_inc(hi_ready, 1)

            def tile_in(name, i, per, u):
                act.wait_ge(w_slot[u % RING], i * (16 * per // RING) + 16 * ((TILES[name] + u) // RING + 1))

            act.wait_ge(c_in, 16)
            act_fn(cb[:, 0, :], cb[:, 0, :], ACT.Silu).then_inc(c_silu, 1)
            act.wait_ge(x_in, 16)
            norm("a1", hT, X, X, mod1[:, 0:KC], also_high=XH1)

            def qk_out(i, u):
                act.wait_ge(acc_full, i * U + (u + 1))
                act_fn(qk[:, i * U + u, :], ps[:, u % BANKS, 0:T], ACT.Copy).then_inc(acc_free, 1)

            with act.Fori(0, 24 // U) as i:
                for u in range(U):
                    tile_in("qk", i, U, u)
                    high(W1, "qk", i, U, u, u % RING)
                    if u:
                        qk_out(i, u - 1)
                qk_out(i, U - 1)

            def v_out(m):
                o = OUTS["v"] + 2 * m + 1
                act.wait_ge(acc_full, o + 1)
                act_fn(v1[:, :, m * T:(m + 1) * T], ps[:, o % BANKS, :].rearrange("p (a b) -> p a b", a=2),
                       ACT.Copy).then_inc(acc_free, 2)

            for n in range(HEADS):
                tile_in("v", 0, 0, n)
                high(W1, "v", 0, 0, n, n % RING)
                if n % 2 == 0 and n:
                    v_out(n // 2 - 1)
            v_out(HEADS // 2 - 1)

            act.wait_ge(zeroed, 1)
            act.wait_ge(const_in, 32)
            for k in range(36):
                o = OUTS["gate"] + k + (4 if k > MIX_AFTER else 0)
                act.wait_ge(acc_full, o + 1)
                if k < 4:
                    act_fn(pads[0][:, k, PAD:], ps[:, o % BANKS, 0:T], ACT.Copy).then_inc(acc_free, 1)
                else:
                    to = ga[:, k - 4, :] if k < 20 else gb[:, k - 20, :]
                    act_fn(to, ps[:, o % BANKS, 0:T], ACT.Sigmoid).then_inc(acc_free, 1)
                if k == MIX_AFTER:
                    for g in range(4):
                        o = OUTS["gate"] + MIX_AFTER + 1 + g
                        act.wait_ge(acc_full, o + 1)
                        act_fn(pool[:, g, :], ps[:, o % BANKS, 0:T], ACT.Copy,
                               scale=vc("pool_scale")[:, g:g + 1]).then_inc(acc_free, 1)
                u = (k - 1) // 4
                if k % 4 == 1 and u < 8:
                    act.wait_ge(max_ready, u + 1)
                    s = sc1[:, :, 0:P * (u % 2 + 1)]
                    act_fn(s, s, ACT.Exp, bias=small[:, 0:1], accum_out=small[:, 1:2]).then_inc(exp_ready, 1)
                if k % 4 == 2 and u < 8:
                    w = 3 * P * (u % 2 + 1)
                    act.wait_ge(pt_ready, u + 1)
                    if u:
                        act.wait_ge(o_ready, u)
                    act_fn(pt1[:, 0:w], ps[:, 6:8, :].rearrange("p a b -> p (a b)")[:, 0:w], ACT.Copy)\
                        .then_inc(pt_copied, 1)
                if k % 4 == 0 and k:
                    u = k // 4 - 1
                    act.wait_ge(o_ready, u + 1)
                    act_fn(attn[:, u // 2, (u % 2) * P:(u % 2 + 1) * P], ps[:, 7, 256:384], ACT.Copy)\
                        .then_inc(o_copied, 1)

            for b in range(4):
                act.wait_ge(merged, b + 1)
                act_fn(GH[:, 4 * b:4 * b + 4, :], ga[:, 4 * b:4 * b + 4, :], ACT.Copy).then_inc(xh_ready, 1)
            for n in range(16):
                tile_in("wo", 0, 0, n)
                high(WO, "wo", 0, 0, n, n % RING)
            act.wait_ge(h_ready, 1)
            norm("b1", hT, X, X, mod1[:, 48:64], high_to=XH)

            def score_out(h):
                act.wait_ge(score_ready, h + 1)
                act_fn(score.rearrange("p (t c) k -> p t c k", t=2)[:, :, 2 * h:2 * h + 2, :],
                       ps[:, 4 + h % 2, :].rearrange("p (t c k) -> p t c k", t=2, c=2), ACT.Copy)\
                    .then_inc(score_copied, 1)

            for n in range(17):
                if n < 16:
                    tile_in("wq", 0, 0, n)
                    high(WP, "wq", 0, 0, n, n % RING)
                if n:
                    o = OUTS["wq"] + n - 1
                    act.wait_ge(acc_full, o + 1)
                    act_fn(pq[:, n - 1, :], ps[:, o % BANKS, 0:T], ACT.Copy).then_inc(acc_free, 1)
                if n % 2 and n >= 3:
                    score_out((n - 3) // 2)
            score_out(EH - 1)
            for tb in range(2):
                act.wait_ge(cand_ready, tb + 1)
                act_fn(ids[:, 2, :].rearrange("p (h k) -> p h k", h=EH), cv, ACT.Exp).then_inc(gate_exp, 1)
                act.wait_ge(ids_turned, tb + 1)
                act_fn(idT[:, :, tb * P:(tb + 1) * P], ps[:, 4, 0:3 * P].rearrange("p (a b) -> p a b", a=3),
                       ACT.Copy).then_inc(ids_copied, 1)
            with act.Fori(0, NBLK // 2) as i:
                for j in range(2):
                    act.wait_ge(g_stored[j], i * 16 + 16)
                    for q in range(OHB):
                        act.wait_ge(g_full, i * (2 * OHB) + (OHB + OHB * j + q + 1))
                        act_fn(stage[j][:, :, OHT * q:OHT * q + OHT],
                               ps[:, 4 + q, :].rearrange("p (t c) -> p c t", t=OHT), ACT.Copy).then_inc(g_copied, 1)
                    act.wait_ge(g_copied, i * (2 * OHB) + (OHB + OHB * (j + 1)))
                    act.dma_start(gates_dram[:, :, i * 2 + j, :].rearrange("g p f -> p g f"),
                                  stage[j].rearrange("p (g c) t -> p g (c t)", g=NG)).then_inc(g_stored[j], 16)
            act.wait_ge(c2_in, 32)
            act_fn(cb[:, 0, :], cb[:, 0, :], ACT.Silu).then_inc(c_silu, 1)
            act_fn(cb[:, 1, :], cb[:, 1, :], ACT.Silu).then_inc(c_silu, 1)
            act.wait_ge(g_stored[0], 16 + 16 * NBLK // 2)
            act.wait_ge(g_stored[1], 16 + 16 * NBLK // 2)

            def gelu(i, u):
                act.wait_ge(acc_full, i * 32 + (OUTS["peer"] + u + 1))
                act.wait_ge(at_ready, i * 16 + (u + TWO - 1))
                act_fn(gl[:, u % 2, :], ps[:, u % BANKS, 0:T], ACT.Gelu).then_inc(gelu_done, 1)

            def peer_turn(i, last=False):
                for u in range(1, 33):
                    if u < 32 or not last:
                        tile_in("peer", i, 32, u)
                        high(WP, "peer", i, 32, u, u % RING)
                    if u <= 16:
                        gelu(i, u - 1)

            tile_in("peer", 0, 32, 0)
            high(WP, "peer", 0, 32, 0, 0)
            with act.Fori(0, NG - 1) as i:
                peer_turn(i)
            peer_turn(NG - 1, last=True)

            act.wait_ge(h_ready, 2)
            norm("f1", hT, X, None)
            act.wait_ge(ctx_in, 16)
            norm("ctx", ctxT, X2[:, :, 0:CTX], X2[:, :, 0:CTX], modc[:, 0:KC], high_to=X2H[:, :, 0:CTX])
            act.wait_ge(scaled, before("f1", "scaled") + KC)
            norm("a2", hT, X2[:, :, CTX:], X2[:, :, CTX:], mod2[:, 0:KC], high_to=X2H[:, :, CTX:])

            def out_copy(o, to, n=T):
                act.wait_ge(acc_full, o + 1)
                src = ps[:, o % BANKS, 0:n]
                if len(to.shape) == 3:
                    src = src.rearrange("p (a b) -> p a b", a=to.shape[1])
                return act_fn(to, src, ACT.Copy)

            for n in range(31):
                if n < 30:
                    name, u = in2_tile(n)
                    tile_in("in2", 0, 0, n)
                    high(W2, name, 0, 0, u, n % RING)
                if not n:
                    continue
                name, u = in2_tile(n - 1)
                bank_at = (OUTS[name] + u) % BANKS
                if name == "q2":
                    out_copy(OUTS[name] + u, q2[:, u, :]).then_inc(acc_free, 1)
                elif name == "k2":
                    out_copy(OUTS[name] + u, k2[:, u, :], TA).then_inc(acc_free, 1)
                elif name == "c2":
                    to = ckv[:, u, :] if u < 2 else kr if u == 2 else cq[:, u - 3, :]
                    out_copy(OUTS[name] + u, to, TA if u < 3 else T).then_inc(acc_free, 1)
                elif u % 2:
                    act.wait_ge(acc_full, OUTS[name] + u + 1)
                    act_fn(v2[:, :, (u // 2) * T:(u // 2 + 1) * T],
                           ps[:, bank_at - 1:bank_at + 1, :].rearrange("p a (b c) -> p (a b) c", c=T), ACT.Copy)\
                        .then_inc(acc_free, 2)
            act.wait_ge(acc_free, BANKS + OUTS["ukv"])
            norm("kv", ckv, kn[:, 0:2, :], None, cols=TA)
            norm("q", cq, sq2[:, 0:3, :], None)
            for n in range(16):
                to = kn[:, n, :] if n < 8 else vm[:, :, (n - 8) * P:(n - 7) * P]
                out_copy(OUTS["ukv"] + n, to, TA).then_inc(acc_free, 1)
            for n in range(16):
                out_copy(OUTS["uq"] + n, qm[:, n, :], T).then_inc(acc_free, 1)
            act.wait_ge(max_ready, 8 + 1)
            act_fn(small[:, 12:14], small[:, 12:14], ACT.Exp).then_inc(lam_exp, 1)

            def stage_exp(u):
                two = u < 16
                act.wait_ge(max_ready, 8 + 1 + u + 1)
                for j in range(2 if two else 1):
                    c = 4 * (u % 3) + j
                    ins = act_fn(prob[u % 3][:, j, :], ps[:, 2 * (u % 3) + j, :], ACT.Exp,
                                 bias=small[:, c:c + 1], scale=SM_DA if two else SM_MLA,
                                 accum_out=small[:, c + 2:c + 3])
                ins.then_inc(exp_ready, 1)

            def stage_turn(u):
                act.wait_ge(pt_ready, 8 + u + 1)
                if u >= 2:
                    act.wait_ge(o_ready, 8 + u - 1)
                act_fn(wt2[u % 2], ps[:, 6, :], ACT.Copy).then_inc(pt_copied, 1)

            def stage_out(u):
                head, qb = u // 2, u % 2
                act.wait_ge(o_ready, 8 + u + 1)
                cols, src = slice(qb * P, (qb + 1) * P), ps[:, 7, (u % 2) * P:(u % 2 + 1) * P]
                if u >= 16:
                    act_fn(mix[:, head, cols], src, ACT.Copy).then_inc(mix_raw, 1)
                    act_fn(MH[:, head, cols], src, ACT.Copy).then_inc(o_copied, 1)
                else:
                    act_fn(mix[:, head, cols], src, ACT.Copy).then_inc(o_copied, 1)

            stage_exp(0)
            for s in range(32 + 1):
                if s + 1 < 32:
                    stage_exp(s + 1)
                if s < 32:
                    stage_turn(s)
                if s >= 1:
                    stage_out(s - 1)
                if s in (17, 18):
                    four = slice(4 * (s - 17), 4 * (s - 17) + 4)
                    act.wait_ge(o_copied, 8 + 16)
                    act_fn(sq8[:, four, :], mix[:, four, :], ACT.Square).then_inc(sub_sq, 1)
                if s == 23:
                    act.wait_ge(sub_var, 2)
                    act_fn(rs8, rs8, ACT.Sqrt).then_inc(sub_std, 1)
                if s in (28, 29):
                    four = slice(4 * (s - 28), 4 * (s - 28) + 4)
                    act.wait_ge(mixed, s - 27)
                    act_fn(MH[:, four, :], mix[:, four, :], ACT.Copy).then_inc(mix_high, 1)
                if s == 30:
                    tile_in("wo2", 0, 0, 0)
                    high(WO2, "wo2", 0, 0, 0, 0)
            for n in range(1, 16):
                tile_in("wo2", 0, 0, n)
                high(WO2, "wo2", 0, 0, n, n % RING)

            act.wait_ge(h_ready, 3)
            norm("b2", hT, X, X, mod2[:, 48:64], high_to=XH)

            def gate_row(i, p):
                act.wait_ge(acc_full, i * U + (OUTS["up"] + 2 * p + 1))
                act.wait_ge(conv_ready, i * 4 + (p + TWO - 1))
                act_fn(gp[p % 2][:, 1:T + 1], ps[:, (OUTS["up"] + 2 * p) % BANKS, 0:T], ACT.Copy)\
                    .then_inc(g_row, 1)

            def gate_silu(i, p):
                act.wait_ge(conv_ready, i * 4 + (p + TWO + 1))
                act_fn(gc[p % 2], gc[p % 2], ACT.Silu).then_inc(silu_done, 1)

            def up_turn(i, last=False):
                for u in range(1, U + 1):
                    if u < U or not last:
                        tile_in("up", i, U, u)
                        high(WF, "up", i, U, u, u % RING)
                    if u % 2:
                        gate_row(i, u // 2)
                    else:
                        gate_silu(i, u // 2 - 1)

            tile_in("up", 0, U, 0)
            high(WF, "up", 0, U, 0, 0)
            with act.Fori(0, FF // 4 - 1) as i:
                up_turn(i)
            up_turn(FF // 4 - 1, last=True)
            with act.Fori(0, 4) as i:
                for u in range(16):
                    act.wait_ge(w_slot[u % RING], i * (16 * 16 // RING) + 16 * ((TILES["down"] + u) // RING + 1))
                    high(WF, "down", i, 16, u, u % RING, n=11, pieces=3)
            act.wait_ge(h_ready, 4)
            norm("f2", hT, X, None)

        @block.tensor
        def _(pe):
            mm = nc.tensor.matmul
            ones, ident = cst("ones"), cst("ident")

            def bank(o):
                pe.wait_ge(acc_free, o + 1)

            def norm_sum(name, sqd, n, cols=T):
                for k in range(n):
                    if k % 4 == 0:
                        pe.wait_ge(squared, before(name, "squares") + k // 4 + 1)
                    ins = mm(ps[:, 4, 0:cols], ones, sqd[:, k, :], start=(k == 0), stop=(k == n - 1))
                ins.then_inc(summed, 1)

            def blocks(to, slot, n, moving, at=0):
                for k in range(n):
                    ins = mm(to, ring[:, slot % RING, (at + k) * P:(at + k + 1) * P], moving(k),
                             start=(k == 0), stop=(k == n - 1))
                return ins

            def one(tile, o, emit):
                pe.wait_ge(w_slot[tile % RING], 16 * (tile // RING + 1))
                bank(o)
                emit(tile % RING, o % BANKS)

            def tokens_first(slot, b, src, n, tbs, at=0):
                for tb in range(tbs):
                    for k in range(n):
                        ins = mm(ps[:, b, tb * P:(tb + 1) * P], src[:, k, tb * P:(tb + 1) * P],
                                 ring[:, slot, (at + k) * P:(at + k + 1) * P], start=(k == 0), stop=(k == n - 1))
                return ins

            def piece(to, parts, m, wait, first, n, high, low, k_all):
                pe.wait_ge(lo_ready, wait)
                for b in range(n):
                    k = first + b
                    w_high, w_low = (parts[:, m, h, b * P:(b + 1) * P] for h in range(2))
                    mm(to, w_high, high(k), start=(k == 0), stop=False)
                    mm(to, w_high, low(k), start=False, stop=False)
                    ins = mm(to, w_low, high(k), start=False, stop=(k == k_all - 1))
                return ins

            def split_tile(name, i, per, u, to, parts, high, low):
                for j in range(PIECES):
                    ins = piece(to, parts, j, i * (per * PIECES) + (16 + SPLIT[name] + PIECES * u + j + 1),
                                PB * j, PB, high, low, KC)
                    ins.then_inc(piece_used if j < PIECES - 1 else acc_full, 1)

            def split_loop(name, parts, high, low):
                with pe.Fori(0, 16 // U) as i:
                    for u in range(U):
                        pe.wait_ge(acc_free, i * U + (OUTS[name] + u + 1))
                        split_tile(name, i, U, u, ps[:, (OUTS[name] + u) % BANKS, 0:T], parts,
                                   lambda k: high[:, k, :], lambda k: low[:, k, :])

            def split_values(name, i, per, m, bank_of, parts, high, low, tbs):
                for t in range(2):
                    u = 2 * m + t
                    for j in range(PIECES):
                        pe.wait_ge(lo_ready, i * (per * PIECES) + (16 + SPLIT[name] + PIECES * u + j + 1))
                        for tb in range(tbs):
                            to, tok = bank_of(tb), slice(tb * P, (tb + 1) * P)
                            for b in range(2):
                                k = 8 * t + 2 * j + b
                                w_high, w_low = (parts[:, j, h, b * 2 * P:(b + 1) * 2 * P] for h in range(2))
                                mm(to, high[:, k, tok], w_high, start=(k == 0 and tb % 2 == 0), stop=False,
                                   skip_group_check=True)
                                mm(to, low[:, k, tok], w_high, start=False, stop=False, skip_group_check=True)
                                ins = mm(to, high[:, k, tok], w_low, start=False, stop=(k == KC - 1),
                                         skip_group_check=True)
                        ins.then_inc(piece_used if j < PIECES - 1 else acc_full, 1)

            pe.wait_ge(const_in, 32)
            norm_sum("a1", X, KC)
            pe.wait_ge(xl_ready, 4)
            with pe.Fori(0, 24 // U) as i:
                for u in range(U):
                    pe.wait_ge(acc_free, i * U + (u + 1))
                    split_tile("qk", i, U, u, ps[:, u % BANKS, 0:T], W1, lambda k: XH1[:, k, :],
                               lambda k: XL1[:, k, :])
            pe.wait_ge(acc_free, BANKS + OUTS["v"])
            pe.wait_ge(tables_in, 32)
            for m in range(HEADS // 2):
                bank(OUTS["v"] + 2 * m + 1)
                split_values("v", 0, 0, m, lambda tb: ps[:, (OUTS["v"] + 2 * m + 1) % BANKS, tb * T:(tb + 1) * T],
                             W1, XH1, XL1, 2)
                for n in (2 * m, 2 * m + 1):
                    if n >= 2:
                        pe.wait_ge(roped, n - 1)
                    mm(ps[:, 4 + n % 2, :], cst("perm1"), qk[:, 2 * n:2 * n + 2, :], start=True, stop=True)\
                        .then_inc(rotated, 1)

            def s1(u):
                hs, qb = u // 2, u % 2
                if u == 0:
                    pe.wait_ge(roped, 12)
                else:
                    pe.wait_ge(max_ready, u)
                nk = P * (qb + 1)
                for g in range(3):
                    h = g * SLOTS + hs
                    ins = mm(ps[:, 4 + g // 2, (g % 2) * T:(g % 2) * T + nk], qk[:, h, qb * P:(qb + 1) * P],
                             qk[:, HEADS + h, 0:nk], start=True, stop=True)
                ins.then_inc(s_ready, 1)

            def t1(u):
                pe.wait_ge(p_ready, u + 1)
                if u:
                    pe.wait_ge(pt_copied, u)
                    pe.wait_ge(o_copied, u)
                nb = u % 2 + 1
                for g in range(3):
                    for kb in range(nb):
                        n = g * nb + kb
                        ins = nc.tensor.transpose(ps[:, 6 + n // 4, (n % 4) * P:(n % 4 + 1) * P],
                                                  sc1[:, g, kb * P:(kb + 1) * P], ident)
                ins.then_inc(pt_ready, 1)

            def y1(u):
                hs, nb = u // 2, u % 2 + 1
                pe.wait_ge(pt_copied, u + 1)
                for g in range(3):
                    h = g * SLOTS + hs
                    for kb in range(nb):
                        n = g * nb + kb
                        ins = mm(ps[:, 7, 256:384], v1[:, kb, h * P:(h + 1) * P], pt1[:, n * P:(n + 1) * P],
                                 start=(n == 0), stop=(n == 3 * nb - 1))
                ins.then_inc(o_ready, 1)

            for k in range(36):
                o = OUTS["gate"] + k + (4 if k > MIX_AFTER else 0)
                one(TILES["gate"] + k, o,
                    lambda s, b: blocks(ps[:, b, 0:T], s, KC, lambda c: X[:, c, :]).then_inc(acc_full, 1))
                if k == MIX_AFTER:
                    pe.wait_ge(pooled, 1)
                    for g in range(4):
                        o = OUTS["gate"] + MIX_AFTER + 1 + g
                        bank(o)
                        mm(ps[:, o % BANKS, 0:T], mixw[:, g, :], pads[2][:, g, PAD:], start=True, stop=True)\
                            .then_inc(acc_full, 1)
                u = k // 4
                if u < 8:
                    if k % 4 == 0:
                        s1(u)
                    if k % 4 == 2:
                        t1(u)
                    if k % 4 == 3:
                        y1(u)
            pe.wait_ge(acc_free, BANKS + OUTS["branch"])
            pe.wait_ge(o_copied, 8)
            for t in range(8):
                src = attn if t % 2 == 0 else pool
                pe.wait_ge(w_slot[t % RING], 16 * ((TILES["branch"] + t) // RING + 1))
                for n in range(4):
                    o = OUTS["branch"] + 4 * t + n
                    bank(o)
                    blocks(ps[:, o % BANKS, 0:T], t, 4, lambda c: src[:, c, :], at=4 * n).then_inc(acc_full, 1)
            pe.wait_ge(merged, 4)
            pe.wait_ge(xl_ready, 4 + 4)
            split_loop("wo", WO, GH, GL)
            norm_sum("b1", X, KC)
            pe.wait_ge(xl_ready, 8 + KC)

            def keys_of(h):
                pe.wait_ge(acc_free, BANKS + OUTS["wq"] + 2 * h + 2)
                if h >= 2:
                    pe.wait_ge(score_copied, h - 1)
                for tb in range(2):
                    for j in range(2):
                        c = 2 * h + j
                        ins = mm(ps[:, 4 + h % 2, (2 * tb + j) * P:(2 * tb + j + 1) * P],
                                 pq[:, c, tb * P:(tb + 1) * P], keys[:, c, :], start=True, stop=True)
                ins.then_inc(score_ready, 1)

            pe.wait_ge(keys_in, 16)
            for n in range(16):
                o = OUTS["wq"] + n
                bank(o)
                split_tile("wq", 0, 0, n, ps[:, o % BANKS, 0:T], WP, lambda k: XH[:, k, :], lambda k: XL[:, k, :])
                if n % 2 == 0 and n:
                    keys_of(n // 2 - 1)
            keys_of(EH - 1)
            for tb in range(2):
                pe.wait_ge(ids_ready, tb + 1)
                if tb:
                    pe.wait_ge(ids_copied, tb)
                for j in range(3):
                    ins = nc.tensor.transpose(ps[:, 4, j * P:(j + 1) * P], ids[:, j, :], ident)
                ins.then_inc(ids_turned, 1)
            pe.wait_ge(ids_copied, 2)
            with pe.Fori(0, NBLK) as i:
                for j in range(OHB):
                    pe.wait_ge(oh_pool, i * OHB + (j + 1))
                    pe.wait_ge(g_copied, i * OHB + (j + 1))
                    for q in range(OHT):
                        ins = mm(ps[:, 4 + j, q * P:(q + 1) * P], oh1[j][:, q, :], oh2[j][:, q, :],
                                 start=True, stop=True)
                    ins.then_inc(g_full, 1)
            with pe.Fori(0, NG) as i:
                for u in range(32):
                    pe.wait_ge(acc_free, i * 32 + (OUTS["peer"] + u + 1))
                    xh, xl = (XH, XL) if u < 16 else (ATH, ATL)
                    for j in range(PIECES):
                        if u == 16:
                            pe.wait_ge(at_ready, i * 16 + (PB * (j + 1) + TWO))
                        ins = piece(ps[:, u % BANKS, 0:T], WP, j,
                                    i * (32 * PIECES) + (16 + SPLIT["peer"] + PIECES * u + j + 1),
                                    PB * j, PB, lambda k: xh[:, k, :], lambda k: xl[:, k, :], KC)
                        ins.then_inc(piece_used if j < PIECES - 1 else acc_full, 1)

            norm_sum("f1", X, KC)
            pe.wait_ge(var_ready, NORM_AT["f1"] + 1)
            norm_sum("ctx", X2[:, :, 0:CTX], KC)
            pe.wait_ge(var_ready, NORM_AT["ctx"] + 1)
            norm_sum("a2", X2[:, :, CTX:], KC)
            pe.wait_ge(xl_ready, 8 + 3 * KC)

            def loop_in2(name, turn):
                with pe.Fori(0, 2) as i:
                    for u in range(4):
                        pe.wait_ge(acc_free, i * 4 + (OUTS[name] + u + 1))
                        turn(i, u)

            loop_in2("q2", lambda i, u: split_tile("q2", i, 4, u, ps[:, u, 0:T], W2, lambda k: X2H[:, k, CTX:],
                                                   lambda k: X2L[:, k, CTX:]))
            loop_in2("k2", lambda i, u: split_tile("k2", i, 4, u, ps[:, u, :], W2, lambda k: X2H[:, k, :],
                                                   lambda k: X2L[:, k, :]))
            with pe.Fori(0, 2) as i:
                for m in range(2):
                    pe.wait_ge(acc_free, i * 4 + (OUTS["v2"] + 2 * m + 2))
                    split_values("v2", i, 4, m, lambda tb: ps[:, 2 * m + tb // 2, (tb % 2) * T:(tb % 2 + 1) * T],
                                 W2, X2H, X2L, 4)
            for n in range(6):
                o, lo = OUTS["c2"] + n, 0 if n < 3 else CTX
                bank(o)
                split_tile("c2", 0, 0, n, ps[:, o % BANKS, 0:TA - lo], W2, lambda k: X2H[:, k, lo:],
                           lambda k: X2L[:, k, lo:])
            norm_sum("kv", kn[:, 0:2, :], 2, TA)
            pe.wait_ge(var_ready, NORM_AT["kv"] + 1)
            norm_sum("q", sq2, 3)
            pe.wait_ge(scaled, before("q", "scaled"))
            for t in range(2):
                tile = TILES["ukv"] + t
                pe.wait_ge(w_slot[tile % RING], 16 * (tile // RING + 1))
                for n in range(8):
                    o = OUTS["ukv"] + 8 * t + n
                    bank(o)
                    if t == 0:
                        ins = blocks(ps[:, o % BANKS, :], tile, 2, lambda k: ckv[:, k, :], at=2 * n)
                    else:
                        ins = tokens_first(tile % RING, o % BANKS, ckv, 2, 4, at=2 * n)
                    ins.then_inc(acc_full, 1)
            pe.wait_ge(scaled, before("q", "scaled") + 3)
            for t in range(4):
                tile = TILES["uq"] + t
                pe.wait_ge(w_slot[tile % RING], 16 * (tile // RING + 1))
                for n in range(4):
                    o = OUTS["uq"] + 4 * t + n
                    bank(o)
                    blocks(ps[:, o % BANKS, 0:T], tile, 3, lambda k: cq[:, k, :], at=3 * n).then_inc(acc_full, 1)
            pe.wait_ge(acc_free, BANKS + OUTS["wo2"])
            for n in range(13):
                if n >= 2:
                    pe.wait_ge(roped, 12 + n - 1)
                src, w = rope_step(n)
                mm(ps[:, 4 + n % 2, 0:w], cst("perm2"), src, start=True, stop=True).then_inc(rotated, 1)

            def s2(u):
                h, qb = (u // 2) % 8, u % 2
                if u == 0:
                    pe.wait_ge(roped, 12 + 13)
                if u >= 3:
                    pe.wait_ge(exp_ready, 8 + u - 2)
                cols = slice(qb * P, (qb + 1) * P)
                if u < 16:
                    for j in range(2):
                        rows = slice(64 * j, 64 * j + 64)
                        ins = mm(ps[:, 2 * (u % 3) + j, :], q2[rows, h, cols], k2[rows, h, :], start=True, stop=True)
                else:
                    mm(ps[:, 2 * (u % 3), :], qm[:, h, cols], kn[:, h, :], start=True, stop=False)
                    ins = mm(ps[:, 2 * (u % 3), :], qm[:, 8 + h, cols], kr, start=False, stop=True)
                ins.then_inc(s_ready, 1)

            def t2(u):
                pe.wait_ge(p_ready, 8 + u + 1)
                if u:
                    pe.wait_ge(pt_copied, 8 + u)
                for kb in range(4):
                    ins = nc.tensor.transpose(ps[:, 6, kb * P:(kb + 1) * P],
                                              prob[u % 3][:, 0, kb * P:(kb + 1) * P], ident)
                ins.then_inc(pt_ready, 1)

            def o2(u):
                h = (u // 2) % 8
                pe.wait_ge(pt_copied, 8 + u + 1)
                if u:
                    pe.wait_ge(o_copied, 8 + u)
                vv = v2 if u < 16 else vm
                for kb in range(4):
                    ins = mm(ps[:, 7, (u % 2) * P:(u % 2 + 1) * P], vv[:, kb, h * P:(h + 1) * P],
                             wt2[u % 2][:, kb * P:(kb + 1) * P], start=(kb == 0), stop=(kb == 3))
                ins.then_inc(o_ready, 1)

            s2(0)
            s2(1)
            for s in range(32 + 1):
                if s + 2 < 32:
                    s2(s + 2)
                if s < 32:
                    t2(s)
                if s >= 1:
                    o2(s - 1)
                if s in (19, 21):
                    b = (s - 19) // 2
                    pe.wait_ge(sub_sq, b + 1)
                    if b:
                        pe.wait_ge(sub_var, b)
                    for j in range(2):
                        ins = mm(ps[:, 1 + 2 * j, :], ones, sq8[:, 4 * b + 2 * j:4 * b + 2 * j + 2, :],
                                 start=True, stop=True)
                    ins.then_inc(sub_sum, 1)
            pe.wait_ge(xl_ready, 8 + 3 * KC + 4)
            split_loop("wo2", WO2, MH, ML)
            norm_sum("b2", X, KC)
            pe.wait_ge(xl_ready, 12 + 4 * KC)
            with pe.Fori(0, FF // 4) as i:
                for u in range(U):
                    pe.wait_ge(acc_free, i * U + (OUTS["up"] + 2 * (u // 2) + 2))
                    for j in range(PIECES):
                        ins = piece(ps[:, (OUTS["up"] + u) % BANKS, 0:T], WF, j,
                                    i * (U * PIECES) + (16 + SPLIT["up"] + PIECES * u + j + 1),
                                    PB * j, PB, lambda k: XH[:, k, :], lambda k: XL[:, k, :], KC)
                        ins.then_inc(piece_used if j < PIECES - 1 else acc_full, 1)
            pe.wait_ge(hid_done, 1)
            with pe.Fori(0, 4) as i:
                for n in range(4):
                    pe.wait_ge(acc_free, i * 4 + (OUTS["down"] + n + 1))
                    for p in range(12):
                        blocks_n = PB if p % 3 < 2 else 3
                        ins = piece(ps[:, (OUTS["down"] + n) % BANKS, 0:T], WF, p % PIECES,
                                    i * 48 + (16 + SPLIT["down"] + 12 * n + p + 1),
                                    11 * (p // 3) + PB * (p % 3), blocks_n,
                                    lambda k: HH[:, k, :], lambda k: HL[:, k, :], FF)
                        ins.then_inc(piece_used if p < 11 else acc_full, 1)
            norm_sum("f2", X, KC)

        @block.vector
        def _(dve):
            ch = Chain(dve, dve_done)
            vv = nc.vector

            def ada_row(slot, wait, c_row, to):
                dve.wait_ge(a_slot[slot], wait)
                vv.tensor_tensor_reduce(ada[:, slot, :], ada[:, slot, :], c_row, 1.0, 0.0, ALU.mult, ALU.add,
                                        to).then_inc(a_free, 1)

            def ada_static(tile, to):
                ada_row(tile % 2, 16 * ((tile - 32) // 2 + 1), cb[:, 0, :], to)

            def norm(name, src, dst, gain, shift_cols=None, cols=T):
                i = NORM_AT[name]
                _, n, _, width, _ = NORMS[i]
                dve.wait_ge(summed, i + 1)
                vv.tensor_scalar(rs[:, 0:cols], ps[:, 4, 0:cols], 1.0 / width, EPS, ALU.mult, ALU.add)\
                    .then_inc(var_ready, 1)
                dve.wait_ge(std_ready, i + 1)
                ch.link(vv.reciprocal(rs[:, 0:cols], rs[:, 0:cols]))
                for k in range(n):
                    vv.scalar_tensor_tensor(dst[:, k, :], src[:, k, :], gain[:, k:k + 1], rs[:, 0:cols],
                                            ALU.mult, ALU.mult).then_inc(scaled, 1)
                dve.wait_ge(scaled, before(name, "scaled") + n)

            def gain_of(scale, g):
                ch.link(vv.scalar_tensor_tensor(coef[:], scale, 1.0, g, ALU.add, ALU.mult))

            dve.sem_inc(acc_free, BANKS)
            dve.sem_inc(lo_ready, 16)
            dve.sem_inc(piece_used, PIECES - 1)
            dve.sem_inc(a_free, TWO)
            dve.sem_inc(at_ready, TWO)
            dve.sem_inc(g_copied, OHB)
            dve.sem_inc(g_full, OHB)
            for j in range(2):
                dve.sem_inc(g_stored[j], 16)

            def low(parts, ready, u, slot, n=PIECES * PB, pieces=PIECES):
                for j in range(pieces):
                    w = min(PB, n - PB * j) * P
                    m = (pieces * u + j) % PIECES
                    dve.wait_ge(hi_ready, ready + j)
                    vv.tensor_tensor(parts[:, m, 1, 0:w], ring[:, slot, j * PB * P:j * PB * P + w],
                                     parts[:, m, 0, 0:w].bitcast(F32), ALU.subtract).then_inc(lo_ready, 1)

            def lows(x, xh, xl, ahead):
                for b in range(4):
                    c = slice(4 * b, 4 * b + 4)
                    dve.wait_ge(xh_ready, ahead + b + 1)
                    vv.tensor_tensor(xl[:, c, :], x[:, c, :], xh[:, c, :].bitcast(F32), ALU.subtract)\
                        .then_inc(xl_ready, 1)

            def shifted_lows(name, x, xh, xl, shift):
                for k in range(KC):
                    dve.wait_ge(shifted, before(name, "shifted") + k + 1)
                    vv.scalar_tensor_tensor(xl[:, k, :], x[:, k, :], shift[:, k:k + 1], xh[:, k, :].bitcast(F32),
                                            ALU.add, ALU.subtract).then_inc(xl_ready, 1)

            dve.wait_ge(c_silu, 1)
            for t in range(32):
                dve.wait_ge(a0_slot[t % 8], 16 * (t // 8 + 1))
                vv.tensor_tensor_reduce(ada0[t % 8], ada0[t % 8], cb[:, 0, :], 1.0, 0.0, ALU.mult, ALU.add,
                                        mod1[:, t:t + 1]).then_inc(a0_used, 1)
            dve.wait_ge(a0_used, 32)
            dve.wait_ge(const_in, 32)
            ch.link(vv.tensor_tensor(mod1[:, 0:32], mod1[:, 0:32], vc("ada_b")[:, 0:32], ALU.add))
            gain_of(mod1[:, 16:32], vc("norm1_g"))
            norm("a1", hT, X, coef)
            lows(X, XH1, XL1, 0)

            with dve.Fori(0, 3) as i:
                ch.enter(i, 1)
                for u in range(8):
                    low(W1, i * (U * PIECES) + (SPLIT["qk"] + PIECES * u + 1), u, u % RING)
                    ada_row(u % 2, i * 64 + 16 * (u // 2 + 1), cb[:, 0, :], modt[:, u:u + 1])
                dve.wait_ge(a_free, i * 8 + (2 + 8))
                ch.link(vv.tensor_copy(mod1[:, bass.ds(i * 8 + 32, 8)], modt[:, 0:8]))
            ch.leave(3)

            def rope(step, rot_n, bankn, chunk, w, a, b, cos, sin):
                dve.wait_ge(rotated, rot_n + 1)
                ch.tick(vv.tensor_tensor(a, ps[:, bankn, 0:w].rearrange("p (a b) -> p a b", b=T), sin, ALU.mult))
                ch.link(vv.tensor_tensor(b, chunk, cos, ALU.mult))
                vv.tensor_tensor(chunk, a, b, ALU.add).then_inc(roped, 1)
                dve.wait_ge(roped, rot_n + 1)

            def both(name, n):
                return cst(name).unsqueeze(1).broadcast_to([P, n, T])

            dve.wait_ge(tables_in, 32)
            at = 56
            for m in range(HEADS // 2):
                for n in (2 * m, 2 * m + 1):
                    low(W1, SPLIT["v"] + PIECES * n + 1, n, n % RING)
                ada_static(at, mod1[:, at:at + 1])
                at += 1
                for n in (2 * m, 2 * m + 1):
                    rope(n, n, 4 + n % 2, qk[:, 2 * n:2 * n + 2, :], 512, rope_a, rope_b, both("cos1", 2),
                         both("sin1", 2))

            dve.wait_ge(acc_full, OUTS["gate"])
            for j in range(3):
                ins = vv.memset(pads[j], 0.0)
            ins.then_inc(zeroed, 1)

            def pool_rows():
                dve.wait_ge(acc_free, BANKS + OUTS["gate"] + 4)
                w = 1
                src = pads[0]
                for level in range(4):
                    to = pads[1 + level % 2]
                    ch.link(vv.tensor_tensor(to[:, level:4, PAD:], src[:, level:4, PAD:],
                                             src[:, level:4, PAD - w:PAD + T - w], ALU.add))
                    src, w = to, 2 * w
                rc = cst("rcount").rearrange("p (a b) -> p a b", a=4)
                for g in range(4):
                    s = pads[1 + g % 2]
                    ch.tick(vv.tensor_tensor(s[:, g, PAD:], s[:, g, PAD:], rc[:, g, :], ALU.mult))
                ch.sync()
                for g in range(4):
                    s = pads[1 + g % 2]
                    ins = vv.tensor_tensor(pads[2][:, g, PAD:], s[:, g, PAD:], pads[0][:, g, PAD:], ALU.subtract)
                ins.then_inc(pooled, 1)

            for u in range(8):
                qb = u % 2
                nk = P * (qb + 1)
                s = sc1[:, :, 0:nk]
                mask = cst(f"mask{qb}").rearrange("p (a b) -> p a b", a=3)
                dve.wait_ge(s_ready, u + 1)
                if u:
                    dve.wait_ge(pt_ready, u)
                scores = ps[:, 4:6, :].rearrange("p a (b c) -> p (a b) c", c=T)[:, 0:3, 0:nk]
                ch.link(vv.scalar_tensor_tensor(s, scores, SM1, mask, ALU.mult, ALU.add))
                ch.link(vv.tensor_reduce(small[:, 2:3], s, mybir.AxisListType.XY, ALU.max))
                vv.tensor_scalar(small[:, 0:1], small[:, 2:3], -1.0, None, ALU.mult).then_inc(max_ready, 1)
                if at < 96:
                    ada_static(at, mod1[:, at:at + 1])
                    at += 1
                if u == 2:
                    pool_rows()
                dve.wait_ge(exp_ready, u + 1)
                ch.link(vv.reciprocal(small[:, 3:4], small[:, 1:2]))
                vv.tensor_scalar(s, s, small[:, 3:4], None, ALU.mult).then_inc(p_ready, 1)
                for _ in range(3):
                    if at < 96:
                        ada_static(at, mod1[:, at:at + 1])
                        at += 1
            while at < 96:
                ada_static(at, mod1[:, at:at + 1])
                at += 1
            dve.wait_ge(a_free, 2 + 64)
            ch.link(vv.tensor_tensor(mod1[:, 32:96], mod1[:, 32:96], vc("ada_b")[:, 32:96], ALU.add))

            for t in range(8):
                g = ga if t % 2 == 0 else gb
                for n in range(4):
                    o, c = OUTS["branch"] + 4 * t + n, 4 * (t // 2) + n
                    dve.wait_ge(acc_full, o + 1)
                    vv.tensor_tensor(g[:, c, :], g[:, c, :], ps[:, o % BANKS, 0:T], ALU.mult).then_inc(acc_free, 1)
                if t % 2:
                    c = 4 * (t // 2)
                    dve.wait_ge(acc_free, BANKS + OUTS["branch"] + 4 * (t + 1))
                    vv.tensor_tensor(ga[:, c:c + 4, :], ga[:, c:c + 4, :], gb[:, c:c + 4, :], ALU.add)\
                        .then_inc(merged, 1)

            lows(ga, GH, GL, 4)
            for n in range(17):
                if n < 16:
                    low(WO, SPLIT["wo"] + PIECES * n + 1, n, n % RING)
                if n:
                    c, o = n - 1, OUTS["wo"] + n - 1
                    dve.wait_ge(acc_full, o + 1)
                    vv.scalar_tensor_tensor(hT[:, c, :], ps[:, o % BANKS, 0:T], mod1[:, 32 + c:33 + c], hT[:, c, :],
                                            ALU.mult, ALU.add).then_inc(acc_free, 1)
            dve.wait_ge(acc_free, BANKS + OUTS["wq"])
            dve.sem_inc(h_ready, 1)
            gain_of(mod1[:, 64:80], vc("norm2_g"))
            norm("b1", hT, X, coef)
            shifted_lows("b1", X, XH, XL, mod1[:, 48:64])

            def best(to_v, to_i, rows, n):
                for r in range(n):
                    ins = vv.max(to_v[:, r, 0:8], rows[:, r, :])
                ch.link(ins)
                for r in range(n):
                    ins = vv.max_index(to_i[:, r, 0:8], to_v[:, r, 0:8], rows[:, r, :])
                ch.link(ins)
                for r in range(n):
                    ins = vv.match_replace(rows[:, r, :], to_v[:, r, 0:8], rows[:, r, :], NEG)
                ch.link(ins)
                for r in range(n):
                    ins = vv.max(to_v[:, r, 8:16], rows[:, r, :])
                ch.link(ins)
                for r in range(n):
                    ins = vv.max_index(to_i[:, r, 8:16], to_v[:, r, 8:16], rows[:, r, :])
                ch.link(ins)

            for n in range(16 + 4):
                if n < 16:
                    low(WP, SPLIT["wq"] + PIECES * n + 1, n, n % RING)
                if n >= 4:
                    h, tb = (n - 4) // 2, n % 2
                    dve.wait_ge(score_copied, h + 1)
                    two = slice(tb * KC + 2 * h, tb * KC + 2 * h + 2)
                    best(topv[:, two, :], topi[:, two, :], score[:, two, :], 2)

            iota = cst("iota")
            for tb in range(2):
                half = slice(tb * KC, (tb + 1) * KC)
                ch.tick(vv.tensor_copy(topf, topi[:, half, :]))
                pairs = topv[:, half, :].rearrange("p (h s) k -> p h s k", s=2)
                c4 = cand.rearrange("p h (i j) -> p h i j", i=TOPK)
                ch.link(vv.tensor_tensor(c4, pairs[:, :, 0, :].unsqueeze(3).broadcast_to([P, EH, TOPK, TOPK]),
                                         pairs[:, :, 1, :].unsqueeze(2).broadcast_to([P, EH, TOPK, TOPK]), ALU.add))
                best(cv, ci, cand, EH)
                ch.tick(vv.tensor_scalar(ca, ci, 4, None, ALU.logical_shift_right))
                ch.link(vv.tensor_scalar(cbi, ci, 15, None, ALU.bitwise_and))
                ch.tick(vv.tensor_copy(caf, ca))
                ch.tick(vv.tensor_copy(cbf, cbi))
                ch.link(vv.tensor_tensor(gsum, cv[:, :, 0], cv[:, :, 0], ALU.max))
                if tb:
                    dve.wait_ge(ids_turned, tb)
                vv.tensor_tensor(cv, cv, gsum.unsqueeze(2).broadcast_to([P, EH, TOPK]), ALU.subtract)\
                    .then_inc(cand_ready, 1)
                ff = topf.rearrange("p (h s) k -> p h s k", s=2)
                for j, pos in enumerate((caf, cbf)):
                    ch.link(vv.tensor_tensor(eq, pos.unsqueeze(3).broadcast_to([P, EH, TOPK, TOPK]),
                                             iota[:, 0:TOPK].unsqueeze(1).unsqueeze(1).broadcast_to([P, EH, TOPK, TOPK]),
                                             ALU.is_equal))
                    ch.link(vv.tensor_tensor(eq, eq, ff[:, :, j, :].unsqueeze(2).broadcast_to([P, EH, TOPK, TOPK]),
                                             ALU.mult))
                    ch.link(vv.tensor_reduce(ids[:, j, :], eq.rearrange("p h k j -> p (h k) j"), AX, ALU.add))
                dve.wait_ge(gate_exp, tb + 1)
                gt = ids[:, 2, :].rearrange("p (h k) -> p h k", h=EH)
                ch.link(vv.tensor_reduce(gsum, gt, AX, ALU.add))
                ch.link(vv.reciprocal(gsum, gsum))
                vv.tensor_tensor(gt, gt, gsum.unsqueeze(2).broadcast_to([P, EH, TOPK]), ALU.mult)\
                    .then_inc(ids_ready, 1)
                dve.wait_ge(ids_ready, tb + 1)

            dve.wait_ge(ids_copied, 2)
            with dve.Fori(0, NBLK) as i:
                for j in range(OHB):
                    tok = bass.ds(i * 16 + OHT * j, OHT)
                    dve.wait_ge(g_full, i * OHB + (j + 1))
                    many = iota.unsqueeze(1).broadcast_to([P, OHT, P])
                    vv.tensor_tensor(oh2[j], many, idT[:, 1, tok].unsqueeze(2).broadcast_to([P, OHT, P]), ALU.is_equal)
                    vv.tensor_tensor(oh1[j], many, idT[:, 0, tok].unsqueeze(2).broadcast_to([P, OHT, P]), ALU.is_equal)\
                        .then_inc(oh_dve, 1)

            dve.wait_ge(c_silu, 3)

            def gated(i, u):
                dve.wait_ge(gelu_done, i * 16 + (u + 1))
                g = gl[:, u % 2, :]
                ch.link(vv.tensor_tensor(g.rearrange("p (a b) -> p a b", a=NBLK),
                                         g.rearrange("p (a b) -> p a b", a=NBLK),
                                         G[:, :, u * BLK:(u + 1) * BLK], ALU.mult))
                ch.link(vv.tensor_copy(ATH[:, u, :], g))
                vv.tensor_tensor(ATL[:, u, :], g, ATH[:, u, :].bitcast(F32), ALU.subtract).then_inc(at_ready, 1)
                dve.wait_ge(at_ready, i * 16 + (u + TWO + 1))
                dve.sem_inc(acc_free, 1)

            def expert_out(i, u):
                dve.wait_ge(acc_full, i * 32 + (OUTS["peer"] + 16 + u + 1))
                vv.scalar_tensor_tensor(hT[:, u, :], ps[:, u % BANKS, 0:T], mod1[:, 80 + u:81 + u], hT[:, u, :],
                                        ALU.mult, ALU.add).then_inc(acc_free, 1)

            def peer_turn(i, last=False):
                for u in range(1, 33):
                    if u < 32 or not last:
                        low(WP, i * (32 * PIECES) + (SPLIT["peer"] + PIECES * u + 1), u, u % RING)
                    if u == 1:
                        dve.wait_ge(g_in, i * 16 + 16)
                    if u <= 16:
                        gated(i, u - 1)
                    else:
                        expert_out(i, u - 17)
                    if u % 2:
                        r = u // 2
                        m = r // 2 if r < 8 else r - 4
                        slot = m % 2
                        dve.wait_ge(a_slot[slot], i * 96 + 16 * ((64 + m) // 2 + 1))
                        if r < 8 and r % 2 == 0:
                            ch.link(vv.tensor_tensor_reduce(junk, ada[:, slot, :], cb[:, 1, :], 1.0, 0.0, ALU.mult,
                                                            ALU.add, modt[:, 12 + m:13 + m]))
                        else:
                            vv.tensor_tensor_reduce(ada[:, slot, :], ada[:, slot, :], cb[:, 0, :], 1.0, 0.0,
                                                    ALU.mult, ALU.add, modt[:, m:m + 1]).then_inc(a_free, 1)
                dve.wait_ge(a_free, i * 12 + (2 + 64 + 12))
                ch.tick(vv.tensor_copy(mod2[:, bass.ds(i * 4, 4)], modt[:, 0:4]))
                ch.tick(vv.tensor_copy(mod2[:, bass.ds(i * 8 + 32, 8)], modt[:, 4:12]))
                ch.link(vv.tensor_copy(modc[:, bass.ds(i * 4, 4)], modt[:, 12:16]))
                dve.wait_ge(acc_free, i * 32 + (BANKS + OUTS["peer"] + 32))

            low(WP, SPLIT["peer"] + 1, 0, 0)
            with dve.Fori(0, NG - 1) as i:
                ch.enter(i, 39)
                peer_turn(i)
            ch.leave(NG - 1)
            peer_turn(NG - 1, last=True)
            ch.link(vv.tensor_tensor(mod2[:], mod2[:], vc("b_ada_2"), ALU.add))
            ch.link(vv.tensor_tensor(modc[:], modc[:], vc("b_ada_2")[:, 0:32], ALU.add))
            dve.sem_inc(h_ready, 1)
            norm("f1", hT, hT, vc("final_g"))
            gain_of(modc[:, 16:32], vc("norm1_w_2"))
            norm("ctx", ctxT, X2[:, :, 0:CTX], coef)
            shifted_lows("ctx", X2[:, :, 0:CTX], X2H[:, :, 0:CTX], X2L[:, :, 0:CTX], modc[:, 0:KC])
            gain_of(mod2[:, 16:32], vc("norm1_w_2"))
            norm("a2", hT, X2[:, :, CTX:], coef)
            shifted_lows("a2", X2[:, :, CTX:], X2H[:, :, CTX:], X2L[:, :, CTX:], mod2[:, 0:KC])
            for n in range(30):
                low(W2, SPLIT["q2"] + PIECES * n + 1, n, n % RING)

            norm("kv", ckv, ckv, vc("kv_norm_w_2"), cols=TA)
            norm("q", cq, cq, vc("q_norm_w_2"))
            for j in range(2):
                ch.tick(vv.tensor_tensor_reduce(vc(f"lambda_q{j + 1}_2"), vc(f"lambda_q{j + 1}_2"),
                                                vc(f"lambda_k{j + 1}_2"), 1.0, 0.0, ALU.mult, ALU.add,
                                                small[:, 12 + j:13 + j]))
            ch.sync()
            dve.sem_inc(max_ready, 1)
            dve.wait_ge(lam_exp, 1)
            ch.link(vv.tensor_tensor(small[:, 14:15], small[:, 13:14], small[:, 12:13], ALU.subtract))
            ch.link(vv.tensor_scalar(small[:, 14:15], small[:, 14:15], -LAMBDA_INIT, None, ALU.add))
            dve.wait_ge(acc_free, BANKS + OUTS["wo2"])
            for n in range(13):
                src, w = rope_step(n)
                m = w // T
                rope(n, 12 + n, 4 + n % 2, src, w, rope2[0][:, 0:m, :], rope2[1][:, 0:m, :],
                     both("cos2", m), both("sin2", m))

            def max2(u):
                two = 2 if u < 16 else 1
                b = 2 * (u % 3)
                dve.wait_ge(s_ready, 8 + u + 1)
                if u >= 3:
                    dve.wait_ge(p_ready, 8 + u - 2)
                m = small[:, 4 * (u % 3):4 * (u % 3) + two]
                ch.link(vv.tensor_reduce(m, ps[:, b:b + two, :], AX, ALU.max))
                vv.tensor_scalar(m, m, -(SM_DA if two == 2 else SM_MLA), None, ALU.mult).then_inc(max_ready, 1)

            def prob2(u):
                two = 2 if u < 16 else 1
                s0 = 4 * (u % 3) + 2
                dve.wait_ge(exp_ready, 8 + u + 1)
                ch.link(vv.reciprocal(small[:, s0:s0 + two], small[:, s0:s0 + two]))
                w = prob[u % 3]
                if two == 2:
                    ch.tick(vv.tensor_scalar(w[:, 1, :], w[:, 1, :], small[:, s0 + 1:s0 + 2], small[:, 14:15],
                                             ALU.mult, ALU.mult))
                    ch.sync()
                    vv.scalar_tensor_tensor(w[:, 0, :], w[:, 0, :], small[:, s0:s0 + 1], w[:, 1, :],
                                            ALU.mult, ALU.add).then_inc(p_ready, 1)
                else:
                    vv.tensor_scalar(w[:, 0, :], w[:, 0, :], small[:, s0:s0 + 1], None, ALU.mult)\
                        .then_inc(p_ready, 1)

            def mix_low(b):
                four = slice(4 * b, 4 * b + 4)
                if b < 2:
                    dve.wait_ge(mix_high, b + 1)
                else:
                    dve.wait_ge(mix_raw, 8 * (b - 1))
                    dve.wait_ge(o_copied, 8 + 8 * (b + 1))
                vv.tensor_tensor(ML[:, four, :], mix[:, four, :], MH[:, four, :].bitcast(F32), ALU.subtract)\
                    .then_inc(xl_ready, 1)

            max2(0)
            max2(1)
            for s in range(32):
                prob2(s)
                if s + 2 < 32:
                    max2(s + 2)
                if s in (20, 22):
                    b = (s - 20) // 2
                    dve.wait_ge(sub_sum, b + 1)
                    ch.link(vv.tensor_scalar(rs8[:, 4 * b:4 * b + 2, :].rearrange("p a b -> p (a b)"), ps[:, 1, :],
                                             1.0 / P, EPS, ALU.mult, ALU.add))
                    vv.tensor_scalar(rs8[:, 4 * b + 2:4 * b + 4, :].rearrange("p a b -> p (a b)"), ps[:, 3, :],
                                     1.0 / P, EPS, ALU.mult, ALU.add).then_inc(sub_var, 1)
                if s in (24, 25):
                    four = slice(4 * (s - 24), 4 * (s - 24) + 4)
                    dve.wait_ge(sub_std, 1)
                    ch.link(vv.reciprocal(rs8[:, four, :], rs8[:, four, :]))
                if s == 25:
                    ch.link(vv.tensor_scalar(small[:, 15:16], vc("subln_w_2"), 1.0 - LAMBDA_INIT, None, ALU.mult))
                if s in (26, 27):
                    four = slice(4 * (s - 26), 4 * (s - 26) + 4)
                    vv.scalar_tensor_tensor(mix[:, four, :], mix[:, four, :], small[:, 15:16], rs8[:, four, :],
                                            ALU.mult, ALU.mult).then_inc(mixed, 1)
                if s == 28:
                    mix_low(2)
                if s in (30, 31):
                    mix_low(s - 30)
            low(WO2, SPLIT["wo2"] + 1, 0, 0)
            mix_low(3)
            for n in range(1, 17):
                if n < 16:
                    low(WO2, SPLIT["wo2"] + PIECES * n + 1, n, n % RING)
                c, o = n - 1, OUTS["wo2"] + n - 1
                dve.wait_ge(acc_full, o + 1)
                vv.scalar_tensor_tensor(hT[:, c, :], ps[:, o % BANKS, 0:T], mod2[:, 32 + c:33 + c], hT[:, c, :],
                                        ALU.mult, ALU.add).then_inc(acc_free, 1)
            dve.wait_ge(acc_free, BANKS + OUTS["up"])
            dve.sem_inc(h_ready, 1)
            gain_of(mod2[:, 64:80], vc("norm2_w_2"))
            norm("b2", hT, X, coef)

            shifted_lows("b2", X, XH, XL, mod2[:, 48:64])

            for j in range(2):
                ch.tick(vv.memset(gp[j], 0.0))
            ch.sync()
            dve.sem_inc(conv_ready, TWO)
            cw = vc("conv_w_2").rearrange("p (j f) -> p j f", j=3)

            def conv(i, p):
                f = bass.ds(i * 4 + p, 1)
                g, c = gp[p % 2], gc[p % 2]
                dve.wait_ge(g_row, i * 4 + (p + 1))
                ch.link(vv.tensor_scalar(c, g[:, 1:T + 1], cw[:, 1, f], vc("conv_b_2")[:, f], ALU.mult, ALU.add))
                ch.link(vv.scalar_tensor_tensor(c, g[:, 0:T], cw[:, 0, f], c, ALU.mult, ALU.add))
                vv.scalar_tensor_tensor(c, g[:, 2:T + 2], cw[:, 2, f], c, ALU.mult, ALU.add)\
                    .then_inc(conv_ready, 1)

            def hidden(i, p):
                c, f = gc[p % 2], i * 4 + p
                o = OUTS["up"] + 2 * p + 1
                dve.wait_ge(silu_done, i * 4 + (p + 1))
                dve.wait_ge(acc_full, i * U + (o + 1))
                vv.tensor_tensor(c, c, ps[:, o % BANKS, 0:T], ALU.mult).then_inc(acc_free, 2)
                dve.wait_ge(acc_free, i * U + (BANKS + OUTS["up"] + 2 * p + 2))
                ch.link(vv.tensor_copy(HH[:, f, :], c))
                ch.link(vv.tensor_tensor(HL[:, f, :], c, HH[:, f, :].bitcast(F32), ALU.subtract))

            def up_turn(i, last=False):
                for u in range(1, U + 1):
                    if u < U or not last:
                        low(WF, i * (U * PIECES) + (SPLIT["up"] + PIECES * u + 1), u, u % RING)
                    if u % 2:
                        conv(i, u // 2)
                    else:
                        hidden(i, u // 2 - 1)

            low(WF, SPLIT["up"] + 1, 0, 0)
            with dve.Fori(0, FF // 4 - 1) as i:
                ch.enter(i, 16)
                up_turn(i)
            ch.leave(FF // 4 - 1)
            up_turn(FF // 4 - 1, last=True)
            dve.sem_inc(hid_done, 1)

            def down_out(i, n):
                dve.wait_ge(acc_full, i * 4 + (OUTS["down"] + n + 1))
                c = i * 4 + n
                vv.scalar_tensor_tensor(hT[:, c, :], ps[:, (OUTS["down"] + n) % BANKS, 0:T],
                                        mod2[:, bass.ds(i * 4 + 80 + n, 1)], hT[:, c, :],
                                        ALU.mult, ALU.add).then_inc(acc_free, 1)

            with dve.Fori(0, 4) as i:
                for u in range(16):
                    low(WF, i * 48 + (SPLIT["down"] + 3 * u + 1), u, u % RING, n=11, pieces=3)
                    if u % 4 == 0 and u:
                        down_out(i, u // 4 - 1)
                down_out(i, 3)
            dve.wait_ge(acc_free, BANKS + OUTS["end"])
            dve.sem_inc(h_ready, 1)
            norm("f2", hT, hT, vc("final_w_2"))


def tiled(w):
    k, n = w.shape
    return w.reshape(k // P, P, n // P, P).transpose(2, 1, 0, 3).reshape(n // P, P, k)


def tiled_values(w):
    k, n = w.shape
    return w.reshape(2, KC // 2, P, n // (2 * P), 2 * P).transpose(3, 0, 2, 1, 4).reshape(n // P, P, k)


def chunks(x):
    n, f = x.shape
    return x.reshape(n, f // P, P).transpose(2, 1, 0)


def columns(v):
    return v.reshape(-1, P).T


def constants():
    c = np.zeros((P, N_CONST), np.float32)

    def put(name, v):
        c[:, CONST[name][0]:CONST[name][1]] = v.reshape(P, -1)

    p = np.arange(P)
    for qb, n in ((0, P), (1, T)):
        dist = (qb * P + p)[:, None] - np.arange(n)[None, :]
        ok = np.stack([(dist >= 0) & (dist % dil == 0) & (dist // dil <= window // dil)
                       for window, dil in GROUPS], axis=1)
        put(f"mask{qb}", np.where(ok, 0.0, MASKED))
    inv = np.power(np.float32(10000.0), -np.arange(64, dtype=np.float32) / np.float32(64)).astype(np.float32)
    ang = (np.arange(T, dtype=np.float32)[None, :] * inv[p % 64][:, None]).astype(np.float32).astype(np.float64)
    put("cos1", np.cos(ang))
    put("sin1", np.sin(ang))
    perm = np.zeros((P, P))
    perm[(p + 64) % P, p] = np.where(p < 64, -1.0, 1.0)
    put("perm1", perm)
    put("ident", np.eye(P))
    put("ones", np.ones((P, P)))
    inv = np.power(np.float32(10000.0), -np.arange(16, dtype=np.float32) / np.float32(16)).astype(np.float32)
    t = np.arange(T)
    pos = np.where((p % 64 < 32)[:, None], (t // 64)[None, :], (t % 64)[None, :]).astype(np.float32)
    ang = (pos * inv[p % 16][:, None]).astype(np.float32).astype(np.float64)
    put("cos2", np.cos(ang))
    put("sin2", np.sin(ang))
    perm = np.zeros((P, P))
    low = p % 32 < 16
    perm[np.where(low, p + 16, p - 16), p] = np.where(low, -1.0, 1.0)
    put("perm2", perm)
    put("iota", np.broadcast_to(np.arange(P), (P, P)))
    count = np.stack([1.0 / np.minimum(t + 1, w) for w in POOLS])
    put("rcount", np.broadcast_to(count, (P, 4, T)).copy())
    return c


def kernel(**inputs):
    import concourse.bacc as bacc
    from concourse.bass_utils import run_bass_kernel_spmd

    a = {k: np.asarray(v) for k, v in inputs.items()}

    def spread(v):
        return np.broadcast_to(v.reshape(1, -1), (P, v.size))

    vectors = []
    for name, (lo, hi) in VEC.items():
        if name.startswith("lambda"):
            vectors.append(spread(a[name]))
        else:
            vectors.append(columns(a[name].reshape(-1)))

    rows1 = a["ada_w"][0].T.reshape(96, P, D)
    rows2 = a["w_ada_2"][0].T.reshape(96, P, D)
    order = [j for g in range(NG) for j in (*range(4 * g, 4 * g + 4), *range(32 + 8 * g, 40 + 8 * g))]

    def wide(w, n):
        t = tiled(w)
        return t.reshape(t.shape[0] // n, n, P, t.shape[2]).transpose(0, 2, 1, 3).reshape(-1, P, n * t.shape[2])

    wa, wp = wide(a["w_attn_branch"][0], 4), wide(a["w_pool_branch"][0], 4)
    w1, w2 = a["w_in"][0], a["w_in_2"][0]
    zeros = np.zeros((D, 64), np.float32)
    w2 = np.concatenate([w2[:, :3072], w2[:, 3456:3712], w2[:, 3712:], zeros, w2[:, 3072:3456]], axis=1)
    uq = a["w_uq_2"][0].reshape(384, H2, 192)
    uq_rope = np.concatenate([uq[:, :, P:], np.zeros((384, H2, 64), np.float32)], axis=2)
    uq = np.concatenate([uq[:, :, :P].reshape(384, -1), uq_rope.reshape(384, -1)], axis=1)
    ukv = a["w_ukv_2"][0].reshape(256, H2, 2, P).transpose(0, 2, 1, 3).reshape(256, 2 * D // 2)
    up = a["w_up_2"][0].reshape(D, 2, FF, P).transpose(0, 2, 1, 3).reshape(D, 2 * FF * P)
    down = tiled(a["w_down_2"][0]).reshape(KC, P, 4, 11 * P).transpose(0, 2, 1, 3).reshape(4 * KC, P, 11 * P)
    arrays = {
        "x": chunks(a["x"][0]),
        "ctx": chunks(a["ctx_2"][0]),
        "c": spread(a["c"]),
        "c_2": spread(a["c_2"]),
        "c_ctx_2": spread(a["c_ctx_2"]),
        "const": constants(),
        "vec": np.concatenate(vectors, axis=1),
        "pool_mix": a["pool_mix"][0].transpose(1, 0, 2),
        "ada": np.concatenate([rows1, rows2[order]], axis=0),
        "w_in": np.concatenate([tiled(w1[:, :3072]), tiled_values(w1[:, 3072:4608]), tiled(w1[:, 4608:])], axis=0),
        "w_branch": np.stack([wa, wp], axis=1).reshape(8, P, D),
        "w_out": tiled(a["w_out"][0]),
        "peer_wq": tiled(a["peer_wq"][0]),
        "keys": a["peer_keys"][0].transpose(3, 0, 1, 2).reshape(P, KC, NKEY),
        "peer_down": a["peer_down"][0].reshape(NKEY, NKEY, KC, P).transpose(1, 3, 2, 0).reshape(NKEY, P, D),
        "peer_up": a["peer_up"][0].reshape(NKEY, NG, 16, KC, P).transpose(1, 3, 0, 2, 4).reshape(NKEY, P, D),
        "w_in_2": np.concatenate([tiled(w2[:, :2048]), tiled_values(w2[:, 2048:3072]), tiled(w2[:, 3072:])], axis=0),
        "w_ukv_2": wide(ukv, 8),
        "w_uq_2": wide(uq, 4),
        "w_o_2": tiled(a["w_o_2"][0]),
        "w_up_2": tiled(up),
        "w_down_2": down,
    }
    arrays = {k: np.ascontiguousarray(v) for k, v in arrays.items()}
    nc = bacc.Bacc("TRN2", target_bir_lowering=False, num_devices=1)
    A = {k: nc.dram_tensor(f"in_{k}", v.shape, F32, kind="ExternalInput").ap() for k, v in arrays.items()}
    out = nc.dram_tensor("out", (P, KC, T), F32, kind="ExternalOutput").ap()
    build_program(nc, A, out)
    r = run_bass_kernel_spmd(nc, [{f"in_{k}": v for k, v in arrays.items()}], core_ids=[0])
    return r.results[0]["out"].transpose(2, 1, 0).reshape(1, T, D)
```
